# Optimizing a Trainium2 kernel written in Bass

```python
import jax
import jax.numpy as jnp
from jax import lax
import numpy as np

D_MODEL = 1024
BATCH = 1
SEQ = 512
DEPTH = 1

GRID_W = 64
CTX_LEN = 256
D_A = 1024
HEAD_A = 64
N_HEADS_A = D_A // HEAD_A
DECAY_LORA = 64
ICLR_LORA = 64
GATE_LORA = 128
N_DIR = 2
D_B = 512
POOL_WINDOWS = (2, 4, 8, 16)
POOL_GROUP = D_B // len(POOL_WINDOWS)
N_BRANCH = 2
PEER_HEADS = 8
PEER_NKEYS = 128
PEER_EXPERTS = PEER_NKEYS * PEER_NKEYS
PEER_QDIM = 256
PEER_HALF = PEER_QDIM // 2
PEER_TOPK = 16
PEER_BLOCK = 128
RMS_EPS = 1e-6
GN_EPS = 64e-5
L2_EPS = 1e-12
SHIFT_COLS = 3 * D_A + N_DIR * DECAY_LORA + N_DIR * ICLR_LORA + GATE_LORA
IN_COLS = SHIFT_COLS + D_B + N_BRANCH * D_MODEL

kernel_name = 'hybrid_rwkv7_pool_peer_dit_block'

def rms_norm(x, g):
    xf = x.astype(jnp.float32)
    y = xf * lax.rsqrt(jnp.mean(xf * xf, axis=-1, keepdims=True) + RMS_EPS)
    return (y * g.astype(jnp.float32)).astype(x.dtype)

def ada_split(cond, w_mod, b_mod):
    m = jax.nn.silu(cond) @ w_mod + b_mod
    return jnp.split(m, 6, axis=-1)

def token_shift_mix(z, mu):
    prev = jnp.pad(z[:, :-1], ((0, 0), (1, 0), (0, 0)))
    nxt = jnp.pad(z[:, 1:], ((0, 0), (0, 1), (0, 0)))
    return z + mu * (0.5 * (prev + nxt) - z)

def split_heads(t):
    return t.reshape(t.shape[:-1] + (N_HEADS_A, HEAD_A))

def rwkv_prepare(zs, w0, w2, a0, a2, g2, k_k, k_a):
    B, T, _ = zs.shape
    bounds = [int(b) for b in np.cumsum([0, D_A, D_A, D_A, N_DIR * DECAY_LORA, N_DIR * ICLR_LORA, GATE_LORA])]
    r, k, v, wd, ad, gd = [zs[..., bounds[i]:bounds[i + 1]] for i in range(6)]
    wd = wd.reshape(B, T, N_DIR, DECAY_LORA)
    ad = ad.reshape(B, T, N_DIR, ICLR_LORA)
    w_log = -jax.nn.softplus(-(w0 + jnp.einsum('btdl,dlc->btdc', jnp.tanh(wd), w2))) - 0.5
    decay = jnp.exp(-jnp.exp(w_log.astype(jnp.float32)))
    iclr = jax.nn.sigmoid(a0 + jnp.einsum('btdl,dlc->btdc', ad, a2))
    gate = jax.nn.sigmoid(gd) @ g2
    kk = split_heads(k * k_k).astype(jnp.float32)
    kk = kk * lax.rsqrt(jnp.maximum(jnp.sum(kk * kk, axis=-1, keepdims=True), L2_EPS * L2_EPS))
    k_dir = k[:, :, None, :] * (1.0 + (iclr - 1.0) * k_a)
    return dict(r=split_heads(r), k_dir=split_heads(k_dir), v=split_heads(v), kk=kk,
                decay=split_heads(decay), iclr=split_heads(iclr), gate=gate)

def both_directions(t, per_dir):
    f, b = (t[:, :, 0], t[:, :, 1]) if per_dir else (t, t)
    return jnp.stack([f, b[:, ::-1]], axis=2).astype(jnp.float32).swapaxes(0, 1)

def rwkv_step(S, inp):
    r, w, k, v, a, b = inp
    sa = jnp.einsum('bdhvk,bdhk->bdhv', S, a)
    S = S * w[..., None, :] + sa[..., None] * b[..., None, :] + v[..., None] * k[..., None, :]
    return S, jnp.einsum('bdhvk,bdhk->bdhv', S, r)

def rwkv_scan(S0, prep):
    xs = (both_directions(prep['r'], False),
          both_directions(prep['decay'], True),
          both_directions(prep['k_dir'], True),
          both_directions(prep['v'], False),
          -both_directions(prep['kk'], False),
          both_directions(prep['kk'][:, :, None] * prep['iclr'], True))
    S, ys = lax.scan(rwkv_step, S0, xs)
    ys = ys.swapaxes(0, 1)
    return S, ys[:, :, 0] + ys[:, ::-1, 1]

def rwkv_readout(y, prep, r_k, ln_w, ln_b, w_a_out):
    dt = prep['gate'].dtype
    mu = jnp.mean(y, axis=-1, keepdims=True)
    var = jnp.mean(jnp.square(y - mu), axis=-1, keepdims=True)
    yn = ((y - mu) * lax.rsqrt(var + GN_EPS)).reshape(y.shape[:2] + (D_A,))
    yn = yn * ln_w.astype(jnp.float32) + ln_b.astype(jnp.float32)
    k_b = jnp.mean(prep['k_dir'], axis=2)
    bonus = jnp.sum(prep['r'] * k_b * split_heads(r_k), axis=-1, keepdims=True) * prep['v']
    out = (yn.astype(dt) + bonus.reshape(y.shape[:2] + (D_A,))) * prep['gate']
    return out @ w_a_out

def box_mean_grid(u, window, rows):
    B, T, C = u.shape
    g = u.astype(jnp.float32).reshape(B, rows, GRID_W, C)
    P = jnp.pad(jnp.cumsum(jnp.cumsum(g, axis=1), axis=2), ((0, 0), (1, 0), (1, 0), (0, 0)))
    half = window // 2
    ri = jnp.arange(rows)
    ci = jnp.arange(GRID_W)
    r0, r1 = jnp.clip(ri - half, 0, rows), jnp.clip(ri + half, 0, rows)
    c0, c1 = jnp.clip(ci - half, 0, GRID_W), jnp.clip(ci + half, 0, GRID_W)
    corner = lambda ra, ca: jnp.take(jnp.take(P, ra, axis=1), ca, axis=2)
    s = corner(r1, c1) - corner(r0, c1) - corner(r1, c0) + corner(r0, c0)
    cnt = ((r1 - r0)[:, None] * (c1 - c0)[None, :]).astype(jnp.float32)[None, :, :, None]
    return (s / cnt).reshape(B, T, C).astype(u.dtype) - u

def window_mean_seq(u, window):
    T = u.shape[1]
    P = jnp.pad(jnp.cumsum(u.astype(jnp.float32), axis=1), ((0, 0), (1, 0), (0, 0)))
    t = jnp.arange(T)
    lo, hi = jnp.clip(t - window // 2, 0, T), jnp.clip(t + window // 2, 0, T)
    s = jnp.take(P, hi, axis=1) - jnp.take(P, lo, axis=1)
    return (s / (hi - lo).astype(jnp.float32)[None, :, None]).astype(u.dtype) - u

def pool_branch(u, mean_fn, w_pool, pool_scale, w_b_out):
    outs = [jnp.einsum('btc,cd->btd', mean_fn(u[..., j * POOL_GROUP:(j + 1) * POOL_GROUP], win), w_pool[j])
            for j, win in enumerate(POOL_WINDOWS)]
    return (jnp.concatenate(outs, axis=-1) * pool_scale) @ w_b_out

def merge_branches(z, ya, mean_fn, b_gate, w_pool, pool_scale, w_b_out, w_o):
    yb = pool_branch(z[..., SHIFT_COLS:SHIFT_COLS + D_B], mean_fn, w_pool, pool_scale, w_b_out)
    gates = jax.nn.sigmoid(z[..., SHIFT_COLS + D_B:] + b_gate)
    m = gates[..., :D_MODEL] * ya + gates[..., D_MODEL:] * yb
    return m @ w_o

def peer_ffn(h, w_q, sub_keys, u_emb, v_emb):
    B, T, D = h.shape
    hb = h.reshape(-1, PEER_BLOCK, D)

    def block(xb):
        n = xb.shape[0]
        q = (xb @ w_q).reshape(n, PEER_HEADS, 2, PEER_HALF)
        s = jnp.einsum('nhpq,hpkq->nhpk', q, sub_keys)
        sv, si = lax.top_k(s, PEER_TOPK)
        cand = sv[:, :, 0, :, None] + sv[:, :, 1, None, :]
        cand_idx = si[:, :, 0, :, None] * PEER_NKEYS + si[:, :, 1, None, :]
        cs, ci = lax.top_k(cand.reshape(n, PEER_HEADS, PEER_TOPK * PEER_TOPK), PEER_TOPK)
        idx = jnp.take_along_axis(cand_idx.reshape(n, PEER_HEADS, -1), ci, axis=-1)
        gate = jax.nn.softmax(cs.astype(jnp.float32), axis=-1).astype(xb.dtype)
        ue = jnp.take(u_emb, idx, axis=0)
        act = jax.nn.gelu(jnp.einsum('nhed,nd->nhe', ue, xb), approximate=False)
        ve = jnp.take(v_emb, idx, axis=0)
        return jnp.einsum('nhe,nhed->nd', gate * act, ve)

    return lax.map(block, hb).reshape(B, T, D)

def setup_inputs(seed: int = 0) -> dict:
    key = jax.random.key(seed)
    ks = list(jax.random.split(key, 32))
    L, D = DEPTH, D_MODEL

    def nrm(i, shape, scale):
        return jax.random.normal(ks[i], shape, jnp.float32) * scale

    return {
        'x': nrm(0, (BATCH, SEQ, D), 1.0),
        'c': nrm(1, (BATCH, D), 1.0),
        'ctx': nrm(2, (BATCH, CTX_LEN, D), 1.0),
        'c_ctx': nrm(3, (D,), 1.0),
        'w_mod': nrm(4, (L, D, 6 * D), 0.5 * D ** -0.5),
        'b_mod': nrm(5, (L, 6 * D), 0.02),
        'g_pre_mix': 1.0 + nrm(6, (L, D), 0.05),
        'g_post_mix': 1.0 + nrm(7, (L, D), 0.05),
        'g_pre_ffn': 1.0 + nrm(8, (L, D), 0.05),
        'g_post_ffn': 1.0 + nrm(9, (L, D), 0.05),
        'w_in': nrm(10, (L, D, IN_COLS), D ** -0.5),
        'b_gate': nrm(11, (L, N_BRANCH * D), 0.02),
        'mu_shift': jax.random.uniform(ks[12], (L, SHIFT_COLS), jnp.float32),
        'w0': jax.random.uniform(ks[13], (L, N_DIR, D_A), jnp.float32, -6.0, -1.0),
        'w2': nrm(14, (L, N_DIR, DECAY_LORA, D_A), 0.1 * DECAY_LORA ** -0.5),
        'a0': nrm(15, (L, N_DIR, D_A), 0.1),
        'a2': nrm(16, (L, N_DIR, ICLR_LORA, D_A), 0.1 * ICLR_LORA ** -0.5),
        'g2': nrm(17, (L, GATE_LORA, D_A), GATE_LORA ** -0.5),
        'k_k': 0.85 + nrm(18, (L, D_A), 0.05),
        'k_a': 1.0 + nrm(19, (L, D_A), 0.05),
        'r_k': nrm(20, (L, D_A), 0.1),
        'ln_x_w': 1.0 + nrm(21, (L, D_A), 0.05),
        'ln_x_b': nrm(22, (L, D_A), 0.02),
        'w_a_out': nrm(23, (L, D_A, D), D_A ** -0.5),
        'w_pool': nrm(24, (L, len(POOL_WINDOWS), POOL_GROUP, POOL_GROUP), POOL_GROUP ** -0.5),
        'pool_scale': 1.0 + nrm(25, (L, D_B), 0.05),
        'w_b_out': nrm(26, (L, D_B, D), D_B ** -0.5),
        'w_o': nrm(27, (L, D, D), D ** -0.5),
        'peer_wq': nrm(28, (L, D, PEER_HEADS * PEER_QDIM), D ** -0.5),
        'peer_keys': nrm(29, (L, PEER_HEADS, 2, PEER_NKEYS, PEER_HALF), PEER_HALF ** -0.5),
        'peer_u': nrm(30, (L, PEER_EXPERTS, D), D ** -0.5),
        'peer_v': nrm(31, (L, PEER_EXPERTS, D), D ** -0.5),
    }

def reference(x, c, ctx, c_ctx, w_mod, b_mod, g_pre_mix, g_post_mix, g_pre_ffn, g_post_ffn,
              w_in, b_gate, mu_shift, w0, w2, a0, a2, g2, k_k, k_a, r_k, ln_x_w, ln_x_b,
              w_a_out, w_pool, pool_scale, w_b_out, w_o, peer_wq, peer_keys, peer_u, peer_v):
    rows = x.shape[1] // GRID_W
    grid_mean = lambda u, win: box_mean_grid(u, win, rows)
    state0 = jnp.zeros((x.shape[0], N_DIR, N_HEADS_A, HEAD_A, HEAD_A), jnp.float32)
    for l in range(DEPTH):
        last = l == DEPTH - 1
        sh1, sc1, gt1, sh2, sc2, gt2 = [t[:, None, :] for t in ada_split(c, w_mod[l], b_mod[l])]
        csh1, csc1, cgt1, csh2, csc2, cgt2 = ada_split(c_ctx, w_mod[l], b_mod[l])
        hx = rms_norm(x, g_pre_mix[l]) * (1.0 + sc1) + sh1
        hc = rms_norm(ctx, g_pre_mix[l]) * (1.0 + csc1) + csh1
        zx = hx @ w_in[l]
        zc = hc @ (w_in[l][:, :SHIFT_COLS] if last else w_in[l])
        rw = (w0[l], w2[l], a0[l], a2[l], g2[l], k_k[l], k_a[l])
        prep_c = rwkv_prepare(token_shift_mix(zc[..., :SHIFT_COLS], mu_shift[l]), *rw)
        prep_x = rwkv_prepare(token_shift_mix(zx[..., :SHIFT_COLS], mu_shift[l]), *rw)
        state_ctx, yc = rwkv_scan(state0, prep_c)
        _, yx = rwkv_scan(state_ctx, prep_x)
        ro = (r_k[l], ln_x_w[l], ln_x_b[l], w_a_out[l])
        ya_x = rwkv_readout(yx, prep_x, *ro)
        mix_x = merge_branches(zx, ya_x, grid_mean, b_gate[l], w_pool[l], pool_scale[l], w_b_out[l], w_o[l])
        x = x + gt1 * rms_norm(mix_x, g_post_mix[l])
        hx2 = rms_norm(x, g_pre_ffn[l]) * (1.0 + sc2) + sh2
        x = x + gt2 * rms_norm(peer_ffn(hx2, peer_wq[l], peer_keys[l], peer_u[l], peer_v[l]), g_post_ffn[l])
        if not last:
            ya_c = rwkv_readout(yc, prep_c, *ro)
            mix_c = merge_branches(zc, ya_c, window_mean_seq, b_gate[l], w_pool[l], pool_scale[l], w_b_out[l], w_o[l])
            ctx = ctx + cgt1 * rms_norm(mix_c, g_post_mix[l])
            hc2 = rms_norm(ctx, g_pre_ffn[l]) * (1.0 + csc2) + csh2
            ctx = ctx + cgt2 * rms_norm(peer_ffn(hc2, peer_wq[l], peer_keys[l], peer_u[l], peer_v[l]), g_post_ffn[l])
    return x


_drawn_inputs = setup_inputs


def setup_inputs(seed=0):
    import zlib

    import numpy as np

    out = dict(_drawn_inputs(seed))
    spreads = {}
    factors = {'g_post_ffn': 3.79, 'b_gate': 3.617, 'w2': 5.135, 'ln_x_b': 3.492}
    for name, (base, spread) in spreads.items():
        noise = np.random.default_rng([zlib.crc32(name.encode()), seed]).standard_normal(out[name].shape)
        drawn = base * np.exp(spread * noise) if base else spread * noise
        out[name] = jnp.asarray(drawn.astype(out[name].dtype))
    for name, factor in factors.items():
        out[name] = (out[name] * factor).astype(out[name].dtype)
    return out
```

```python
import numpy as np
import concourse.bass as bass
from concourse import mybir
from contextlib import ExitStack

FP32 = mybir.dt.float32
F32R = mybir.dt.float32r
U32 = mybir.dt.uint32
ALU = mybir.AluOpType
ACT = mybir.ActivationFunctionType
AX = mybir.AxisListType

P = 128
D = 1024
KT = D // P
SEQ, CTX = 512, 256
T = CTX + SEQ
TT = SEQ // P
XT = T // P
HEAD = 64
NPAIR = D // P
NDIR = 2
CHUNK = 64
NC = T // CHUNK
CC = CTX // CHUNK
UNITS = NDIR * NC * 2
HB = 32
MODG = 12
GRID_W = 64
ROWS = SEQ // GRID_W
WINDOWS = (2, 4, 8, 16)
NEXP = 16384
HEADS, TOPK, NKEYS = 8, 16, 128
SLOTS = HEADS * TOPK
RMS_EPS, GN_EPS, L2_EPS2 = 1e-6, 64e-5, 1e-24
DECAY_C = float(np.exp(-0.5))

GV_C, GV_CCTX, GV_BMOD = 0, 8, 16
GV_GPM, GV_GPOM, GV_GPF, GV_GPOF = 64, 72, 80, 88
GV_MUL, GV_BG, GV_PS, GV_N = 96, 99, 115, 119
PV_MU, PV_W0, PV_KK, PV_KA, PV_RK, PV_LNW, PV_LNB, PV_N = 0, 3, 7, 8, 9, 10, 11, 12
RC_RA = 0
RC_KB = RC_RA + NDIR * NC * 2 * CHUNK
RC_V = RC_KB + NDIR * NC * 2 * CHUNK
RC_EC = RC_V + NDIR * T
RC_BO = RC_EC + NDIR * NC
RC_GA = RC_BO + SEQ
RC_N = RC_GA + SEQ


class Chain:

    def __init__(self, eng, sem, gate, base=0):
        self.eng, self.sem, self.gate, self.base, self.n, self.i, self.per = eng, sem, gate, base, 0, None, 0

    def loop(self, i, per):
        self.base, self.n, self.i, self.per = self.base + self.n, 0, i, per

    def end(self, trips):
        assert self.n == self.per, (self.sem, self.n, self.per)
        self.base, self.n, self.i = self.base + trips * self.per, 0, None

    def __call__(self, ins):
        ins.then_inc(self.sem, 1)
        self.n += 1
        if self.i is None:
            self.eng.wait_ge(self.sem, self.base + self.n)
        else:
            hold(self.eng, self.gate, self.sem, self.i * self.per + (self.base + self.n))


def hold(eng, gate, sem, value):
    eng.wait_ge(sem, value)
    eng.sem_inc(gate, 1)


def split_mm(tensor, out, w_hi, w_lo, x_hi, x_lo, first, last):
    tensor.matmul(out, w_hi, x_hi, start=first, stop=False)
    tensor.matmul(out, w_hi, x_lo, start=False, stop=False)
    return tensor.matmul(out, w_lo, x_hi, start=False, stop=last)


def build(nc, x, ctx_in, gvec_in, wmod, wlora_in, wpair_in, pvec_in, lora_in, wpu_in, wpool_in,
          invcnt_in, wmerge_in, wo_in, wq_in, keys_in, peer_u, peer_v, out):
    record = nc.dram_tensor("pair_record", (NPAIR, P, RC_N), FP32, kind="Internal").ap()
    tri_dram = nc.dram_tensor("tri_dram", (UNITS, CHUNK, CHUNK), FP32, kind="Internal").ap()
    inv_dram = nc.dram_tensor("inv_dram", (2, UNITS, HB, HB), FP32, kind="Internal").ap()
    m_dram = nc.dram_tensor("m_dram", (NPAIR, P, SEQ), FP32, kind="Internal").ap()
    invt_dram = nc.dram_tensor("invt_dram", (UNITS, HB, HB), FP32, kind="Internal").ap()

    stage_sems = {}

    def release(stack):
        nc.clear_and_free_semaphores(stage_sems.pop(stack))
        nc.all_engine_barrier()

    top = ExitStack()
    with top:
        def sb(stack, name, shape, dt=FP32):
            return stack.enter_context(nc.sbuf_tensor(name, shape, dt))

        def sem(stack, name):
            if stack not in stage_sems:
                stage_sems[stack] = []
                stack.callback(release, stack)
            stage_sems[stack].append(nc.alloc_semaphore(name=name))
            return stage_sems[stack][-1]

        bank = [top.enter_context(nc.psum_tensor(f"bank{i}", [P, 512], FP32)) for i in range(8)]
        ident = sb(top, "ident", [P, P])
        gv = sb(top, "gv", [P, GV_N])
        mod = sb(top, "mod", [P, 48, 2])
        colv = sb(top, "colv", [P, 4, KT])
        blk = sb(top, "blk", [P, P])
        modulate(nc, top, sb, sem, locals())
        with ExitStack() as mid:
            ht_hi = sb(mid, "ht_hi", [P, KT, T], F32R)
            ht_lo = sb(mid, "ht_lo", [P, KT, T], F32R)
            normalise(nc, sb, sem, locals())
            project(nc, sb, sem, locals())
            o_all = sb(mid, "o_all", [P, NPAIR, SEQ])
            scan(nc, sb, sem, locals())
            merge(nc, sb, sem, locals())
        tail(nc, sb, sem, locals())


def modulate(nc, top, sb, sem, g):
    gv, mod, colv, ident, blk, bank = (g[k] for k in ("gv", "mod", "colv", "ident", "blk", "bank"))
    with ExitStack() as st:
        wm = sb(st, "wm", [P, 2, KT, 512])
        modrow = sb(st, "modrow", [2, MODG * 512])
        sc = sb(st, "sc", [P, KT, 2])
        th = sb(st, "th", [P, 16])
        s_gv, s_w0, s_w1 = (sem(st, n) for n in ("gvec_loaded", "wmod0_loaded", "wmod1_loaded"))
        s_w = [s_w0, s_w1]
        s_id, s_th, s_sc, s_mm, s_ev, s_col, s_ch = (sem(st, n) for n in (
            "consts_made", "tanh_done", "silu_done", "mod_mm", "mod_copied", "mod_col", "dve_chain_a"))
        gate = {k: sem(st, "gate_a_" + k) for k in ("pe", "act")}
        with nc.Block() as block:
            @block.sync
            def _(sp):
                sp.dma_start(gv[:, :], g["gvec_in"]).then_inc(s_gv, 16)
                for b in range(2):
                    sp.dma_start(wm[:, b, :, :], g["wmod"][b].rearrange("p (k n) -> p k n", k=KT)).then_inc(s_w[b], 16)
                with sp.Fori(1, MODG // 2) as i:
                    for b in range(2):
                        sp.wait_ge(s_mm, 2 * i + (b - 1))
                        sp.dma_start(wm[:, b, :, :], g["wmod"][bass.ds(2 * i + b, 1), :, :].rearrange(
                            "o p (k n) -> (o p) k n", k=KT)).then_inc(s_w[b], 16)

            @block.gpsimd
            def _(pool):
                pool.memset(ident[:, :], 0.0).then_inc(s_id, 1)
                pool.wait_ge(s_id, 1)
                pool.memset(blk[:, :], 0.0).then_inc(s_id, 1)
                pool.wait_ge(s_id, 2)
                pool.affine_select(out=ident[:, :], in_=ident[:, :], compare_op=ALU.not_equal, fill=1.0, base=0,
                                   pattern=[[-1, P]], channel_multiplier=1).then_inc(s_id, 1)
                for h in range(2):
                    pool.wait_ge(s_id, 3 + h)
                    pool.memset(blk[64 * h:64 * h + 64, 64 * h:64 * h + 64], 1.0).then_inc(s_id, 1)

            @block.scalar
            def _(act):
                act.wait_ge(s_gv, 16)
                act.activation(th[:, :], gv[:, GV_C:GV_C + 16], ACT.Tanh, scale=0.5).then_inc(s_th, 1)
                with act.Fori(0, MODG // 2) as i:
                    for b in range(2):
                        hold(act, gate["act"], s_mm, 2 * i + (b + 1))
                        act.activation(modrow[:, bass.ds((2 * i + b) * 512, 512)], bank[b][0:2, :],
                                       ACT.Copy).then_inc(s_ev, 1)

            @block.vector
            def _(dve):
                ch = Chain(dve, s_ch, None)
                dve.wait_ge(s_th, 1)
                ch(dve.scalar_tensor_tensor(th[:, :], th[:, :], 1.0, gv[:, GV_C:GV_C + 16], ALU.add, ALU.mult))
                dve.tensor_scalar(sc[:, :, :].rearrange("p k c -> p c k"), th[:, :].rearrange("p (c k) -> p c k", c=2),
                                  0.5, None, ALU.mult).then_inc(s_sc, 1)
                dve.wait_ge(s_col, 1)
                bm = gv[:, GV_BMOD:GV_BMOD + 48]
                for c in range(2):
                    ch(dve.tensor_tensor(mod[:, :, c], bank[2][:, 0:96].rearrange("p (m c) -> p m c", c=2)[:, :, c],
                                         bm, ALU.add))
                for c in range(2):
                    ch(dve.scalar_tensor_tensor(mod[:, 8:16, c], mod[:, 8:16, c], 1.0, gv[:, GV_GPM:GV_GPM + 8],
                                                ALU.add, ALU.mult))
                ch(dve.tensor_tensor(colv[:, 0, :], mod[:, 16:24, 0], gv[:, GV_GPOM:GV_GPOM + 8], ALU.mult))
                ch(dve.scalar_tensor_tensor(colv[:, 1, :], mod[:, 32:40, 0], 1.0, gv[:, GV_GPF:GV_GPF + 8],
                                            ALU.add, ALU.mult))
                ch(dve.tensor_copy(colv[:, 2, :], mod[:, 24:32, 0]))
                ch(dve.tensor_tensor(colv[:, 3, :], mod[:, 40:48, 0], gv[:, GV_GPOF:GV_GPOF + 8], ALU.mult))

            @block.tensor
            def _(pe):
                pe.wait_ge(s_sc, 1)
                pe.wait_ge(s_id, 5)
                with pe.Fori(0, MODG // 2) as i:
                    for b in range(2):
                        hold(pe, gate["pe"], s_w[b], 16 * i + 16)
                        hold(pe, gate["pe"], s_ev, 2 * i)
                        for k in range(KT):
                            mm = pe.matmul(bank[b][0:2, :], sc[:, k, :], wm[:, b, k, :], start=k == 0, stop=k == KT - 1)
                        mm.then_inc(s_mm, 1)
                pe.wait_ge(s_ev, MODG)
                for m in range(48):
                    mm = pe.matmul(bank[2][:, 2 * m:2 * m + 2], modrow[0:2, m * P:m * P + P], ident[0:2, 0:2],
                                   start=True, stop=True)
                mm.then_inc(s_col, 1)


def normalise(nc, sb, sem, g):
    mod, ident, bank, ht_hi, ht_lo = (g[k] for k in ("mod", "ident", "bank", "ht_hi", "ht_lo"))
    with ExitStack() as st:
        xt = sb(st, "xt", [P, XT, D])
        sq = sb(st, "sq", [P, D])
        rs = sb(st, "rs", [P, XT])
        epsc = sb(st, "epsc", [P, 1])
        hf = sb(st, "hf", [P, 2, 512])
        s_x, s_ssq, s_ms, s_std, s_rs, s_xn, s_t, s_hf, s_hi, s_lo, s_eps = (sem(st, n) for n in (
            "tokens_loaded", "ssq_done", "ms_done", "std_done", "rstd_done", "tokens_scaled", "tokens_transposed",
            "modulated", "hi_done", "lo_done", "eps_set"))
        groups = [(k, a, n) for k in range(KT) for a, n in ((0, 2), (2, 4))]
        with nc.Block() as block:
            @block.sync
            def _(sp):
                sp.dma_start(xt[:, 0:2, :], g["ctx_in"].rearrange("o (t p) d -> p (o t) d", p=P)).then_inc(s_x, 16)
                sp.dma_start(xt[:, 2:6, :], g["x"].rearrange("o (t p) d -> p (o t) d", p=P)).then_inc(s_x, 16)
                sp.wait_ge(s_x, 32)

            @block.scalar
            def _(act):
                act.wait_ge(s_x, 32)
                for t in range(XT):
                    if t:
                        act.wait_ge(s_ssq, t)
                    act.activation(sq[:, :], xt[:, t, :], ACT.Square, accum_out=rs[:, t:t + 1]).then_inc(s_ssq, 1)
                act.wait_ge(s_ms, 1)
                act.activation(rs[:, :], rs[:, :], ACT.Sqrt).then_inc(s_std, 1)
                act.wait_ge(s_rs, 1)
                for t in range(XT):
                    act.activation(xt[:, t, :], xt[:, t, :], ACT.Copy, scale=rs[:, t:t + 1]).then_inc(s_xn, 1)
                for i, (k, a, n) in enumerate(groups):
                    act.wait_ge(s_hf, i + 1)
                    act.activation(ht_hi[:, k, a * P:(a + n) * P], hf[:, i % 2, 0:n * P], ACT.Copy).then_inc(s_hi, 1)

            @block.vector
            def _(dve):
                dve.wait_ge(s_ssq, XT)
                dve.tensor_scalar(rs[:, :], rs[:, :], 1.0 / D, RMS_EPS, ALU.mult, ALU.add).then_inc(s_ms, 1)
                dve.wait_ge(s_std, 1)
                dve.reciprocal(rs[:, :], rs[:, :]).then_inc(s_rs, 1)
                for i, (k, a, n) in enumerate(groups):
                    c = 1 if a == 0 else 0
                    dve.wait_ge(s_t, i + 1)
                    if i >= 2:
                        dve.wait_ge(s_hi, i - 1)
                        dve.wait_ge(s_lo, i - 1)
                    dve.tensor_scalar(hf[:, i % 2, 0:n * P], bank[i % 2][:, 0:n * P], mod[:, 8 + k, c:c + 1],
                                      mod[:, k, c:c + 1], ALU.mult, ALU.add).then_inc(s_hf, 1)
                    dve.wait_ge(s_hi, i + 1)
                    dve.tensor_tensor(ht_lo[:, k, a * P:(a + n) * P], hf[:, i % 2, 0:n * P],
                                      ht_hi[:, k, a * P:(a + n) * P].bitcast(FP32), ALU.subtract).then_inc(s_lo, 1)

            @block.tensor
            def _(pe):
                pe.wait_ge(s_xn, XT)
                for i, (k, a, n) in enumerate(groups):
                    if i >= 2:
                        pe.wait_ge(s_hf, i - 1)
                    for t in range(n):
                        tr = pe.transpose(bank[i % 2][:, t * P:t * P + P], xt[:, a + t, k * P:k * P + P], ident[:, :])
                    tr.then_inc(s_t, 1)


def project(nc, sb, sem, g):
    gv, blk, bank, ht_hi, ht_lo, record = (g[k] for k in ("gv", "blk", "bank", "ht_hi", "ht_lo", "record"))
    LORA_ORDER, PAIR_ORDER = (0, 1, 2), (1, 0, 2)
    with ExitStack() as st:
        wraw = sb(st, "wraw", [P, 3, KT, P])
        wh = sb(st, "wh", [P, 2, KT, P], F32R)
        wl = sb(st, "wl", [P, 2, KT, P], F32R)
        lw = sb(st, "lw", [P, 3, P])
        pv = sb(st, "pv", [P, PV_N])
        vv = sb(st, "vv", [P, 16])
        zp = sb(st, "zp", [P, 3, T + 4])
        zs = sb(st, "zs", [P, 3, T])
        ns = sb(st, "ns", [P, T])
        zr = sb(st, "zr", [P, 3, T])
        lin = sb(st, "lin", [P, 2, T])
        gin = sb(st, "gin", [P, SEQ])
        dl = sb(st, "dl", [P, NDIR, T])
        al = sb(st, "al", [P, NDIR, T])
        ex = sb(st, "ex", [P, NDIR, NC, CHUNK + 1])
        ei = sb(st, "ei", [P, NDIR, T])
        kk = sb(st, "kk", [P, T])
        rn = sb(st, "rn", [P, T])
        tmp = sb(st, "tmp", [P, T])
        kf = sb(st, "kf", [P, NDIR, T])
        cm = sb(st, "cm", [P, NC, CHUNK])
        rec = sb(st, "rec", [P, RC_N])
        ra = rec[:, RC_RA:RC_KB].rearrange("p (d c q s) -> p d c q s", d=NDIR, c=NC, q=2)
        kb = rec[:, RC_KB:RC_V].rearrange("p (d c q s) -> p d c q s", d=NDIR, c=NC, q=2)
        vd = rec[:, RC_V:RC_EC].rearrange("p (d t) -> p d t", d=NDIR)
        ecr = rec[:, RC_EC:RC_BO].rearrange("p (d c) -> p d c", d=NDIR)
        bo, ga = rec[:, RC_BO:RC_GA], rec[:, RC_GA:RC_N]
        (s_w, s_hi, s_lo, s_vec, s_z, s_zc, s_zs, s_sq, s_n2, s_mx, s_std, s_lw, s_lt, s_la, s_at, s_g, s_gc, s_ld,
         s_ex, s_ev, s_bk, s_bm, s_rec, s_st, s_c, s_ch, s_li, s_kfd, s_pv) = (sem(st, n) for n in (
             "weights_loaded", "weights_hi", "weights_lo", "vectors_made", "z_product", "z_copied", "z_shifted",
             "kk_squared", "kk_norm2", "kk_norm2_ready", "kk_norm", "decay_product", "decay_tanh", "rate_product",
             "rate_tanh", "gate_product", "gate_copied", "log_decay", "exp_done", "exp_neg_done", "bonus_operand",
             "bonus_product", "record_made", "record_stored", "cleared", "dve_chain_b", "lora_inputs", "kk_operand", "pair_vectors_loaded"))
        gp, ga_, gd, gs = (sem(st, "gate_b_" + k) for k in ("pe", "act", "dve", "sp"))

        def col(v, n=1):
            return vv[:, v:v + n]

        HMU, OMU, HW, HKA, OKA, HRK = 0, 3, 6, 10, 11, 12

        with nc.Block() as block:
            @block.sync
            def _(sp):
                sp.dma_start(wraw[:, :, :, :], g["wlora_in"].rearrange("p (q k n) -> p q k n", q=3, k=KT)).then_inc(s_w, 16)
                with sp.Fori(0, NPAIR) as j:
                    sp.wait_ge(s_lo, 3 * j + 3)
                    sp.wait_ge(s_hi, 3 * j + 3)
                    sp.dma_start(wraw[:, :, :, :], g["wpair_in"][bass.ds(j, 1), :, :].rearrange(
                        "o p (q k n) -> (o p) q k n", q=3, k=KT)).then_inc(s_w, 16)
                    sp.wait_ge(s_rec, j)
                    sp.dma_start(pv[:, :], g["pvec_in"][bass.ds(j, 1), :, :].rearrange("o p v -> (o p) v")).then_inc(s_pv, 16)
                    sp.dma_start(lw[:, :, :], g["lora_in"][bass.ds(j, 1), :, :].rearrange(
                        "o p (q n) -> (o p) q n", q=3)).then_inc(s_pv, 16)
                    sp.wait_ge(s_rec, j + 1)
                    sp.wait_ge(s_gc, j + 1)
                    sp.dma_start(record[bass.ds(j, 1), :, :].rearrange("o p n -> (o p) n"), rec[:, :]).then_inc(s_st, 16)
                sp.wait_ge(s_st, 16 * NPAIR)

            @block.gpsimd
            def _(pool):
                for n, ins in enumerate((lambda: pool.memset(zp[:, :, :], 0.0), lambda: pool.memset(ex[:, :, :, 0:1], 1.0),
                                         lambda: pool.memset(cm[:, :, :], 1.0), lambda: pool.memset(cm[:, :, 0:1], 0.0))):
                    ins().then_inc(s_c, 1)
                    pool.wait_ge(s_c, n + 1)

            def z_evac(act, q, n, wait, omu, lora=False):
                b = bank[0 + 2 * (q % 2)], bank[1 + 2 * (q % 2)]
                wait()
                act.activation(zp[:, q, 1:1 + CTX], b[0][:, 0:CTX], ACT.Copy).then_inc(s_zc, 1)
                act.activation(zp[:, q, CTX + 3:CTX + 3 + SEQ], b[1][:, :], ACT.Copy).then_inc(s_zc, 1)
                act.activation(zs[:, q, 0:CTX], b[0][:, 0:CTX], ACT.Copy, scale=omu).then_inc(s_zc, 1)
                act.activation(zs[:, q, CTX:T], b[1][:, :], ACT.Copy, scale=omu).then_inc(s_zc, 1)

            @block.scalar
            def _(act):
                act.wait_ge(s_w, 16)
                act.wait_ge(s_c, 4)
                for n, q in enumerate(LORA_ORDER):
                    if n >= 2:
                        act.wait_ge(s_z, n - 1)
                    act.activation(wh[:, n % 2, :, :], wraw[:, q, :, :], ACT.Copy).then_inc(s_hi, 1)
                act.wait_ge(s_vec, 1)
                for n, q in enumerate(LORA_ORDER):
                    z_evac(act, q, n, lambda: act.wait_ge(s_z, n + 1), col(OMU + q))
                act.wait_ge(s_zs, 3)
                act.activation(lin[:, 0, :], zs[:, 0, :], ACT.Tanh).then_inc(s_li, 1)
                act.activation(gin[:, :], zs[:, 2, CTX:T], ACT.Tanh, scale=0.5).then_inc(s_li, 1)
                act.wait_ge(s_li, 3)
                with act.Fori(0, NPAIR) as j:
                    for n, q in enumerate(PAIR_ORDER):
                        if n == 0:
                            hold(act, ga_, s_w, 16 * j + 32)
                        hold(act, ga_, s_z, 3 * j + (4 if n == 2 else 3))
                        act.activation(wh[:, n % 2, :, :], wraw[:, q, :, :], ACT.Copy).then_inc(s_hi, 1)
                    hold(act, ga_, s_vec, j + 2)
                    hold(act, ga_, s_rec, j)
                    for n, q in enumerate(PAIR_ORDER):
                        z_evac(act, q, n, lambda: hold(act, ga_, s_z, 3 * j + (3 + n + 1)), col(OMU + q))
                        if n == 1:
                            hold(act, ga_, s_lw, j + 1)
                            for d in range(NDIR):
                                act.activation(dl[:, d, 0:CTX], bank[6 + d][:, 0:CTX], ACT.Tanh, bias=col(HW + d),
                                               scale=0.5).then_inc(s_lt, 1)
                                act.activation(dl[:, d, CTX:T], bank[4 + d][:, :], ACT.Tanh, bias=col(HW + d),
                                               scale=0.5).then_inc(s_lt, 1)
                    hold(act, ga_, s_la, j + 1)
                    for d in range(NDIR):
                        act.activation(al[:, d, 0:CTX], bank[6 + d][:, 0:CTX], ACT.Tanh, bias=col(HW + 2 + d),
                                       scale=0.5).then_inc(s_at, 1)
                        act.activation(al[:, d, CTX:T], bank[4 + d][:, :], ACT.Tanh, bias=col(HW + 2 + d),
                                       scale=0.5).then_inc(s_at, 1)
                    hold(act, ga_, s_kfd, j + 1)
                    act.activation(tmp[:, :], kk[:, :], ACT.Square).then_inc(s_sq, 1)
                    hold(act, ga_, s_g, j + 1)
                    hold(act, ga_, s_st, 16 * j)
                    act.activation(ga, bank[4][:, :], ACT.Copy).then_inc(s_gc, 1)
                    hold(act, ga_, s_ld, j + 1)
                    for d in range(NDIR):
                        act.activation(ex[:, d, :, 1:CHUNK + 1], dl[:, d, :].rearrange("p (c s) -> p c s", c=NC),
                                       ACT.Exp).then_inc(s_ex, 1)
                        act.activation(ei[:, d, :], dl[:, d, :], ACT.Exp, scale=-1.0).then_inc(s_ex, 1)
                    hold(act, ga_, s_mx, j + 1)
                    act.activation(rn[:, :], rn[:, :], ACT.Sqrt).then_inc(s_std, 1)

            @block.vector
            def _(dve):
                ch = Chain(dve, s_ch, gd)

                def vectors(mu, n_mu):
                    ch(dve.tensor_scalar(vv[:, HMU:HMU + 3], mu, 0.5, None, ALU.mult))
                    return dve.tensor_scalar(vv[:, OMU:OMU + 3], mu, -1.0, 1.0, ALU.mult, ALU.add)

                def low_half(n, q):
                    dve.tensor_tensor(wl[:, n % 2, :, :], wraw[:, q, :, :], wh[:, n % 2, :, :].bitcast(FP32),
                                      ALU.subtract).then_inc(s_lo, 1)

                def shift(q):
                    for a, o, m in ((0, 0, CTX), (CTX, CTX + 2, SEQ)):
                        ch(dve.tensor_tensor(ns[:, a:a + m], zp[:, q, o:o + m], zp[:, q, o + 2:o + 2 + m], ALU.add))
                    ch(dve.scalar_tensor_tensor(zs[:, q, :], ns[:, :], col(HMU + q), zs[:, q, :], ALU.mult, ALU.add))

                def reverse(dst, src):
                    ch(dve.tensor_copy(dst[:, 0:CTX], src[:, 0:CTX][:, ::-1]))
                    ch(dve.tensor_copy(dst[:, CTX:T], src[:, CTX:T][:, ::-1]))

                ch(vectors(gv[:, GV_MUL:GV_MUL + 3], 3))
                dve.sem_inc(s_vec, 1)
                for n, q in enumerate(LORA_ORDER):
                    dve.wait_ge(s_hi, n + 1)
                    if n >= 2:
                        dve.wait_ge(s_z, n - 1)
                    low_half(n, q)
                for n, q in enumerate(LORA_ORDER):
                    dve.wait_ge(s_zc, 4 * n + 4)
                    shift(q)
                dve.sem_inc(s_zs, 3)
                dve.wait_ge(s_li, 2)
                H = slice(64, P)
                ch(dve.tensor_copy(lin[:, 1, :], zs[:, 1, :]))
                ch(dve.tensor_scalar(gin[:, :], gin[:, :], 0.5, 0.5, ALU.mult, ALU.add))
                ch(dve.tensor_copy(tmp[H, :], lin[H, 0, :]))
                reverse(lin[H, 0, :], tmp[H, :])
                reverse(lin[H, 1, :], zs[H, 1, :])
                dve.sem_inc(s_li, 1)

                with dve.Fori(0, NPAIR) as j:
                    ch.loop(j, DVE_B_STEPS)
                    hold(dve, gd, s_pv, 32 * j + 32)
                    ch(vectors(pv[:, PV_MU:PV_MU + 3], 3))
                    ch(dve.tensor_scalar(col(HW, 4), pv[:, PV_W0:PV_W0 + 4], 0.5, None, ALU.mult))
                    ch(dve.tensor_scalar(col(HKA), pv[:, PV_KA:PV_KA + 1], 0.5, None, ALU.mult))
                    ch(dve.tensor_scalar(col(OKA), pv[:, PV_KA:PV_KA + 1], -0.5, 1.0, ALU.mult, ALU.add))
                    ch(dve.tensor_scalar(col(HRK), pv[:, PV_RK:PV_RK + 1], 0.5, None, ALU.mult))
                    dve.sem_inc(s_vec, 1)
                    for n, q in enumerate(PAIR_ORDER):
                        hold(dve, gd, s_hi, 3 * j + (3 + n + 1))
                        low_half(n, q)
                    for n, q in enumerate(PAIR_ORDER):
                        hold(dve, gd, s_zc, 12 * j + (12 + 4 * n + 4))
                        shift(q)
                        if q == 1:
                            ch(dve.tensor_scalar(kk[:, :], zs[:, 1, :], pv[:, PV_KK:PV_KK + 1], None, ALU.mult))
                            dve.sem_inc(s_kfd, 1)
                    hold(dve, gd, s_n2, j + 1)
                    ch(dve.tensor_scalar(rn[:, 0:CTX], bank[2][:, 0:CTX], L2_EPS2, None, ALU.max))
                    ch(dve.tensor_scalar(rn[:, CTX:T], bank[3][:, :], L2_EPS2, None, ALU.max))
                    hold(dve, gd, s_lt, 4 * j + 4)
                    for d in range(NDIR):
                        ch(dve.tensor_scalar(dl[:, d, :], dl[:, d, :], -0.5 * DECAY_C, -0.5 * DECAY_C, ALU.mult, ALU.add))
                        ch(dve.tensor_tensor_scan(dl[:, d, :], cm[:, :, :].rearrange("p c s -> p (c s)"), dl[:, d, :],
                                                  0.0, ALU.mult, ALU.add))
                    dve.sem_inc(s_ld, 1)
                    dve.sem_inc(s_mx, 1)
                    hold(dve, gd, s_st, 16 * j)
                    reverse(zr[:, 0, :], zs[:, 0, :])
                    reverse(zr[:, 1, :], zs[:, 1, :])
                    ch(dve.tensor_copy(vd[:, 0, :], zs[:, 2, :]))
                    reverse(vd[:, 1, :], zs[:, 2, :])
                    hold(dve, gd, s_at, 4 * j + 4)
                    for d in range(NDIR):
                        ch(dve.tensor_scalar(kf[:, d, :], al[:, d, :], col(HKA), col(OKA), ALU.mult, ALU.add))
                        ch(dve.tensor_scalar(al[:, d, :], al[:, d, :], 0.5, 0.5, ALU.mult, ALU.add))
                    ch(dve.tensor_tensor(tmp[:, 0:SEQ], kf[:, 0, CTX:T], kf[:, 1, CTX:T][:, ::-1], ALU.add))
                    ch(dve.tensor_tensor(tmp[:, 0:SEQ], tmp[:, 0:SEQ], zs[:, 1, CTX:T], ALU.mult))
                    ch(dve.scalar_tensor_tensor(tmp[:, 0:SEQ], tmp[:, 0:SEQ], col(HRK), zs[:, 0, CTX:T],
                                                ALU.mult, ALU.mult))
                    dve.sem_inc(s_bk, 1)
                    hold(dve, gd, s_std, j + 1)
                    ch(dve.reciprocal(rn[:, :], rn[:, :]))
                    ch(dve.tensor_tensor(kk[:, :], kk[:, :], rn[:, :], ALU.mult))
                    reverse(zr[:, 2, :], kk[:, :])
                    hold(dve, gd, s_ex, 4 * j + 4)
                    for d in range(NDIR):
                        r, k, u = (zs[:, 0, :], zs[:, 1, :], kk[:, :]) if d == 0 else (zr[:, 0, :], zr[:, 1, :], zr[:, 2, :])
                        cs = lambda a: a.rearrange("p (c s) -> p c s", c=NC)
                        ch(dve.tensor_tensor(ra[:, d, :, 0, :], cs(r), ex[:, d, :, 1:CHUNK + 1], ALU.mult))
                        ch(dve.scalar_tensor_tensor(ra[:, d, :, 1, :], cs(u), -1.0, ex[:, d, :, 0:CHUNK],
                                                    ALU.mult, ALU.mult))
                        ch(dve.tensor_tensor(kf[:, d, :], kf[:, d, :], k, ALU.mult))
                        ch(dve.tensor_tensor(kb[:, d, :, 0, :], cs(kf[:, d, :]), cs(ei[:, d, :]), ALU.mult))
                        ch(dve.tensor_tensor(al[:, d, :], al[:, d, :], u, ALU.mult))
                        ch(dve.tensor_tensor(kb[:, d, :, 1, :], cs(al[:, d, :]), cs(ei[:, d, :]), ALU.mult))
                        ch(dve.tensor_copy(ecr[:, d, :], ex[:, d, :, CHUNK]))
                    hold(dve, gd, s_bm, j + 1)
                    ch(dve.tensor_tensor(bo, bank[5][:, :], zs[:, 2, CTX:T], ALU.mult))
                    dve.sem_inc(s_rec, 1)
                ch.end(NPAIR)

            @block.tensor
            def _(pe):
                def z_tile(q, n):
                    b = bank[0 + 2 * (q % 2)], bank[1 + 2 * (q % 2)]
                    for lo, hi, o in ((0, CTX, b[0][:, 0:CTX]), (CTX, T, b[1][:, :])):
                        for k in range(KT):
                            mm = split_mm(pe, o, wh[:, n % 2, k, :], wl[:, n % 2, k, :], ht_hi[:, k, lo:hi],
                                          ht_lo[:, k, lo:hi], k == 0, k == KT - 1)
                    mm.then_inc(s_z, 1)

                def lora(i, last_sem):
                    for d in range(NDIR):
                        R = slice(64 * d, 64 * d + 64)
                        pe.matmul(bank[6 + d][:, 0:CTX], lw[R, i, :], lin[R, i, 0:CTX], start=True, stop=True)
                        mm = pe.matmul(bank[4 + d][:, :], lw[R, i, :], lin[R, i, CTX:T], start=True, stop=True)
                    mm.then_inc(last_sem, 1)

                for n, q in enumerate(LORA_ORDER):
                    pe.wait_ge(s_lo, n + 1)
                    if n >= 2:
                        pe.wait_ge(s_zc, 4 * (n - 1))
                    z_tile(q, n)
                pe.wait_ge(s_li, 3)
                with pe.Fori(0, NPAIR) as j:
                    for n, q in enumerate(PAIR_ORDER):
                        hold(pe, gp, s_lo, 3 * j + (3 + n + 1))
                        hold(pe, gp, s_zc, 12 * j + (20 if n == 2 else 12))
                        if n == 0:
                            hold(pe, gp, s_mx, j)
                        z_tile(q, n)
                        if n == 1:
                            hold(pe, gp, s_at, 4 * j)
                            hold(pe, gp, s_gc, j)
                            hold(pe, gp, s_rec, j)
                            hold(pe, gp, s_pv, 32 * j + 32)
                            lora(0, s_lw)
                    hold(pe, gp, s_lt, 4 * j + 4)
                    lora(1, s_la)
                    hold(pe, gp, s_sq, j + 1)
                    hold(pe, gp, s_zc, 12 * j + 16)
                    pe.matmul(bank[2][:, 0:CTX], blk[:, :], tmp[:, 0:CTX], start=True, stop=True)
                    pe.matmul(bank[3][:, :], blk[:, :], tmp[:, CTX:T], start=True, stop=True).then_inc(s_n2, 1)
                    hold(pe, gp, s_at, 4 * j + 4)
                    pe.matmul(bank[4][:, :], lw[:, 2, :], gin[:, :], start=True, stop=True).then_inc(s_g, 1)
                    hold(pe, gp, s_bk, j + 1)
                    pe.matmul(bank[5][:, :], blk[:, :], tmp[:, 0:SEQ], start=True, stop=True).then_inc(s_bm, 1)


DVE_B_STEPS = 55


def scan(nc, sb, sem, g):
    ident, blk, bank, o_all, record = (g[k] for k in ("ident", "blk", "bank", "o_all", "record"))
    tri_dram, inv_dram, invt_dram, gv = (g[k] for k in ("tri_dram", "inv_dram", "invt_dram", "gv"))
    LO, HI = slice(0, 64), slice(64, P)
    B1, B2 = slice(64, 96), slice(96, P)
    XC = NC - CC
    with ExitStack() as st:
        rec = sb(st, "rec2", [P, RC_N])
        ra = rec[:, RC_RA:RC_KB].rearrange("p (d c q s) -> p d c q s", d=NDIR, c=NC, q=2)
        kb = rec[:, RC_KB:RC_V].rearrange("p (d c q s) -> p d c q s", d=NDIR, c=NC, q=2)
        vd = rec[:, RC_V:RC_EC].rearrange("p (d t) -> p d t", d=NDIR)
        ecr = rec[:, RC_EC:RC_BO].rearrange("p (d c) -> p d c", d=NDIR)
        bo, ga = rec[:, RC_BO:RC_GA], rec[:, RC_GA:RC_N]
        pv = sb(st, "pv2", [P, PV_N])
        kbt = sb(st, "kbt", [P, NDIR, NC, P])
        vu = sb(st, "vu", [P, NDIR, NC, 2, HEAD])
        am = sb(st, "am", [P, NDIR, NC, 2, P])
        zi = sb(st, "zi", [P, NDIR, NC, 2, CHUNK])
        xi = sb(st, "xi", [P, NDIR, NC, 2, HB])
        hs = sb(st, "hs", [P, NDIR, NC + 1, HEAD])
        he = sb(st, "he", [P, NDIR, HEAD])
        qs = sb(st, "qs", [P, 2, NDIR, HEAD])
        mask = sb(st, "mask", [P, P])
        eye = sb(st, "eye", [96, HB, HB])
        gt = sb(st, "gt", [96, HB, HB])
        gz = sb(st, "gz", [96, HB, HB])
        gx = sb(st, "gx", [96, HB, HB])
        gm = sb(st, "gm", [96, HB, HB])
        y = sb(st, "y", [P, SEQ])
        yc = sb(st, "yc", [P, SEQ])
        ysq = sb(st, "ysq", [P, SEQ])
        b64 = sb(st, "b64", [P, P])
        epsg = sb(st, "epsg", [P, 1])
        (s_rec, s_c, s_vt, s_vc, s_kt, s_kc, s_a, s_am, s_tri, s_gt, s_inv, s_io, s_il, s_r1, s_r1c, s_r2, s_r2c, s_p,
         s_pc, s_q, s_qs, s_u, s_uc, s_h, s_hs, s_he, s_y, s_yc, s_mu, s_cen, s_sq, s_var, s_vs, s_std, s_o, s_ch,
         s_yd) = (sem(st, n) for n in (
             "record_loaded", "consts_c", "v_transposed", "v_copied", "kb_transposed", "kb_copied", "a_product",
             "a_masked", "triangles_out", "triangles_in", "inverted", "inverse_out", "inverse_in", "a21_x11",
             "a21_x11_copied", "z12", "z12_copied", "akv", "akv_copied", "q_product", "q_ready", "u_product", "u_ready",
             "h_product", "state_ready", "state_decayed", "y_products", "y_ready", "mean_product", "centred", "squared",
             "var_product", "var_ready", "std_ready", "readout_ready", "dve_chain_c", "y_summed"))
        gp, ga_, gd, gs = (sem(st, "gate_c_" + k) for k in ("pe", "act", "dve", "sp"))
        units = lambda a: a.rearrange("p d c h s -> p (d c h) s")

        with nc.Block() as block:
            @block.gpsimd
            def _(pool):
                made = 0

                def done(ins):
                    nonlocal made
                    made += 1
                    ins.then_inc(s_c, 1)
                    pool.wait_ge(s_c, made)

                done(pool.memset(mask[:, :], 1.0))
                done(pool.memset(eye[:, :, :], 0.0))
                done(pool.memset(zi[:, :, :, :, :], 0.0))
                done(pool.memset(hs[:, :, 0:1, :], 0.0))
                done(pool.tensor_scalar(b64[:, :], blk[:, :], 1.0 / HEAD, 0.0, ALU.mult, ALU.add))
                for h in range(2):
                    R = slice(64 * h, 64 * h + 64)
                    done(pool.affine_select(out=mask[R, 0:64], in_=mask[R, 0:64], compare_op=ALU.is_ge, fill=0.0, base=0,
                                            pattern=[[1, 64]], channel_multiplier=-1))
                    done(pool.affine_select(out=mask[R, 64:P], in_=mask[R, 64:P], compare_op=ALU.is_gt, fill=0.0, base=0,
                                            pattern=[[1, 64]], channel_multiplier=-1))
                done(pool.affine_select(out=eye[:, :, :], in_=eye[:, :, :], compare_op=ALU.not_equal, fill=1.0, base=0,
                                        pattern=[[1, HB], [-1, HB]], channel_multiplier=0))

            @block.sync
            def _(sp):
                with sp.Fori(0, NPAIR) as j:
                    sp.wait_ge(s_o, j)
                    sp.dma_start(rec[:, :], record[bass.ds(j, 1), :, :].rearrange("o p n -> (o p) n")).then_inc(s_rec, 16)
                    sp.dma_start(pv[:, :], g["pvec_in"][bass.ds(j, 1), :, :].rearrange("o p v -> (o p) v")).then_inc(s_rec, 16)
                    sp.wait_ge(s_am, 12 * j + 12)
                    sp.dma_start(tri_dram.rearrange("u s t -> s u t"), units(am)[HI, :, HI]).then_inc(s_tri, 16)
                    sp.wait_ge(s_tri, 16 * j + 16)
                    for h in range(2):
                        sp.dma_start(gt[UNITS * h:UNITS * h + UNITS, :, :],
                                     tri_dram[:, HB * h:HB * h + HB, HB * h:HB * h + HB]).then_inc(s_gt, 16)
                    sp.wait_ge(s_inv, j + 1)
                    sp.dma_start(inv_dram.rearrange("h u s t -> (h u) s t"), gz[:, :, :]).then_inc(s_io, 16)
                    sp.dma_start(invt_dram, gx[0:UNITS, :, :]).then_inc(s_io, 16)
                    sp.wait_ge(s_io, 32 * j + 32)
                    for h in range(2):
                        R = slice(64 + HB * h, 64 + HB * h + HB)
                        sp.dma_start(units(zi)[R, :, HB * h:HB * h + HB], inv_dram[h].rearrange("u s t -> s u t")).then_inc(s_il, 16)
                    sp.dma_start(units(xi)[B1, :, :], invt_dram.rearrange("u s t -> s u t")).then_inc(s_il, 16)
                sp.wait_ge(s_o, NPAIR)

            @block.scalar
            def _(act):
                with act.Fori(0, NPAIR) as j:
                    for n in range(6):
                        d, c = divmod(4 * n, NC)
                        hold(act, ga_, s_vt, 6 * j + (n + 1))
                        act.activation(vu[LO, d, c:c + 4, :, :].rearrange("p c h v -> p (c h v)"), bank[n % 2][LO, :],
                                       ACT.Copy).then_inc(s_vc, 1)
                    for n in range(6):
                        d, c = divmod(4 * n, NC)
                        hold(act, ga_, s_kt, 6 * j + (n + 1))
                        act.activation(kbt[:, d, c:c + 4, :].rearrange("p c k -> p (c k)"), bank[2 + n % 2][:, :],
                                       ACT.Copy).then_inc(s_kc, 1)
                    for n in range(6):
                        hold(act, ga_, s_p, 6 * j + (n + 1))
                        hold(act, ga_, s_r1, 3 * j + 3)
                        act.activation(units(am)[HI, 8 * n:8 * n + 8, HI],
                                       bank[4 + n % 2][HI, :].rearrange("p (u v) -> p u v", v=HEAD), ACT.Copy).then_inc(s_pc, 1)
                    for n in range(3):
                        hold(act, ga_, s_r1, 3 * j + (n + 1))
                        act.activation(units(xi)[B2, 16 * n:16 * n + 16, :],
                                       bank[n][B2, :].rearrange("p (u t) -> p u t", t=HB), ACT.Copy).then_inc(s_r1c, 1)
                    for n in range(3):
                        hold(act, ga_, s_r2, 3 * j + (n + 1))
                        act.activation(units(zi)[B1, 16 * n:16 * n + 16, HB:CHUNK],
                                       bank[n][B1, :].rearrange("p (u t) -> p u t", t=HB), ACT.Copy).then_inc(s_r2c, 1)
                    for c in range(NC):
                        if c:
                            hold(act, ga_, s_hs, NC * j + c)
                        for d in range(NDIR):
                            act.activation(he[:, d, :], hs[:, d, c, :], ACT.Copy, scale=ecr[:, d, c:c + 1]).then_inc(s_he, 1)
                        hold(act, ga_, s_u, NC * j + (c + 1))
                        act.activation(vu[HI, :, c, :, :], bank[2][HI, 0:4 * HEAD].rearrange(
                            "p (d h v) -> p d h v", d=NDIR, h=2), ACT.Copy).then_inc(s_uc, 1)
                    hold(act, ga_, s_y, j + 1)
                    act.activation(y[:, :], bank[4][:, :], ACT.Copy).then_inc(s_yc, 1)
                    hold(act, ga_, s_cen, j + 1)
                    act.activation(ysq[:, :], yc[:, :], ACT.Square).then_inc(s_sq, 1)
                    hold(act, ga_, s_vs, j + 1)
                    act.activation(ysq[:, :], ysq[:, :], ACT.Sqrt).then_inc(s_std, 1)

            @block.vector
            def _(dve):
                ch = Chain(dve, s_ch, gd)
                dve.wait_ge(s_c, 10)
                with dve.Fori(0, NPAIR) as j:
                    ch.loop(j, DVE_C_STEPS)
                    for n in range(12):
                        d, h, c = n // 6, n // 3 % 2, 4 * (n % 3)
                        hold(dve, gd, s_a, 12 * j + (n + 1))
                        dve.tensor_tensor(am[:, d, c:c + 4, h, :], bank[4 + n % 4][:, :].rearrange("p (c t) -> p c t", c=4),
                                          mask[:, :].unsqueeze(1).broadcast_to((P, 4, P)), ALU.mult).then_inc(s_am, 1)
                    ch(dve.tensor_copy(gz[:, :, :], eye[:, :, :]))
                    hold(dve, gd, s_gt, 32 * j + 32)
                    for u in range(HB - 1):
                        n, m = u + 1, HB - 1 - u
                        o = gm[:, 0:n, 0:m]
                        ch(dve.tensor_tensor(o, gz[:, 0:n, u:u + 1].broadcast_to((96, n, m)),
                                             gt[:, u:u + 1, n:HB].broadcast_to((96, n, m)), ALU.mult))
                        ch(dve.tensor_tensor(gz[:, 0:n, n:HB], gz[:, 0:n, n:HB], o, ALU.add))
                    ch(dve.tensor_copy(gx[:, :, :], gz[:, :, :].rearrange("p s t -> p t s")))
                    dve.sem_inc(s_inv, 1)
                    for c in range(NC):
                        hold(dve, gd, s_q, NC * j + (c + 1))
                        if c == 0:
                            hold(dve, gd, s_pc, 6 * j + 6)
                        for h in range(2):
                            dve.tensor_tensor(qs[HI, h, :, :], bank[h][HI, 0:2 * HEAD].rearrange("p (d v) -> p d v", d=2),
                                              am[HI, :, c, h, HI], ALU.add).then_inc(s_qs, 1)
                        hold(dve, gd, s_h, NC * j + (c + 1))
                        hold(dve, gd, s_he, 2 * NC * j + (2 * c + 2))
                        for d in range(NDIR):
                            ch(dve.scalar_tensor_tensor(hs[:, d, c + 1, :], bank[3][:, d * HEAD:d * HEAD + HEAD],
                                                        ecr[:, d, c:c + 1], he[:, d, :], ALU.mult, ALU.add))
                        dve.sem_inc(s_hs, 1)
                    hold(dve, gd, s_yc, j + 1)
                    ch(dve.tensor_tensor(y[:, :], y[:, :], bank[6][:, :], ALU.add))
                    ch(dve.tensor_tensor(y[:, :], y[:, :], bank[5][:, ::-1], ALU.add))
                    ch(dve.tensor_tensor(y[:, :], y[:, :], bank[7][:, ::-1], ALU.add))
                    dve.sem_inc(s_yd, 1)
                    hold(dve, gd, s_mu, j + 1)
                    ch(dve.tensor_tensor(yc[:, :], y[:, :], bank[0][:, :], ALU.subtract))
                    dve.sem_inc(s_cen, 1)
                    hold(dve, gd, s_var, j + 1)
                    ch(dve.tensor_scalar(ysq[:, :], bank[1][:, :], GN_EPS, None, ALU.add))
                    dve.sem_inc(s_vs, 1)
                    hold(dve, gd, s_std, j + 1)
                    ch(dve.reciprocal(ysq[:, :], ysq[:, :]))
                    ch(dve.scalar_tensor_tensor(yc[:, :], yc[:, :], pv[:, PV_LNW:PV_LNW + 1], ysq[:, :], ALU.mult, ALU.mult))
                    ch(dve.tensor_tensor(yc[:, :], yc[:, :], bo, ALU.add))
                    ch(dve.scalar_tensor_tensor(o_all[:, bass.ds(j, 1), :].rearrange("p o t -> p (o t)"), yc[:, :],
                                                pv[:, PV_LNB:PV_LNB + 1], ga, ALU.add, ALU.mult))
                    dve.sem_inc(s_o, 1)
                ch.end(NPAIR)

            @block.tensor
            def _(pe):
                pe.wait_ge(s_c, 10)
                with pe.Fori(0, NPAIR) as j:
                    hold(pe, gp, s_rec, 32 * j + 32)
                    hold(pe, gp, s_o, j)
                    for n in range(6):
                        d, c = divmod(4 * n, NC)
                        if n >= 2:
                            hold(pe, gp, s_vc, 6 * j + (n - 1))
                        for i in range(4):
                            t = (c + i) * CHUNK
                            mm = pe.transpose(bank[n % 2][LO, i * P:i * P + P], vd[:, d, t:t + CHUNK], ident[:, :])
                        mm.then_inc(s_vt, 1)
                    for n in range(6):
                        d, c = divmod(4 * n, NC)
                        if n >= 2:
                            hold(pe, gp, s_kc, 6 * j + (n - 1))
                        for i in range(4):
                            mm = pe.transpose(bank[2 + n % 2][:, i * P:i * P + P],
                                              kb[:, d, c + i, :, :].rearrange("p q s -> p (q s)"), ident[:, :])
                        mm.then_inc(s_kt, 1)
                    for n in range(12):
                        d, h, c = n // 6, n // 3 % 2, 4 * (n % 3)
                        R = slice(64 * h, 64 * h + 64)
                        if n >= 4:
                            hold(pe, gp, s_am, 12 * j + (n - 3))
                        for i in range(4):
                            mm = pe.matmul(bank[4 + n % 4][:, i * P:i * P + P],
                                           kb[R, d, c + i, :, :].rearrange("p q s -> p (q s)"),
                                           ra[R, d, c + i, :, :].rearrange("p q s -> p (q s)"), start=True, stop=True)
                        mm.then_inc(s_a, 1)
                    hold(pe, gp, s_vc, 6 * j + 6)
                    hold(pe, gp, s_am, 12 * j + 12)
                    vuu, amu, ziu, xiu = units(vu), units(am), units(zi), units(xi)
                    def a21(n):
                        for i in range(16):
                            u = 16 * n + i
                            mm = pe.matmul(bank[n][B2, HB * i:HB * i + HB], amu[B1, u, 64 + HB:P], xiu[B1, u, :],
                                           start=True, stop=True)
                        mm.then_inc(s_r1, 1)

                    def akv(n):
                        for i in range(8):
                            u = 8 * n + i
                            mm = pe.matmul(bank[4 + n % 2][HI, HEAD * i:HEAD * i + HEAD], amu[LO, u, HI], vuu[LO, u, :],
                                           start=True, stop=True)
                        mm.then_inc(s_p, 1)

                    akv(0)
                    akv(1)
                    hold(pe, gp, s_il, 48 * j + 48)
                    hold(pe, gp, s_kc, 6 * j + 6)
                    for n in range(3):
                        a21(n)
                    for n in range(2, 6):
                        hold(pe, gp, s_pc, 6 * j + (n - 1))
                        akv(n)
                    for n in range(3):
                        hold(pe, gp, s_r1c, 3 * j + (n + 1))
                        for i in range(16):
                            u = 16 * n + i
                            mm = pe.matmul(bank[n][B1, HB * i:HB * i + HB], xiu[B2, u, :], ziu[B2, u, HB:CHUNK],
                                           start=True, stop=True)
                        mm.then_inc(s_r2, 1)
                    hold(pe, gp, s_r2c, 3 * j + 3)
                    for c in range(NC):
                        hold(pe, gp, s_hs, NC * j + c)
                        for h in range(2):
                            R = slice(64 * h, 64 * h + 64)
                            for d in range(NDIR):
                                mm = pe.matmul(bank[h][HI, d * HEAD:d * HEAD + HEAD], ra[R, d, c, 1, :], hs[R, d, c, :],
                                               start=True, stop=True)
                        mm.then_inc(s_q, 1)
                        hold(pe, gp, s_qs, 2 * NC * j + (2 * c + 2))
                        for d in range(NDIR):
                            for h in range(2):
                                o = (2 * d + h) * HEAD
                                mm = pe.matmul(bank[2][HI, o:o + HEAD], zi[HI, d, c, h, :], qs[HI, h, d, :],
                                               start=True, stop=True)
                        mm.then_inc(s_u, 1)
                        hold(pe, gp, s_uc, NC * j + (c + 1))
                        for d in range(NDIR):
                            for h in range(2):
                                R = slice(64 * h, 64 * h + 64)
                                mm = pe.matmul(bank[3][R, d * HEAD:d * HEAD + HEAD], kbt[:, d, c, R], vu[:, d, c, h, :],
                                               start=True, stop=True)
                        mm.then_inc(s_h, 1)
                    hold(pe, gp, s_pc, 6 * j + 6)
                    for d in range(NDIR):
                        for h in range(2):
                            R = slice(64 * h, 64 * h + 64)
                            for c in range(XC):
                                o = slice(c * CHUNK, c * CHUNK + CHUNK)
                                pe.matmul(bank[4 + d][R, o], hs[R, d, CC + c, :], ra[R, d, CC + c, 0, :], start=True, stop=True)
                        for h in range(2):
                            R = slice(64 * h, 64 * h + 64)
                            for c in range(XC):
                                o = slice(c * CHUNK, c * CHUNK + CHUNK)
                                mm = pe.matmul(bank[6 + d][R, o], vu[:, d, CC + c, h, :], am[:, d, CC + c, h, LO],
                                               start=True, stop=True)
                    mm.then_inc(s_y, 1)
                    hold(pe, gp, s_yd, j + 1)
                    pe.matmul(bank[0][:, :], b64[:, :], y[:, :], start=True, stop=True).then_inc(s_mu, 1)
                    hold(pe, gp, s_sq, j + 1)
                    pe.matmul(bank[1][:, :], b64[:, :], ysq[:, :], start=True, stop=True).then_inc(s_var, 1)


DVE_C_STEPS = 97


def merge(nc, sb, sem, g):
    gv, bank, ht_hi, ht_lo, o_all, m_dram = (g[k] for k in ("gv", "bank", "ht_hi", "ht_lo", "o_all", "m_dram"))
    NW = len(WINDOWS)
    PAD = max(WINDOWS) // 2
    PR, PC = ROWS + 2 * PAD, GRID_W + 2 * PAD
    NM = 3 * KT + NW
    with ExitStack() as st:
        p_hi = sb(st, "p_hi", [P, NW, SEQ], F32R)
        p_lo = sb(st, "p_lo", [P, NW, SEQ], F32R)
        with ExitStack() as s1:
            wu = sb(s1, "wu", [P, NW, KT, P])
            wuh = sb(s1, "wuh", [P, 2, KT, P], F32R)
            wul = sb(s1, "wul", [P, 2, KT, P], F32R)
            wp = sb(s1, "wp", [P, NW, P])
            icn = sb(s1, "icn", [P, NW, SEQ])
            u0, ca, cb, ea, eb = (sb(s1, n, [P, PR, PC]) for n in ("u0", "ca", "cb", "ea", "eb"))
            pl = sb(s1, "pl", [P, SEQ])
            pf = sb(s1, "pf", [P, SEQ])
            s_w, s_z0, s_hi, s_lo, s_u, s_ue, s_pl, s_pp, s_pe, s_ph, s_plo, s_ch = (sem(s1, n) for n in (
                "pool_weights", "pool_zeroed", "pool_w_hi", "pool_w_lo", "u_made", "u_padded", "pooled",
                "pool_product", "pool_scaled", "pool_hi", "pool_lo", "dve_chain_d"))
            centre = lambda a: a[:, PAD:PAD + ROWS, PAD:PAD + GRID_W]
            grid = lambda a: a.rearrange("p (r c) -> p r c", c=GRID_W)
            with nc.Block() as block:
                def pool_out(act, q):
                    act.wait_ge(s_pp, q + 1)
                    if q:
                        act.wait_ge(s_plo, q)
                    act.activation(pf[:, :], bank[2 + q % 2][:, :], ACT.Copy, scale=gv[:, GV_PS + q:GV_PS + q + 1]).then_inc(s_pe, 1)
                    act.wait_ge(s_pe, q + 1)
                    act.activation(p_hi[:, q, :], pf[:, :], ACT.Copy).then_inc(s_ph, 1)

                def low(dve, q):
                    dve.wait_ge(s_ph, q + 1)
                    dve.tensor_tensor(p_lo[:, q, :], pf[:, :], p_hi[:, q, :].bitcast(FP32), ALU.subtract).then_inc(s_plo, 1)

                def pooled(pe, q):
                    pe.wait_ge(s_pl, q + 1)
                    if q >= 2:
                        pe.wait_ge(s_pe, q - 1)
                    pe.matmul(bank[2 + q % 2][:, :], wp[:, q, :], pl[:, :], start=True, stop=True).then_inc(s_pp, 1)

                @block.sync
                def _(sp):
                    sp.dma_start(wu[:, :, :, :], g["wpu_in"].rearrange("p (q k n) -> p q k n", q=NW, k=KT)).then_inc(s_w, 16)
                    sp.dma_start(wp[:, :, :], g["wpool_in"]).then_inc(s_w, 16)
                    sp.dma_start(icn[:, :, :], g["invcnt_in"].unsqueeze(0).broadcast_to((P, NW, SEQ))).then_inc(s_w, 16)
                    sp.wait_ge(s_w, 48)

                @block.gpsimd
                def _(pool):
                    for n, a in enumerate((u0, ca, cb)):
                        pool.memset(a[:, :, :], 0.0).then_inc(s_z0, 1)
                        pool.wait_ge(s_z0, n + 1)

                @block.scalar
                def _(act):
                    act.wait_ge(s_w, 48)
                    act.wait_ge(s_z0, 3)
                    for q in range(NW):
                        if q >= 2:
                            act.wait_ge(s_u, q - 1)
                        act.activation(wuh[:, q % 2, :, :], wu[:, q, :, :], ACT.Copy).then_inc(s_hi, 1)
                        if q:
                            pool_out(act, q - 1)
                        act.wait_ge(s_u, q + 1)
                        if q:
                            act.wait_ge(s_pl, q)
                        act.activation(centre(u0), grid(bank[q % 2][:, :]), ACT.Copy).then_inc(s_ue, 1)
                    pool_out(act, NW - 1)

                @block.vector
                def _(dve):
                    ch = Chain(dve, s_ch, None)
                    dve.wait_ge(s_z0, 3)
                    for q, w in enumerate(WINDOWS):
                        dve.wait_ge(s_hi, q + 1)
                        dve.tensor_tensor(wul[:, q % 2, :, :], wu[:, q, :, :], wuh[:, q % 2, :, :].bitcast(FP32),
                                          ALU.subtract).then_inc(s_lo, 1)
                        if q:
                            low(dve, q - 1)
                        dve.wait_ge(s_ue, q + 1)
                        src = u0
                        R = slice(PAD, PAD + ROWS)
                        for n in range(q + 1):
                            dst = (ca, cb)[n % 2]
                            m = w // 2 - (1 << n)
                            a, b = (1, 0) if n == 0 else (1 << (n - 1), 1 << (n - 1))
                            lo, hi = PAD - m, PAD + GRID_W + m
                            ch(dve.tensor_tensor(dst[:, R, lo:hi], src[:, R, lo - a:hi - a], src[:, R, lo + b:hi + b], ALU.add))
                            src = dst
                        C = slice(PAD, PAD + GRID_W)
                        for n in range(q + 1):
                            dst = (ea, eb)[n % 2]
                            m = w // 2 - (1 << n)
                            a, b = (1, 0) if n == 0 else (1 << (n - 1), 1 << (n - 1))
                            lo, hi = PAD - m, PAD + ROWS + m
                            ch(dve.tensor_tensor(dst[:, lo:hi, C], src[:, lo - a:hi - a, C], src[:, lo + b:hi + b, C], ALU.add))
                            src = dst
                        if q:
                            dve.wait_ge(s_pp, q)
                        ch(dve.tensor_tensor(grid(pl[:, :]), centre(src), grid(icn[:, q, :]), ALU.mult))
                        dve.tensor_tensor(grid(pl[:, :]), grid(pl[:, :]), centre(u0), ALU.subtract).then_inc(s_pl, 1)
                        dve.wait_ge(s_pl, q + 1)
                    low(dve, NW - 1)

                @block.tensor
                def _(pe):
                    for q in range(NW):
                        pe.wait_ge(s_lo, q + 1)
                        if q >= 2:
                            pe.wait_ge(s_ue, q - 1)
                        for k in range(KT):
                            mm = split_mm(pe, bank[q % 2][:, :], wuh[:, q % 2, k, :], wul[:, q % 2, k, :],
                                          ht_hi[:, k, CTX:T], ht_lo[:, k, CTX:T], k == 0, k == KT - 1)
                        mm.then_inc(s_u, 1)
                        if q:
                            pooled(pe, q - 1)
                    pooled(pe, NW - 1)

        wm = sb(st, "wmg", [P, NM, P])
        wh = sb(st, "wmg_hi", [P, NM, P], F32R)
        wl = sb(st, "wmg_lo", [P, NM, P], F32R)
        o_hi = sb(st, "o_hi", [P, NPAIR, SEQ], F32R)
        o_lo = sb(st, "o_lo", [P, NPAIR, SEQ], F32R)
        hbg = sb(st, "hbg", [P, 2, KT])
        hb = sb(st, "hb", [P, 2])
        tg = sb(st, "tg", [P, 2, SEQ])
        mt = sb(st, "mt", [P, SEQ])
        s_w, s_hi, s_lo, s_oh, s_ol, s_hb, s_mm, s_tg, s_m, s_st, s_ch = (sem(st, n) for n in (
            "merge_weights", "merge_hi", "merge_lo", "o_hi_made", "o_lo_made", "gate_bias", "merge_products",
            "gate_tanh", "m_made", "m_stored", "dve_chain_e"))
        gp, ga_, gd = (sem(st, "gate_e_" + k) for k in ("pe", "act", "dve"))
        with nc.Block() as block:
            @block.sync
            def _(sp):
                with sp.Fori(0, NPAIR) as j:
                    sp.wait_ge(s_lo, j)
                    sp.wait_ge(s_hi, j)
                    sp.dma_start(wm[:, :, :], g["wmerge_in"][bass.ds(j, 1), :, :].rearrange(
                        "o p (m n) -> (o p) m n", m=NM)).then_inc(s_w, 16)
                    sp.wait_ge(s_m, j + 1)
                    sp.dma_start(m_dram[bass.ds(j, 1), :, :].rearrange("o p t -> (o p) t"), mt[:, :]).then_inc(s_st, 16)
                sp.wait_ge(s_st, 16 * NPAIR)

            @block.scalar
            def _(act):
                for k in range(NPAIR):
                    act.activation(o_hi[:, k, :], o_all[:, k, :], ACT.Copy).then_inc(s_oh, 1)
                with act.Fori(0, NPAIR) as j:
                    hold(act, ga_, s_w, 16 * j + 16)
                    hold(act, ga_, s_mm, j)
                    act.activation(wh[:, :, :], wm[:, :, :], ACT.Copy).then_inc(s_hi, 1)
                    hold(act, ga_, s_hb, j + 1)
                    hold(act, ga_, s_mm, j + 1)
                    for i in range(2):
                        act.activation(tg[:, i, :], bank[i][:, :], ACT.Tanh, bias=hb[:, i:i + 1], scale=0.5).then_inc(s_tg, 1)

            @block.vector
            def _(dve):
                ch = Chain(dve, s_ch, gd)
                ch(dve.tensor_scalar(hbg[:, :, :], gv[:, GV_BG:GV_BG + 16].rearrange("p (i k) -> p i k", i=2), 0.5, None, ALU.mult))
                for k in range(NPAIR):
                    dve.wait_ge(s_oh, k + 1)
                    dve.tensor_tensor(o_lo[:, k, :], o_all[:, k, :], o_hi[:, k, :].bitcast(FP32), ALU.subtract).then_inc(s_ol, 1)
                with dve.Fori(0, NPAIR) as j:
                    ch.loop(j, 5)
                    hold(dve, gd, s_hi, j + 1)
                    dve.tensor_tensor(wl[:, :, :], wm[:, :, :], wh[:, :, :].bitcast(FP32), ALU.subtract).then_inc(s_lo, 1)
                    ch(dve.tensor_copy(hb[:, :], hbg[:, :, bass.ds(j, 1)].rearrange("p i o -> p (i o)")))
                    dve.sem_inc(s_hb, 1)
                    hold(dve, gd, s_tg, 2 * j + 2)
                    hold(dve, gd, s_st, 16 * j)
                    for i in range(2):
                        ch(dve.scalar_tensor_tensor(tg[:, i, :], tg[:, i, :], 1.0, bank[2 + i][:, :], ALU.add, ALU.mult))
                    ch(dve.tensor_tensor(mt[:, :], tg[:, 0, :], tg[:, 1, :], ALU.add))
                    ch(dve.tensor_scalar(mt[:, :], mt[:, :], 0.5, None, ALU.mult))
                    dve.sem_inc(s_m, 1)
                ch.end(NPAIR)

            @block.tensor
            def _(pe):
                pe.wait_ge(s_ol, NPAIR)
                with pe.Fori(0, NPAIR) as j:
                    hold(pe, gp, s_lo, j + 1)
                    hold(pe, gp, s_m, j)
                    w = 0
                    for i, (n, xh, xl, a) in enumerate(((KT, ht_hi, ht_lo, CTX), (KT, ht_hi, ht_lo, CTX),
                                                        (KT, o_hi, o_lo, 0), (NW, p_hi, p_lo, 0))):
                        for k in range(n):
                            mm = split_mm(pe, bank[i][:, :], wh[:, w, :], wl[:, w, :], xh[:, k, a:a + SEQ],
                                          xl[:, k, a:a + SEQ], k == 0, k == n - 1)
                            w += 1
                    mm.then_inc(s_mm, 1)


def tail(nc, sb, sem, g):
    gv, bank, colv, ident, m_dram = (g[k] for k in ("gv", "bank", "colv", "ident", "m_dram"))
    with ExitStack() as st:
        x2 = sb(st, "x2", [P, TT, D])
        h2 = sb(st, "h2", [P, TT, D])
        gt2b = sb(st, "gt2b", [P, D])
        idx = sb(st, "idx", [P, TT * SLOTS + 2 * TOPK], U32)
        pg = sb(st, "pg", [P, TT * SLOTS])
        with ExitStack() as s2:
            h2h = sb(s2, "h2h", [P, KT, SEQ], F32R)
            h2l = sb(s2, "h2l", [P, KT, SEQ], F32R)
            with ExitStack() as s1:
                out_projection(nc, s1, sb, sem, dict(g, **locals()))
            qt_ = sb(s2, "qt_", [P, 2 * HEADS, SEQ])
            with ExitStack() as s1:
                queries(nc, s1, sb, sem, dict(g, **locals()))
            with ExitStack() as s1:
                routing(nc, s1, sb, sem, dict(g, **locals()))
        experts(nc, st, sb, sem, dict(g, **locals()))


def out_projection(nc, st, sb, sem, g):
    bank, colv, ident, m_dram, x2, h2, gt2b, h2h, h2l = (g[k] for k in (
        "bank", "colv", "ident", "m_dram", "x2", "h2", "gt2b", "h2h", "h2l"))
    mr = sb(st, "mr", [P, KT, SEQ])
    mh = sb(st, "mh", [P, KT, SEQ], F32R)
    ml = sb(st, "ml", [P, KT, SEQ], F32R)
    wr = sb(st, "wr", [P, KT, 512])
    wh = sb(st, "woh", [P, KT, 512], F32R)
    wl = sb(st, "wol", [P, KT, 512], F32R)
    bc = sb(st, "bc", [P, 3, D])
    sq = sb(st, "sq2", [P, D])
    rs = sb(st, "rs2", [P, 2 * TT])
    hf = sb(st, "hf2", [P, 2, 512])
    cb = sb(st, "cbx", [P, 2, 4, P])
    (s_m, s_w, s_x, s_mh, s_ml, s_wh, s_wl, s_cb, s_bm, s_bc, s_mm, s_mx, s_ch, s_ssq, s_v, s_std, s_t, s_hf, s_hh,
     s_hl) = (sem(st, n) for n in (
         "m_loaded", "wo_loaded", "x_loaded", "m_hi_made", "m_lo_made", "wo_hi", "wo_lo", "column_spread",
         "broadcast_product", "broadcast_ready", "mix_product", "mix_copied", "dve_chain_f", "row_ssq", "row_ms",
         "row_std", "h2_transposed", "h2_copied", "h2_hi", "h2_lo"))
    with nc.Block() as block:
        @block.sync
        def _(sp):
            sp.dma_start(mr[:, :, :], m_dram.rearrange("k p t -> p k t")).then_inc(s_m, 16)
            sp.dma_start(wr[:, :, :], g["wo_in"][0]).then_inc(s_w, 16)
            sp.dma_start(x2[:, :, :], g["x"].rearrange("o (t p) d -> p (o t) d", p=P)).then_inc(s_x, 16)
            sp.wait_ge(s_wl, 1)
            sp.wait_ge(s_wh, 1)
            sp.dma_start(wr[:, :, :], g["wo_in"][1]).then_inc(s_w, 16)
            sp.wait_ge(s_w, 32)

        @block.scalar
        def _(act):
            act.wait_ge(s_m, 16)
            act.activation(mh[:, :, :], mr[:, :, :], ACT.Copy).then_inc(s_mh, 1)
            for n in range(2):
                act.wait_ge(s_w, 16 * n + 16)
                if n:
                    act.wait_ge(s_mm, TT)
                act.activation(wh[:, :, :], wr[:, :, :], ACT.Copy).then_inc(s_wh, 1)
                if n == 0:
                    for i in range(8):
                        act.wait_ge(s_bm, i + 1)
                        dst = bc[:, i // 2, :] if i < 6 else gt2b[:, :]
                        act.activation(dst[:, 512 * (i % 2):512 * (i % 2) + 512], bank[6 + i % 2][:, :], ACT.Copy).then_inc(s_bc, 1)
                for t in range(TT):
                    act.wait_ge(s_mm, TT * n + t + 1)
                    act.activation(h2[:, t, 512 * n:512 * n + 512], bank[t][:, :], ACT.Copy).then_inc(s_mx, 1)
            act.wait_ge(s_mx, 2 * TT)
            for t in range(TT):
                if t:
                    act.wait_ge(s_ssq, t)
                act.activation(sq[:, :], h2[:, t, :], ACT.Square, accum_out=rs[:, t:t + 1]).then_inc(s_ssq, 1)
            act.wait_ge(s_v, 1)
            act.activation(rs[:, 0:TT], rs[:, 0:TT], ACT.Sqrt).then_inc(s_std, 1)
            act.wait_ge(s_v, 2)
            for t in range(TT):
                act.wait_ge(s_ssq, TT + t)
                act.activation(sq[:, :], x2[:, t, :], ACT.Square, accum_out=rs[:, TT + t:TT + t + 1]).then_inc(s_ssq, 1)
            act.wait_ge(s_v, 3)
            act.activation(rs[:, TT:], rs[:, TT:], ACT.Sqrt).then_inc(s_std, 1)
            for k in range(KT):
                act.wait_ge(s_t, k + 1)
                if k >= 2:
                    act.wait_ge(s_hl, k - 1)
                act.activation(hf[:, k % 2, :], bank[k % 2][:, :], ACT.Copy).then_inc(s_hf, 1)
                act.wait_ge(s_hf, k + 1)
                act.activation(h2h[:, k, :], hf[:, k % 2, :], ACT.Copy).then_inc(s_hh, 1)

        @block.vector
        def _(dve):
            ch = Chain(dve, s_ch, None)
            for i in range(8):
                v, n = i // 2, i % 2
                if i >= 2:
                    dve.wait_ge(s_bm, i - 1)
                dve.tensor_copy(cb[:, i % 2, :, :], colv[:, v, 4 * n:4 * n + 4].unsqueeze(2).broadcast_to((P, 4, P))).then_inc(s_cb, 1)
            dve.wait_ge(s_mh, 1)
            dve.tensor_tensor(ml[:, :, :], mr[:, :, :], mh[:, :, :].bitcast(FP32), ALU.subtract).then_inc(s_ml, 1)
            for n in range(2):
                dve.wait_ge(s_wh, n + 1)
                dve.tensor_tensor(wl[:, :, :], wr[:, :, :], wh[:, :, :].bitcast(FP32), ALU.subtract).then_inc(s_wl, 1)
            dve.wait_ge(s_ssq, TT)
            dve.tensor_scalar(rs[:, 0:TT], rs[:, 0:TT], 1.0 / D, RMS_EPS, ALU.mult, ALU.add).then_inc(s_v, 1)
            dve.wait_ge(s_std, 1)
            ch(dve.reciprocal(rs[:, 0:TT], rs[:, 0:TT]))
            dve.wait_ge(s_x, 16)
            dve.wait_ge(s_bc, 8)
            for t in range(TT):
                ch(dve.scalar_tensor_tensor(h2[:, t, :], h2[:, t, :], rs[:, t:t + 1], bc[:, 0, :], ALU.mult, ALU.mult))
                ch(dve.tensor_tensor(x2[:, t, :], x2[:, t, :], h2[:, t, :], ALU.add))
            dve.sem_inc(s_v, 1)
            dve.wait_ge(s_ssq, 2 * TT)
            dve.tensor_scalar(rs[:, TT:], rs[:, TT:], 1.0 / D, RMS_EPS, ALU.mult, ALU.add).then_inc(s_v, 1)
            dve.wait_ge(s_std, 2)
            ch(dve.reciprocal(rs[:, TT:], rs[:, TT:]))
            for t in range(TT):
                ch(dve.scalar_tensor_tensor(h2[:, t, :], x2[:, t, :], rs[:, TT + t:TT + t + 1], bc[:, 1, :], ALU.mult, ALU.mult))
                ch(dve.tensor_tensor(h2[:, t, :], h2[:, t, :], bc[:, 2, :], ALU.add))
            dve.sem_inc(s_v, 1)
            for k in range(KT):
                dve.wait_ge(s_hh, k + 1)
                dve.tensor_tensor(h2l[:, k, :], hf[:, k % 2, :], h2h[:, k, :].bitcast(FP32), ALU.subtract).then_inc(s_hl, 1)

        @block.tensor
        def _(pe):
            for i in range(8):
                pe.wait_ge(s_cb, i + 1)
                if i >= 2:
                    pe.wait_ge(s_bc, i - 1)
                for q in range(4):
                    mm = pe.matmul(bank[6 + i % 2][:, q * P:q * P + P], cb[:, i % 2, q, :], ident[:, :], start=True, stop=True)
                mm.then_inc(s_bm, 1)
            pe.wait_ge(s_ml, 1)
            for n in range(2):
                pe.wait_ge(s_wl, n + 1)
                for t in range(TT):
                    if n:
                        pe.wait_ge(s_mx, t + 1)
                    for k in range(KT):
                        mm = split_mm(pe, bank[t][:, :], mh[:, k, t * P:t * P + P], ml[:, k, t * P:t * P + P],
                                      wh[:, k, :], wl[:, k, :], k == 0, k == KT - 1)
                    mm.then_inc(s_mm, 1)
            pe.wait_ge(s_mx, 2 * TT)
            pe.wait_ge(s_v, 4)
            for k in range(KT):
                if k >= 2:
                    pe.wait_ge(s_hf, k - 1)
                for t in range(TT):
                    mm = pe.transpose(bank[k % 2][:, t * P:t * P + P], h2[:, t, k * P:k * P + P], ident[:, :])
                mm.then_inc(s_t, 1)


def queries(nc, st, sb, sem, g):
    bank, qt_, h2h, h2l = (g[k] for k in ("bank", "qt_", "h2h", "h2l"))
    wr = sb(st, "wqr", [P, 2, KT, P])
    wh = sb(st, "wqh", [P, 2, KT, P], F32R)
    wl = sb(st, "wql", [P, 2, KT, P], F32R)
    s_w = [sem(st, "wq0_loaded"), sem(st, "wq1_loaded")]
    s_hi, s_lo, s_mm, s_qc = (sem(st, n) for n in ("wq_hi", "wq_lo", "q_product2", "q_copied"))
    gp, ga_, gd = (sem(st, "gate_q_" + k) for k in ("pe", "act", "dve"))
    N2 = HEADS
    with nc.Block() as block:
        @block.sync
        def _(sp):
            with sp.Fori(0, N2) as i:
                for b in range(2):
                    sp.wait_ge(s_lo, 2 * i)
                    sp.wait_ge(s_hi, 2 * i)
                    sp.dma_start(wr[:, b, :, :], g["wq_in"][bass.ds(2 * i + b, 1), :, :].rearrange(
                        "o p (k n) -> (o p) k n", k=KT)).then_inc(s_w[b], 16)

        @block.scalar
        def _(act):
            with act.Fori(0, N2) as i:
                for b in range(2):
                    hold(act, ga_, s_w[b], 16 * i + 16)
                    hold(act, ga_, s_mm, 2 * i)
                    act.activation(wh[:, b, :, :], wr[:, b, :, :], ACT.Copy).then_inc(s_hi, 1)
                for b in range(2):
                    hold(act, ga_, s_mm, 2 * i + (b + 1))
                    act.activation(qt_[:, bass.ds(2 * i + b, 1), :].rearrange("p o t -> p (o t)"), bank[b][:, :],
                                   ACT.Copy).then_inc(s_qc, 1)

        @block.vector
        def _(dve):
            with dve.Fori(0, N2) as i:
                for b in range(2):
                    hold(dve, gd, s_hi, 2 * i + (b + 1))
                    dve.tensor_tensor(wl[:, b, :, :], wr[:, b, :, :], wh[:, b, :, :].bitcast(FP32), ALU.subtract).then_inc(s_lo, 1)

        @block.tensor
        def _(pe):
            with pe.Fori(0, N2) as i:
                for b in range(2):
                    hold(pe, gp, s_lo, 2 * i + (b + 1))
                    hold(pe, gp, s_qc, 2 * i)
                    for k in range(KT):
                        mm = split_mm(pe, bank[b][:, :], wh[:, b, k, :], wl[:, b, k, :], h2h[:, k, :], h2l[:, k, :],
                                      k == 0, k == KT - 1)
                    mm.then_inc(s_mm, 1)


def routing(nc, st, sb, sem, g):
    bank, qt_, idx, pg = (g[k] for k in ("bank", "qt_", "idx", "pg"))
    HP = 2 * HEADS
    kt = sb(st, "keys_sb", [P, HP, NKEYS])
    sc = sb(st, "sc_", [P, HP, NKEYS])
    sc2 = sb(st, "sc2", [P, NKEYS])
    sv = sb(st, "sv", [P, HEADS, 2, TOPK])
    si = sb(st, "si", [P, HEADS, 2, TOPK], U32)
    sif = sb(st, "sif", [P, HEADS, 2, TOPK])
    cand = sb(st, "cand", [P, HEADS, TOPK, TOPK])
    cand2 = sb(st, "cand2", [P, TOPK * TOPK])
    cs = sb(st, "cs", [P, HEADS, TOPK])
    ci = sb(st, "ci", [P, HEADS, TOPK], U32)
    cj = sb(st, "cj", [P, 2, SLOTS], U32)
    cjf = sb(st, "cjf", [P, 2, SLOTS])
    iot = sb(st, "iot", [P, TOPK])
    oh = sb(st, "oh", [P, SLOTS, TOPK])
    kf = sb(st, "kf2", [P, 2, SLOTS])
    sm = sb(st, "sm", [P, HEADS])
    s_k, s_c, s_s, s_sc, s_ch, s_e, s_x, s_top = (sem(st, n) for n in (
        "keys_loaded", "iota_made", "scores", "scores_copied", "dve_chain_g", "gates_exp", "gates_shifted", "halves_topped"))
    NEG = -3.0e38
    with nc.Block() as block:
        @block.sync
        def _(sp):
            sp.dma_start(kt[:, :, :], g["keys_in"]).then_inc(s_k, 16)

        @block.gpsimd
        def _(pool):
            pool.iota(iot[:, :], pattern=[[1, TOPK]], base=0, channel_multiplier=0,
                      allow_small_or_imprecise_dtypes=True).then_inc(s_c, 1)
            pool.wait_ge(s_c, 1)
            pool.memset(idx[:, TT * SLOTS:], 0).then_inc(s_c, 1)

        @block.tensor
        def _(pe):
            pe.wait_ge(s_k, 16)
            for t in range(TT):
                for b in range(4):
                    if t:
                        pe.wait_ge(s_sc, 4 * (t - 1) + b + 1)
                    for i in range(4):
                        hp = 4 * b + i
                        mm = pe.matmul(bank[b][:, i * P:i * P + P], qt_[:, hp, t * P:t * P + P], kt[:, hp, :],
                                       start=True, stop=True)
                    mm.then_inc(s_s, 1)

        @block.scalar
        def _(act):
            for t in range(TT):
                if t:
                    act.wait_ge(s_top, t)
                for b in range(4):
                    act.wait_ge(s_s, 4 * t + b + 1)
                    act.activation(sc[:, 4 * b:4 * b + 4, :].rearrange("p a k -> p (a k)"), bank[b][:, :], ACT.Copy).then_inc(s_sc, 1)
                act.wait_ge(s_x, t + 1)
                act.activation(pg[:, t * SLOTS:(t + 1) * SLOTS], cs[:, :, :].rearrange("p h k -> p (h k)"), ACT.Exp).then_inc(s_e, 1)

        @block.vector
        def _(dve):
            ch = Chain(dve, s_ch, None)
            dve.wait_ge(s_c, 2)

            def top16(vals, scratch, v, i):
                ch(dve.max(v[:, 0:8], vals))
                ch(dve.max_index(i[:, 0:8], v[:, 0:8], vals))
                ch(dve.match_replace(scratch, v[:, 0:8], vals, NEG))
                ch(dve.max(v[:, 8:16], scratch))
                ch(dve.max_index(i[:, 8:16], v[:, 8:16], scratch))

            for t in range(TT):
                dve.wait_ge(s_sc, 4 * t + 4)
                for h in range(HEADS):
                    for p in range(2):
                        top16(sc[:, 2 * h + p, :], sc2[:, :], sv[:, h, p, :], si[:, h, p, :])
                dve.sem_inc(s_top, 1)
                ch(dve.tensor_tensor(cand[:, :, :, :], sv[:, :, 0, :].unsqueeze(3).broadcast_to((P, HEADS, TOPK, TOPK)),
                                     sv[:, :, 1, :].unsqueeze(2).broadcast_to((P, HEADS, TOPK, TOPK)), ALU.add))
                if t:
                    dve.wait_ge(s_e, t)
                for h in range(HEADS):
                    top16(cand[:, h, :, :].rearrange("p a b -> p (a b)"), cand2[:, :], cs[:, h, :], ci[:, h, :])
                cif = ci[:, :, :].rearrange("p h k -> p (h k)")
                ch(dve.tensor_scalar(cj[:, 0, :], cif, 4, None, ALU.logical_shift_right))
                ch(dve.tensor_scalar(cj[:, 1, :], cif, 15, None, ALU.bitwise_and))
                ch(dve.tensor_copy(cjf[:, :, :], cj[:, :, :]))
                ch(dve.tensor_copy(sif[:, :, :, :], si[:, :, :, :]))
                for p in range(2):
                    ch(dve.tensor_tensor(oh[:, :, :], cjf[:, p, :].unsqueeze(2).broadcast_to((P, SLOTS, TOPK)),
                                         iot[:, :].unsqueeze(1).broadcast_to((P, SLOTS, TOPK)), ALU.is_equal))
                    o4 = oh[:, :, :].rearrange("p (h k) i -> p h k i", h=HEADS)
                    ch(dve.tensor_tensor(o4, o4, sif[:, :, p, :].unsqueeze(2).broadcast_to((P, HEADS, TOPK, TOPK)), ALU.mult))
                    ch(dve.tensor_reduce(kf[:, p, :], oh[:, :, :], AX.X, ALU.add))
                ch(dve.scalar_tensor_tensor(kf[:, 0, :], kf[:, 0, :], float(NKEYS), kf[:, 1, :], ALU.mult, ALU.add))
                ch(dve.tensor_copy(idx[:, t * SLOTS:(t + 1) * SLOTS], kf[:, 0, :]))
                ch(dve.tensor_copy(sm[:, :], cs[:, :, 0]))
                ch(dve.tensor_tensor(cs[:, :, :], cs[:, :, :], sm[:, :].unsqueeze(2).broadcast_to((P, HEADS, TOPK)), ALU.subtract))
                dve.sem_inc(s_x, 1)
                dve.wait_ge(s_e, t + 1)
                pgt = pg[:, t * SLOTS:(t + 1) * SLOTS].rearrange("p (h k) -> p h k", h=HEADS)
                ch(dve.tensor_reduce(sm[:, :], pgt, AX.X, ALU.add))
                ch(dve.reciprocal(sm[:, :], sm[:, :]))
                ch(dve.tensor_tensor(pgt, pgt, sm[:, :].unsqueeze(2).broadcast_to((P, HEADS, TOPK)), ALU.mult))


def experts(nc, st, sb, sem, g):
    x2, h2, gt2b, idx, pg = (g[k] for k in ("x2", "h2", "gt2b", "idx", "pg"))
    ur = sb(st, "ur", [P, TOPK, D])
    vr = sb(st, "vr", [P, TOPK, D])
    ic = sb(st, "ic", [P, 2, TOPK], U32)
    gc = sb(st, "gc_", [P, TOPK])
    hc = sb(st, "hc", [P, D])
    junk = sb(st, "junk", [P, 2, D])
    acc = sb(st, "acc", [P, 2, D])
    dt = sb(st, "dt_", [P, TOPK])
    ge = sb(st, "ge", [P, TOPK])
    rs = sb(st, "rs3", [P, 1])
    sq = sb(st, "sq3", [P, D])
    su = [sem(st, f"u_row{k}") for k in range(TOPK)]
    sv = [sem(st, f"v_row{k}") for k in range(TOPK)]
    s_ic, s_ch, s_ud, s_ge, s_gc, s_vd, s_ssq, s_v, s_std, s_acc, s_out = (sem(st, n) for n in (
        "numbers_set", "dve_chain_h", "u_used", "gelu_done", "coefficients", "v_used", "peer_ssq", "peer_ms",
        "peer_std", "tile_summed", "out_stored"))
    gp, ga_, gd, gq = (sem(st, "gate_h_" + k) for k in ("pe", "act", "dve", "pool"))
    outv = g["out"].rearrange("o (t p) d -> (o t) p d", p=P)
    NP2 = HEADS // 2
    with nc.Block() as block:
        @block.gpsimd
        def _(pool):
            with pool.Fori(0, TT * NP2) as i:
                for b in range(2):
                    hold(pool, gq, s_ic, 2 * i + (b + 1))
                    for ring, s, src, used in ((ur, su, g["peer_u"], s_ud), (vr, sv, g["peer_v"], s_vd)):
                        for k in range(TOPK):
                            hold(pool, gq, used, 2 * TOPK * i + (TOPK * b + k + 1))
                            pool.indirect_dma_start(ring[:, k, :], None, src, bass.IndirectOffsetOnAxis(
                                ap=ic[:, b, k:k + 1], axis=0)).then_inc(s[k], 16)

        @block.scalar
        def _(act):
            with act.Fori(0, TT) as t:
                with act.Fori(0, NP2) as h:
                    for b in range(2):
                        hold(act, ga_, s_ud, t * (HEADS * TOPK) + h * (2 * TOPK) + (TOPK * (b + 2)))
                        act.activation(ge[:, :], dt[:, :], ACT.Gelu).then_inc(s_ge, 1)
                hold(act, ga_, s_acc, 2 * t + 1)
                act.activation(sq[:, :], acc[:, 0, :], ACT.Square, accum_out=rs[:, :]).then_inc(s_ssq, 1)
                hold(act, ga_, s_v, t + 1)
                act.activation(rs[:, :], rs[:, :], ACT.Sqrt).then_inc(s_std, 1)

        @block.sync
        def _(sp):
            with sp.Fori(0, TT) as t:
                sp.wait_ge(s_acc, 2 * t + 2)
                sp.dma_start(outv[bass.ds(t, 1), :, :].rearrange("o p d -> (o p) d"), acc[:, 0, :]).then_inc(s_out, 16)
            sp.wait_ge(s_out, 16 * TT)

        @block.vector
        def _(dve):
            ch = Chain(dve, s_ch, gd)
            for b in range(2):
                dve.tensor_copy(ic[:, b, :], idx[:, TOPK * b:TOPK * b + TOPK]).then_inc(s_ic, 1)
            dve.sem_inc(s_ud, TOPK)
            dve.sem_inc(s_vd, TOPK)
            with dve.Fori(0, TT) as t:
                ch.loop(t, 7)
                hold(dve, gd, s_out, 16 * t)
                ch(dve.tensor_copy(hc[:, :], h2[:, bass.ds(t, 1), :].rearrange("p o d -> p (o d)")))
                ch(dve.memset(acc[:, :, :], 0.0))
                with dve.Fori(0, NP2) as h:
                    for b in range(2):
                        base = t * SLOTS + h * (2 * TOPK)
                        head = t * HEADS + h * 2
                        for k in range(TOPK):
                            hold(dve, gd, su[k], head * 16 + 16 * (b + 1))
                            hold(dve, gd, s_ud, base + (TOPK * b + k + TOPK - 1))
                            dve.scalar_tensor_tensor(junk[:, k % 2, :], ur[:, k, :], 1.0, hc[:, :], ALU.mult, ALU.mult,
                                                     accum_out=dt[:, k:k + 1]).then_inc(s_ud, 1)
                        hold(dve, gd, s_ge, head + (b + 1))
                        dve.tensor_tensor(gc[:, :], ge[:, :], pg[:, bass.ds(base + TOPK * b, TOPK)], ALU.mult).then_inc(s_gc, 1)
                        hold(dve, gd, s_gc, head + (b + 1))
                        for k in range(TOPK):
                            hold(dve, gd, sv[k], head * 16 + 16 * (b + 1))
                            hold(dve, gd, s_vd, base + (TOPK * b + k + TOPK - 1))
                            dve.scalar_tensor_tensor(acc[:, k % 2, :], vr[:, k, :], gc[:, k:k + 1], acc[:, k % 2, :],
                                                     ALU.mult, ALU.add).then_inc(s_vd, 1)
                        dve.tensor_copy(ic[:, b, :], idx[:, bass.ds(base + TOPK * (b + 2), TOPK)]).then_inc(s_ic, 1)
                hold(dve, gd, s_vd, (t + 1) * SLOTS + TOPK)
                ch(dve.tensor_tensor(acc[:, 0, :], acc[:, 0, :], acc[:, 1, :], ALU.add))
                dve.sem_inc(s_acc, 1)
                hold(dve, gd, s_ssq, t + 1)
                ch(dve.tensor_scalar(rs[:, :], rs[:, :], 1.0 / D, RMS_EPS, ALU.mult, ALU.add))
                dve.sem_inc(s_v, 1)
                hold(dve, gd, s_std, t + 1)
                ch(dve.reciprocal(rs[:, :], rs[:, :]))
                ch(dve.scalar_tensor_tensor(acc[:, 0, :], acc[:, 0, :], rs[:, 0:1], gt2b[:, :], ALU.mult, ALU.mult))
                ch(dve.tensor_tensor(acc[:, 0, :], acc[:, 0, :], x2[:, bass.ds(t, 1), :].rearrange("p o d -> p (o d)"), ALU.add))
                dve.sem_inc(s_acc, 1)
            ch.end(TT)



def _tiles(w, cols):
    k = w.shape[0] // P
    return [np.ascontiguousarray(w[:, c:c + P].reshape(k, P, P).transpose(1, 0, 2).reshape(P, k * P)) for c in cols]


def _cols(v):
    return v.reshape(-1, P).T


def _pack(a):
    i = {k: np.asarray(v) for k, v in a.items()}
    w_in, w_mod = i["w_in"][0], i["w_mod"][0]
    shift = 3 * D + 3 * P
    gvec = np.concatenate([_cols(i["c"][0]), _cols(i["c_ctx"]), _cols(i["b_mod"][0]), _cols(i["g_pre_mix"][0]),
                           _cols(i["g_post_mix"][0]), _cols(i["g_pre_ffn"][0]), _cols(i["g_post_ffn"][0]),
                           _cols(i["mu_shift"][0][3 * D:]), _cols(i["b_gate"][0]), _cols(i["pool_scale"][0])], axis=1)
    mu = i["mu_shift"][0][:3 * D].reshape(3, NPAIR, P)
    rows = [mu[0], mu[1], mu[2]] + [i[n][0][d].reshape(NPAIR, P) for n in ("w0", "a0") for d in range(2)] + [
        i[n][0].reshape(NPAIR, P) for n in ("k_k", "k_a", "r_k", "ln_x_w", "ln_x_b")]
    lora = np.stack([i["w2"][0].reshape(P, NPAIR, P), i["a2"][0].reshape(P, NPAIR, P), i["g2"][0].reshape(P, NPAIR, P)])
    wa, wb, wo = i["w_a_out"][0], i["w_b_out"][0], i["w_o"][0]
    half = np.arange(SEQ)
    inv = []
    for w in WINDOWS:
        r, c = half // GRID_W, half % GRID_W
        n = (np.minimum(r + w // 2, ROWS) - np.maximum(r - w // 2, 0)) * (
            np.minimum(c + w // 2, GRID_W) - np.maximum(c - w // 2, 0))
        inv.append(1.0 / n)
    return {
        "x": i["x"], "ctx_in": i["ctx"], "gvec_in": gvec,
        "wmod": w_mod.reshape(KT, P, MODG, 512).transpose(2, 1, 0, 3).reshape(MODG, P, KT * 512),
        "wlora_in": np.concatenate(_tiles(w_in, [3 * D + q * P for q in range(3)]), axis=1),
        "wpair_in": np.stack([np.concatenate(_tiles(w_in, [q * D + j * P for q in range(3)]), axis=1) for j in range(NPAIR)]),
        "pvec_in": np.stack(rows).transpose(1, 2, 0),
        "lora_in": lora.transpose(2, 1, 0, 3).reshape(NPAIR, P, 3 * P),
        "wpu_in": np.concatenate(_tiles(w_in, [shift + q * P for q in range(4)]), axis=1),
        "wpool_in": i["w_pool"][0].transpose(1, 0, 2),
        "invcnt_in": np.array(inv, dtype=np.float32),
        "wmerge_in": np.stack([np.concatenate(
            _tiles(w_in, [shift + 512 + j * P, shift + 512 + D + j * P]) + _tiles(wa, [j * P]) + _tiles(wb, [j * P]),
            axis=1) for j in range(NPAIR)]),
        "wo_in": wo.reshape(KT, P, 2, 512).transpose(2, 1, 0, 3),
        "wq_in": np.stack(_tiles(i["peer_wq"][0], [q * P for q in range(16)])),
        "keys_in": i["peer_keys"][0].reshape(16, P, P).transpose(2, 0, 1),
        "peer_u": i["peer_u"][0], "peer_v": i["peer_v"][0],
    }


def kernel(**inputs):
    import concourse.bacc as bacc
    from concourse.bass_utils import run_bass_kernel_spmd
    nc = bacc.Bacc("TRN2", target_bir_lowering=False, num_devices=1)
    arrays, args = {}, {}
    for name, a in _pack(inputs).items():
        a = np.ascontiguousarray(a)
        arrays["in_" + name] = a
        args[name] = nc.dram_tensor("in_" + name, a.shape, mybir.dt.from_np(a.dtype), kind="ExternalInput").ap()
    args["out"] = nc.dram_tensor("out_0", (1, SEQ, D), FP32, kind="ExternalOutput").ap()
    build(nc, **args)
    r = run_bass_kernel_spmd(nc, [arrays], core_ids=[0])
    return r.results[0]["out_0"]
```

```python
import numpy as np
import concourse.bass as bass
from concourse import mybir
from contextlib import ExitStack

FP32 = mybir.dt.float32
F32R = mybir.dt.float32r
U32 = mybir.dt.uint32
ALU = mybir.AluOpType
ACT = mybir.ActivationFunctionType
AX = mybir.AxisListType

P = 128
D = 1024
KT = D // P
SEQ, CTX = 512, 256
T = CTX + SEQ
TT = SEQ // P
XT = T // P
HEAD = 64
NPAIR = D // P
NDIR = 2
CHUNK = 64
NC = T // CHUNK
CC = CTX // CHUNK
UNITS = NDIR * NC * 2
HB = 32
MODG = 12
GRID_W = 64
ROWS = SEQ // GRID_W
WINDOWS = (2, 4, 8, 16)
NEXP = 16384
HEADS, TOPK, NKEYS = 8, 16, 128
SLOTS = HEADS * TOPK
RMS_EPS, GN_EPS, L2_EPS2 = 1e-6, 64e-5, 1e-24
DECAY_C = float(np.exp(-0.5))

GV_C, GV_CCTX, GV_BMOD = 0, 8, 16
GV_GPM, GV_GPOM, GV_GPF, GV_GPOF = 64, 72, 80, 88
GV_MUL, GV_BG, GV_PS, GV_N = 96, 99, 115, 119
PV_MU, PV_W0, PV_KK, PV_KA, PV_RK, PV_LNW, PV_LNB, PV_N = 0, 3, 7, 8, 9, 10, 11, 12
RC_RA = 0
RC_KB = RC_RA + NDIR * NC * 2 * CHUNK
RC_V = RC_KB + NDIR * NC * 2 * CHUNK
RC_EC = RC_V + NDIR * T
RC_BO = RC_EC + NDIR * NC
RC_GA = RC_BO + SEQ
RC_N = RC_GA + SEQ


class Chain:

    def __init__(self, eng, sem):
        self.eng, self.sem, self.n = eng, sem, 0

    def loop(self):
        self.eng.sem_clear(self.sem)
        self.n = 0

    def __call__(self, ins):
        ins.then_inc(self.sem, 1)
        self.n += 1
        self.eng.wait_ge(self.sem, self.n)


def hold(eng, gate, sem, value):
    eng.wait_ge(sem, value)
    eng.sem_inc(gate, 1)


def split_mm(tensor, out, w_hi, w_lo, x_hi, x_lo, first, last):
    tensor.matmul(out, w_hi, x_hi, start=first, stop=False)
    tensor.matmul(out, w_hi, x_lo, start=False, stop=False)
    return tensor.matmul(out, w_lo, x_hi, start=False, stop=last)


def build(nc, x, ctx_in, gvec_in, wmod, wlora_in, wpair_in, pvec_in, lora_in, wpu_in, wpool_in,
          invcnt_in, wmerge_in, wo_in, wq_in, keys_in, peer_u, peer_v, out):
    record = nc.dram_tensor("pair_record", (NPAIR, P, RC_N), FP32, kind="Internal").ap()
    tri_dram = nc.dram_tensor("tri_dram", (UNITS, CHUNK, CHUNK), FP32, kind="Internal").ap()
    inv_dram = nc.dram_tensor("inv_dram", (2, UNITS, HB, HB), FP32, kind="Internal").ap()
    m_dram = nc.dram_tensor("m_dram", (NPAIR, P, SEQ), FP32, kind="Internal").ap()
    scores_dram = nc.dram_tensor("scores_dram", (TT - 1, P, 2 * HEADS * NKEYS), FP32, kind="Internal").ap()
    invt_dram = nc.dram_tensor("invt_dram", (UNITS, HB, HB), FP32, kind="Internal").ap()

    stage_sems = {}

    def release(stack):
        nc.clear_and_free_semaphores(stage_sems.pop(stack))
        nc.all_engine_barrier()

    top = ExitStack()
    with top:
        def sb(stack, name, shape, dt=FP32):
            return stack.enter_context(nc.sbuf_tensor(name, shape, dt))

        def sem(stack, name):
            if stack not in stage_sems:
                stage_sems[stack] = []
                stack.callback(release, stack)
            stage_sems[stack].append(nc.alloc_semaphore(name=name))
            return stage_sems[stack][-1]

        bank = [top.enter_context(nc.psum_tensor(f"bank{i}", [P, 512], FP32)) for i in range(8)]
        ident = sb(top, "ident", [P, P])
        gv = sb(top, "gv", [P, GV_N])
        mod = sb(top, "mod", [P, 48, 2])
        colv = sb(top, "colv", [P, 4, KT])
        blk = sb(top, "blk", [P, P])
        modulate(nc, top, sb, sem, locals())
        with ExitStack() as mid:
            ht_hi = sb(mid, "ht_hi", [P, KT, T], F32R)
            ht_lo = sb(mid, "ht_lo", [P, KT, T], F32R)
            normalise(nc, sb, sem, locals())
            project(nc, sb, sem, locals())
            o_all = sb(mid, "o_all", [P, NPAIR, SEQ])
            scan(nc, sb, sem, locals())
            merge(nc, sb, sem, locals())
        tail(nc, sb, sem, locals())


def modulate(nc, top, sb, sem, g):
    gv, mod, colv, ident, blk, bank = (g[k] for k in ("gv", "mod", "colv", "ident", "blk", "bank"))
    with ExitStack() as st:
        wm = sb(st, "wm", [P, 2, KT, 512])
        modrow = sb(st, "modrow", [2, MODG * 512])
        sc = sb(st, "sc", [P, KT, 2])
        th = sb(st, "th", [P, 16])
        s_gv, s_w0, s_w1 = (sem(st, n) for n in ("gvec_loaded", "wmod0_loaded", "wmod1_loaded"))
        s_w = [s_w0, s_w1]
        s_id, s_th, s_sc, s_mm, s_ev, s_col, s_ch = (sem(st, n) for n in (
            "consts_made", "tanh_done", "silu_done", "mod_mm", "mod_copied", "mod_col", "dve_chain_a"))
        gate = {k: sem(st, "gate_a_" + k) for k in ("pe", "act")}
        with nc.Block() as block:
            @block.sync
            def _(sp):
                sp.dma_start(gv[:, :], g["gvec_in"]).then_inc(s_gv, 16)
                for b in range(2):
                    sp.dma_start(wm[:, b, :, :], g["wmod"][b].rearrange("p (k n) -> p k n", k=KT)).then_inc(s_w[b], 16)
                with sp.Fori(1, MODG // 2) as i:
                    for b in range(2):
                        sp.wait_ge(s_mm, 2 * i + (b - 1))
                        sp.dma_start(wm[:, b, :, :], g["wmod"][bass.ds(2 * i + b, 1), :, :].rearrange(
                            "o p (k n) -> (o p) k n", k=KT)).then_inc(s_w[b], 16)

            @block.gpsimd
            def _(pool):
                pool.memset(ident[:, :], 0.0).then_inc(s_id, 1)
                pool.wait_ge(s_id, 1)
                pool.memset(blk[:, :], 0.0).then_inc(s_id, 1)
                pool.wait_ge(s_id, 2)
                pool.affine_select(out=ident[:, :], in_=ident[:, :], compare_op=ALU.not_equal, fill=1.0, base=0,
                                   pattern=[[-1, P]], channel_multiplier=1).then_inc(s_id, 1)
                for h in range(2):
                    pool.wait_ge(s_id, 3 + h)
                    pool.memset(blk[64 * h:64 * h + 64, 64 * h:64 * h + 64], 1.0).then_inc(s_id, 1)

            @block.scalar
            def _(act):
                act.wait_ge(s_gv, 16)
                act.activation(th[:, :], gv[:, GV_C:GV_C + 16], ACT.Tanh, scale=0.5).then_inc(s_th, 1)
                with act.Fori(0, MODG // 2) as i:
                    for b in range(2):
                        hold(act, gate["act"], s_mm, 2 * i + (b + 1))
                        act.activation(modrow[:, bass.ds((2 * i + b) * 512, 512)], bank[b][0:2, :],
                                       ACT.Copy).then_inc(s_ev, 1)

            @block.vector
            def _(dve):
                ch = Chain(dve, s_ch)
                dve.sem_inc(s_ev, 1)
                dve.wait_ge(s_th, 1)
                ch(dve.scalar_tensor_tensor(th[:, :], th[:, :], 1.0, gv[:, GV_C:GV_C + 16], ALU.add, ALU.mult))
                dve.tensor_scalar(sc[:, :, :].rearrange("p k c -> p c k"), th[:, :].rearrange("p (c k) -> p c k", c=2),
                                  0.5, None, ALU.mult).then_inc(s_sc, 1)
                dve.wait_ge(s_col, 1)
                bm = gv[:, GV_BMOD:GV_BMOD + 48]
                for c in range(2):
                    ch(dve.tensor_tensor(mod[:, :, c], bank[2][:, 0:96].rearrange("p (m c) -> p m c", c=2)[:, :, c],
                                         bm, ALU.add))
                for c in range(2):
                    ch(dve.scalar_tensor_tensor(mod[:, 8:16, c], mod[:, 8:16, c], 1.0, gv[:, GV_GPM:GV_GPM + 8],
                                                ALU.add, ALU.mult))
                ch(dve.tensor_tensor(colv[:, 0, :], mod[:, 16:24, 0], gv[:, GV_GPOM:GV_GPOM + 8], ALU.mult))
                ch(dve.scalar_tensor_tensor(colv[:, 1, :], mod[:, 32:40, 0], 1.0, gv[:, GV_GPF:GV_GPF + 8],
                                            ALU.add, ALU.mult))
                ch(dve.tensor_copy(colv[:, 2, :], mod[:, 24:32, 0]))
                ch(dve.tensor_tensor(colv[:, 3, :], mod[:, 40:48, 0], gv[:, GV_GPOF:GV_GPOF + 8], ALU.mult))

            @block.tensor
            def _(pe):
                pe.wait_ge(s_sc, 1)
                pe.wait_ge(s_id, 5)
                with pe.Fori(0, MODG // 2) as i:
                    for b in range(2):
                        hold(pe, gate["pe"], s_w[b], 16 * i + 16)
                        hold(pe, gate["pe"], s_ev, 2 * i + 1)
                        for k in range(KT):
                            mm = pe.matmul(bank[b][0:2, :], sc[:, k, :], wm[:, b, k, :], start=k == 0, stop=k == KT - 1)
                        mm.then_inc(s_mm, 1)
                pe.wait_ge(s_ev, MODG + 1)
                for m in range(48):
                    mm = pe.matmul(bank[2][:, 2 * m:2 * m + 2], modrow[0:2, m * P:m * P + P], ident[0:2, 0:2],
                                   start=True, stop=True)
                mm.then_inc(s_col, 1)


def normalise(nc, sb, sem, g):
    mod, ident, bank, ht_hi, ht_lo = (g[k] for k in ("mod", "ident", "bank", "ht_hi", "ht_lo"))
    with ExitStack() as st:
        xt = sb(st, "xt", [P, XT, D])
        sq = sb(st, "sq", [P, D])
        rs = sb(st, "rs", [P, XT])
        hf = sb(st, "hf", [P, 2, 512])
        s_x, s_ssq, s_ms, s_std, s_rs, s_xn, s_t, s_hf, s_hi, s_lo = (sem(st, n) for n in (
            "tokens_loaded", "ssq_done", "ms_done", "std_done", "rstd_done", "tokens_scaled", "tokens_transposed",
            "modulated", "hi_done", "lo_done"))
        groups = [(k, a, n) for k in range(KT) for a, n in ((0, 2), (2, 4))]
        with nc.Block() as block:
            @block.sync
            def _(sp):
                sp.dma_start(xt[:, 0:2, :], g["ctx_in"].rearrange("o (t p) d -> p (o t) d", p=P)).then_inc(s_x, 16)
                sp.dma_start(xt[:, 2:6, :], g["x"].rearrange("o (t p) d -> p (o t) d", p=P)).then_inc(s_x, 16)
                sp.wait_ge(s_x, 32)

            @block.scalar
            def _(act):
                act.wait_ge(s_x, 32)
                for t in range(XT):
                    if t:
                        act.wait_ge(s_ssq, t)
                    act.activation(sq[:, :], xt[:, t, :], ACT.Square, accum_out=rs[:, t:t + 1]).then_inc(s_ssq, 1)
                act.wait_ge(s_ms, 1)
                act.activation(rs[:, :], rs[:, :], ACT.Sqrt).then_inc(s_std, 1)
                act.wait_ge(s_rs, 1)
                for t in range(XT):
                    act.activation(xt[:, t, :], xt[:, t, :], ACT.Copy, scale=rs[:, t:t + 1]).then_inc(s_xn, 1)
                for i, (k, a, n) in enumerate(groups):
                    act.wait_ge(s_hf, i + 1)
                    act.activation(ht_hi[:, k, a * P:(a + n) * P], hf[:, i % 2, 0:n * P], ACT.Copy).then_inc(s_hi, 1)

            @block.vector
            def _(dve):
                dve.wait_ge(s_ssq, XT)
                dve.tensor_scalar(rs[:, :], rs[:, :], 1.0 / D, RMS_EPS, ALU.mult, ALU.add).then_inc(s_ms, 1)
                dve.wait_ge(s_std, 1)
                dve.reciprocal(rs[:, :], rs[:, :]).then_inc(s_rs, 1)
                for i, (k, a, n) in enumerate(groups):
                    c = 1 if a == 0 else 0
                    dve.wait_ge(s_t, i + 1)
                    if i >= 2:
                        dve.wait_ge(s_hi, i - 1)
                        dve.wait_ge(s_lo, i - 1)
                    dve.tensor_scalar(hf[:, i % 2, 0:n * P], bank[i % 2][:, 0:n * P], mod[:, 8 + k, c:c + 1],
                                      mod[:, k, c:c + 1], ALU.mult, ALU.add).then_inc(s_hf, 1)
                    dve.wait_ge(s_hi, i + 1)
                    dve.tensor_tensor(ht_lo[:, k, a * P:(a + n) * P], hf[:, i % 2, 0:n * P],
                                      ht_hi[:, k, a * P:(a + n) * P].bitcast(FP32), ALU.subtract).then_inc(s_lo, 1)

            @block.tensor
            def _(pe):
                pe.wait_ge(s_xn, XT)
                for i, (k, a, n) in enumerate(groups):
                    if i >= 2:
                        pe.wait_ge(s_hf, i - 1)
                    for t in range(n):
                        tr = pe.transpose(bank[i % 2][:, t * P:t * P + P], xt[:, a + t, k * P:k * P + P], ident[:, :])
                    tr.then_inc(s_t, 1)


def project(nc, sb, sem, g):
    gv, blk, bank, ht_hi, ht_lo, record = (g[k] for k in ("gv", "blk", "bank", "ht_hi", "ht_lo", "record"))
    LORA_ORDER, PAIR_ORDER = (0, 1, 2), (1, 0, 2)
    with ExitStack() as st:
        wraw = sb(st, "wraw", [P, 3, KT, P])
        wh = sb(st, "wh", [P, 2, KT, P], F32R)
        wl = sb(st, "wl", [P, 2, KT, P], F32R)
        lw = sb(st, "lw", [P, 3, P])
        pva = sb(st, "pva", [P, NPAIR, PV_N])
        vva = sb(st, "vva", [P, NPAIR, 14])
        vv = sb(st, "vv", [P, 14])
        zp = sb(st, "zp", [P, 3, T + 4])
        zs = sb(st, "zs", [P, 3, T])
        ns = sb(st, "ns", [P, T])
        zr = sb(st, "zr", [P, 3, T])
        lin = sb(st, "lin", [P, 2, T])
        gin = sb(st, "gin", [P, SEQ])
        dl = sb(st, "dl", [P, NDIR, T])
        al = sb(st, "al", [P, NDIR, T])
        ex = sb(st, "ex", [P, NDIR, NC, CHUNK + 1])
        ei = sb(st, "ei", [P, NDIR, T])
        kk = sb(st, "kk", [P, T])
        rn = sb(st, "rn", [P, T])
        tmp = sb(st, "tmp", [P, T])
        kf = sb(st, "kf", [P, NDIR, T])
        cm = sb(st, "cm", [P, NC, CHUNK])
        rec = sb(st, "rec", [P, RC_N])
        ra = rec[:, RC_RA:RC_KB].rearrange("p (d c q s) -> p d c q s", d=NDIR, c=NC, q=2)
        kb = rec[:, RC_KB:RC_V].rearrange("p (d c q s) -> p d c q s", d=NDIR, c=NC, q=2)
        vd = rec[:, RC_V:RC_EC].rearrange("p (d t) -> p d t", d=NDIR)
        ecr = rec[:, RC_EC:RC_BO].rearrange("p (d c) -> p d c", d=NDIR)
        bo, ga = rec[:, RC_BO:RC_GA], rec[:, RC_GA:RC_N]
        (s_w, s_hi, s_lo, s_vec, s_z, s_zc, s_zs, s_sq, s_n2, s_mx, s_std, s_lw, s_lt, s_la, s_at, s_g, s_gc, s_ld,
         s_ex, s_rv, s_bk, s_bm, s_rec, s_st, s_c, s_ch, s_li, s_kfd, s_pv, s_lw0) = (sem(st, n) for n in (
             "weights_loaded", "weights_hi", "weights_lo", "vectors_made", "z_product", "z_copied", "z_shifted",
             "kk_squared", "kk_norm2", "kk_norm2_ready", "kk_norm", "decay_product", "decay_tanh", "rate_product",
             "rate_tanh", "gate_product", "gate_copied", "log_decay", "exp_done", "reversed", "bonus_operand",
             "bonus_product", "record_made", "record_stored", "cleared", "dve_chain_b", "lora_inputs", "kk_operand",
             "pair_vectors_loaded", "lora_weights_loaded"))
        gp, ga_, gd, gs = (sem(st, "gate_b_" + k) for k in ("pe", "act", "dve", "sp"))

        def col(v, n=1):
            return vv[:, v:v + n]

        HMU, OMU, HW, HKA, OKA, HRK, KK = 0, 3, 6, 10, 11, 12, 13

        with nc.Block() as block:
            @block.sync
            def _(sp):
                sp.dma_start(wraw[:, :, :, :], g["wlora_in"].rearrange("p (q k n) -> p q k n", q=3, k=KT)).then_inc(s_w, 16)
                sp.dma_start(pva[:, :, :], g["pvec_in"].rearrange("j p v -> p j v")).then_inc(s_pv, 16)
                sp.dma_start(lw[:, :, :], g["lora_in"][0].rearrange("p (q n) -> p q n", q=3)).then_inc(s_lw0, 16)
                sp.wait_ge(s_lo, 3)
                sp.wait_ge(s_hi, 3)
                sp.dma_start(wraw[:, :, :, :], g["wpair_in"][0].rearrange("p (q k n) -> p q k n", q=3, k=KT)).then_inc(s_w, 16)

                def pair(j, last):
                    if not last:
                        hold(sp, gs, s_lo, 3 * j + 6)
                        hold(sp, gs, s_hi, 3 * j + 6)
                        sp.dma_start(wraw[:, :, :, :], g["wpair_in"][bass.ds(j + 1, 1), :, :].rearrange(
                            "o p (q k n) -> (o p) q k n", q=3, k=KT)).then_inc(s_w, 16)
                        hold(sp, gs, s_g, j + 1)
                        sp.dma_start(lw[:, :, :], g["lora_in"][bass.ds(j + 1, 1), :, :].rearrange(
                            "o p (q n) -> (o p) q n", q=3)).then_inc(s_lw0, 16)
                    hold(sp, gs, s_rec, j + 1 + 1)
                    hold(sp, gs, s_gc, j + 1 + 1)
                    sp.dma_start(record[bass.ds(j, 1), :, :].rearrange("o p n -> (o p) n"), rec[:, :]).then_inc(s_st, 16)

                with sp.Fori(0, NPAIR - 1) as j:
                    pair(j, False)
                pair(NPAIR - 1, True)
                sp.wait_ge(s_st, 16 * NPAIR + 1)

            @block.gpsimd
            def _(pool):
                for n, ins in enumerate((lambda: pool.memset(zp[:, :, :], 0.0), lambda: pool.memset(ex[:, :, :, 0:1], 1.0),
                                         lambda: pool.memset(cm[:, :, :], 1.0), lambda: pool.memset(cm[:, :, 0:1], 0.0))):
                    ins().then_inc(s_c, 1)
                    pool.wait_ge(s_c, n + 1)

            def z_evac(act, q, n, wait, omu, lora=False):
                b = bank[0 + 2 * (q % 2)], bank[1 + 2 * (q % 2)]
                wait()
                act.activation(zp[:, q, 1:1 + CTX], b[0][:, 0:CTX], ACT.Copy).then_inc(s_zc, 1)
                act.activation(zp[:, q, CTX + 3:CTX + 3 + SEQ], b[1][:, :], ACT.Copy).then_inc(s_zc, 1)
                act.activation(zs[:, q, 0:CTX], b[0][:, 0:CTX], ACT.Copy, scale=omu).then_inc(s_zc, 1)
                act.activation(zs[:, q, CTX:T], b[1][:, :], ACT.Copy, scale=omu).then_inc(s_zc, 1)

            @block.scalar
            def _(act):
                act.wait_ge(s_w, 16)
                act.wait_ge(s_c, 4)
                for n, q in enumerate(LORA_ORDER):
                    if n >= 2:
                        act.wait_ge(s_z, n - 1)
                    act.activation(wh[:, n % 2, :, :], wraw[:, q, :, :], ACT.Copy).then_inc(s_hi, 1)
                act.wait_ge(s_vec, 1)
                for n, q in enumerate(LORA_ORDER):
                    z_evac(act, q, n, lambda: act.wait_ge(s_z, n + 1), col(OMU + q))
                act.wait_ge(s_zs, 3)
                act.activation(lin[:, 0, :], zs[:, 0, :], ACT.Tanh).then_inc(s_li, 1)
                act.activation(gin[:, :], zs[:, 2, CTX:T], ACT.Tanh, scale=0.5).then_inc(s_li, 1)
                act.wait_ge(s_li, 3)

                def high(n):
                    act.activation(wh[:, n % 2, :, :], wraw[:, PAIR_ORDER[n], :, :], ACT.Copy).then_inc(s_hi, 1)

                act.wait_ge(s_w, 32)
                act.wait_ge(s_z, 3)
                high(0)
                high(1)
                act.wait_ge(s_z, 4)
                high(2)

                def pair(j, last):
                    hold(act, ga_, s_vec, j + 2)
                    hold(act, ga_, s_rec, j + 1)
                    for n, q in enumerate(PAIR_ORDER):
                        z_evac(act, q, n, lambda: hold(act, ga_, s_z, 3 * j + (3 + n + 1)), col(OMU + q))
                        if n == 1:
                            hold(act, ga_, s_lw, j + 1)
                            for d in range(NDIR):
                                act.activation(dl[:, d, 0:CTX], bank[6 + d][:, 0:CTX], ACT.Tanh, bias=col(HW + d),
                                               scale=0.5).then_inc(s_lt, 1)
                                act.activation(dl[:, d, CTX:T], bank[4 + d][:, :], ACT.Tanh, bias=col(HW + d),
                                               scale=0.5).then_inc(s_lt, 1)
                    hold(act, ga_, s_kfd, j + 1)
                    act.activation(tmp[:, :], kk[:, :], ACT.Square).then_inc(s_sq, 1)
                    hold(act, ga_, s_la, j + 1)
                    for d in range(NDIR):
                        act.activation(al[:, d, 0:CTX], bank[6 + d][:, 0:CTX], ACT.Tanh, bias=col(HW + 2 + d),
                                       scale=0.5).then_inc(s_at, 1)
                        act.activation(al[:, d, CTX:T], bank[4 + d][:, :], ACT.Tanh, bias=col(HW + 2 + d),
                                       scale=0.5).then_inc(s_at, 1)
                    if not last:
                        hold(act, ga_, s_w, 16 * j + 48)
                        hold(act, ga_, s_z, 3 * j + 6)
                        high(0)
                        high(1)
                    hold(act, ga_, s_ld, j + 1)
                    for d in range(NDIR):
                        act.activation(ex[:, d, :, 1:CHUNK + 1], dl[:, d, :].rearrange("p (c s) -> p c s", c=NC),
                                       ACT.Exp).then_inc(s_ex, 1)
                        act.activation(ei[:, d, :], dl[:, d, :], ACT.Exp, scale=-1.0).then_inc(s_ex, 1)
                    hold(act, ga_, s_mx, j + 1)
                    act.activation(rn[:, :], rn[:, :], ACT.Sqrt).then_inc(s_std, 1)
                    hold(act, ga_, s_zs, 3 * j + 6)
                    hold(act, ga_, s_st, 16 * j + 1)
                    for dst, src in ((zr[:, 0, :], zs[:, 0, :]), (zr[:, 1, :], zs[:, 1, :]), (vd[:, 1, :], zs[:, 2, :])):
                        for a, b in ((0, CTX), (CTX, T)):
                            act.activation(dst[:, a:b], src[:, a:b][:, ::-1], ACT.Copy).then_inc(s_rv, 1)
                    act.activation(vd[:, 0, :], zs[:, 2, :], ACT.Copy).then_inc(s_rv, 1)
                    hold(act, ga_, s_g, j + 1)
                    act.activation(ga, bank[4][:, :], ACT.Copy).then_inc(s_gc, 1)
                    if not last:
                        hold(act, ga_, s_z, 3 * j + 7)
                        high(2)

                with act.Fori(0, NPAIR - 1) as j:
                    pair(j, False)
                pair(NPAIR - 1, True)

            @block.vector
            def _(dve):
                ch = Chain(dve, s_ch)

                def vectors(mu):
                    ch(dve.tensor_scalar(vv[:, HMU:HMU + 3], mu, 0.5, None, ALU.mult))
                    return dve.tensor_scalar(vv[:, OMU:OMU + 3], mu, -1.0, 1.0, ALU.mult, ALU.add)

                def low_half(n, q):
                    dve.tensor_tensor(wl[:, n % 2, :, :], wraw[:, q, :, :], wh[:, n % 2, :, :].bitcast(FP32),
                                      ALU.subtract).then_inc(s_lo, 1)

                def shift(q):
                    for a, o, m in ((0, 0, CTX), (CTX, CTX + 2, SEQ)):
                        ch(dve.tensor_tensor(ns[:, a:a + m], zp[:, q, o:o + m], zp[:, q, o + 2:o + 2 + m], ALU.add))
                    ch(dve.scalar_tensor_tensor(zs[:, q, :], ns[:, :], col(HMU + q), zs[:, q, :], ALU.mult, ALU.add))

                def reverse(dst, src):
                    ch(dve.tensor_copy(dst[:, 0:CTX], src[:, 0:CTX][:, ::-1]))
                    ch(dve.tensor_copy(dst[:, CTX:T], src[:, CTX:T][:, ::-1]))

                for s in (s_rec, s_st, s_at, s_gc):
                    dve.sem_inc(s, 1)
                ch(vectors(gv[:, GV_MUL:GV_MUL + 3]))
                dve.sem_inc(s_vec, 1)
                for n, q in enumerate(LORA_ORDER):
                    dve.wait_ge(s_hi, n + 1)
                    if n >= 2:
                        dve.wait_ge(s_z, n - 1)
                    low_half(n, q)
                for n, q in enumerate(LORA_ORDER):
                    dve.wait_ge(s_zc, 4 * n + 4)
                    shift(q)
                dve.sem_inc(s_zs, 3)
                dve.wait_ge(s_li, 2)
                H = slice(64, P)
                ch(dve.tensor_copy(lin[:, 1, :], zs[:, 1, :]))
                ch(dve.tensor_scalar(gin[:, :], gin[:, :], 0.5, 0.5, ALU.mult, ALU.add))
                ch(dve.tensor_copy(tmp[H, :], lin[H, 0, :]))
                reverse(lin[H, 0, :], tmp[H, :])
                reverse(lin[H, 1, :], zs[H, 1, :])
                dve.sem_inc(s_li, 1)

                dve.wait_ge(s_pv, 16)
                for dst, src, m, o in ((HMU, slice(PV_MU, PV_MU + 3), 0.5, 0.0), (OMU, slice(PV_MU, PV_MU + 3), -1.0, 1.0),
                                       (HW, slice(PV_W0, PV_W0 + 4), 0.5, 0.0), (HKA, slice(PV_KA, PV_KA + 1), 0.5, 0.0),
                                       (OKA, slice(PV_KA, PV_KA + 1), -0.5, 1.0), (HRK, slice(PV_RK, PV_RK + 1), 0.5, 0.0)):
                    n = src.stop - src.start
                    ch(dve.tensor_scalar(vva[:, :, dst:dst + n], pva[:, :, src], m, o, ALU.mult, ALU.add))
                ch(dve.tensor_copy(vva[:, :, KK:KK + 1], pva[:, :, PV_KK:PV_KK + 1]))
                for n in range(3):
                    dve.wait_ge(s_hi, 3 + n + 1)
                    low_half(n, PAIR_ORDER[n])

                def pair(j, last):
                    ch(dve.tensor_copy(vv[:, :], vva[:, bass.ds(j, 1), :].rearrange("p o v -> p (o v)")))
                    dve.sem_inc(s_vec, 1)
                    hold(dve, gd, s_zc, 12 * j + 16)
                    shift(1)
                    dve.sem_inc(s_zs, 1)
                    ch(dve.tensor_scalar(kk[:, :], zs[:, 1, :], col(KK), None, ALU.mult))
                    dve.sem_inc(s_kfd, 1)
                    hold(dve, gd, s_zc, 12 * j + 20)
                    shift(0)
                    dve.sem_inc(s_zs, 1)
                    hold(dve, gd, s_lt, 4 * j + 4)
                    for d in range(NDIR):
                        ch(dve.tensor_scalar(dl[:, d, :], dl[:, d, :], -0.5 * DECAY_C, -0.5 * DECAY_C, ALU.mult, ALU.add))
                        ch(dve.tensor_tensor_scan(dl[:, d, :], cm[:, :, :].rearrange("p c s -> p (c s)"), dl[:, d, :],
                                                  0.0, ALU.mult, ALU.add))
                    dve.sem_inc(s_ld, 1)
                    hold(dve, gd, s_n2, j + 1)
                    ch(dve.tensor_scalar(rn[:, 0:CTX], bank[2][:, 0:CTX], L2_EPS2, None, ALU.max))
                    ch(dve.tensor_scalar(rn[:, CTX:T], bank[3][:, :], L2_EPS2, None, ALU.max))
                    dve.sem_inc(s_mx, 1)
                    hold(dve, gd, s_zc, 12 * j + 24)
                    shift(2)
                    dve.sem_inc(s_zs, 1)
                    hold(dve, gd, s_at, 4 * j + 4 + 1)
                    for d in range(NDIR):
                        ch(dve.tensor_scalar(kf[:, d, :], al[:, d, :], col(HKA), col(OKA), ALU.mult, ALU.add))
                        ch(dve.tensor_scalar(al[:, d, :], al[:, d, :], 0.5, 0.5, ALU.mult, ALU.add))
                    ch(dve.tensor_tensor(tmp[:, 0:SEQ], kf[:, 0, CTX:T], kf[:, 1, CTX:T][:, ::-1], ALU.add))
                    ch(dve.tensor_tensor(tmp[:, 0:SEQ], tmp[:, 0:SEQ], zs[:, 1, CTX:T], ALU.mult))
                    ch(dve.scalar_tensor_tensor(tmp[:, 0:SEQ], tmp[:, 0:SEQ], col(HRK), zs[:, 0, CTX:T],
                                                ALU.mult, ALU.mult))
                    dve.sem_inc(s_bk, 1)
                    if not last:
                        for n in range(2):
                            hold(dve, gd, s_hi, 3 * j + (6 + n + 1))
                            low_half(n, PAIR_ORDER[n])
                    hold(dve, gd, s_st, 16 * j + 1)
                    hold(dve, gd, s_std, j + 1)
                    ch(dve.reciprocal(rn[:, :], rn[:, :]))
                    ch(dve.tensor_tensor(kk[:, :], kk[:, :], rn[:, :], ALU.mult))
                    reverse(zr[:, 2, :], kk[:, :])
                    hold(dve, gd, s_ex, 4 * j + 4)
                    for d in range(NDIR):
                        if d:
                            hold(dve, gd, s_rv, 7 * j + 7)
                        r, k, u = (zs[:, 0, :], zs[:, 1, :], kk[:, :]) if d == 0 else (zr[:, 0, :], zr[:, 1, :], zr[:, 2, :])
                        cs = lambda a: a.rearrange("p (c s) -> p c s", c=NC)
                        ch(dve.tensor_tensor(ra[:, d, :, 0, :], cs(r), ex[:, d, :, 1:CHUNK + 1], ALU.mult))
                        ch(dve.scalar_tensor_tensor(ra[:, d, :, 1, :], cs(u), -1.0, ex[:, d, :, 0:CHUNK],
                                                    ALU.mult, ALU.mult))
                        ch(dve.tensor_tensor(kf[:, d, :], kf[:, d, :], k, ALU.mult))
                        ch(dve.tensor_tensor(kb[:, d, :, 0, :], cs(kf[:, d, :]), cs(ei[:, d, :]), ALU.mult))
                        ch(dve.tensor_tensor(al[:, d, :], al[:, d, :], u, ALU.mult))
                        ch(dve.tensor_tensor(kb[:, d, :, 1, :], cs(al[:, d, :]), cs(ei[:, d, :]), ALU.mult))
                        ch(dve.tensor_copy(ecr[:, d, :], ex[:, d, :, CHUNK]))
                    hold(dve, gd, s_bm, j + 1)
                    ch(dve.tensor_tensor(bo, bank[5][:, :], zs[:, 2, CTX:T], ALU.mult))
                    dve.sem_inc(s_rec, 1)
                    if not last:
                        hold(dve, gd, s_hi, 3 * j + 9)
                        low_half(2, PAIR_ORDER[2])

                with dve.Fori(0, NPAIR - 1) as j:
                    ch.loop()
                    pair(j, False)
                pair(NPAIR - 1, True)

            @block.tensor
            def _(pe):
                def z_tile(q, n):
                    b = bank[0 + 2 * (q % 2)], bank[1 + 2 * (q % 2)]
                    for lo, hi, o in ((0, CTX, b[0][:, 0:CTX]), (CTX, T, b[1][:, :])):
                        for k in range(KT):
                            mm = split_mm(pe, o, wh[:, n % 2, k, :], wl[:, n % 2, k, :], ht_hi[:, k, lo:hi],
                                          ht_lo[:, k, lo:hi], k == 0, k == KT - 1)
                    mm.then_inc(s_z, 1)

                def lora(i, last_sem):
                    for d in range(NDIR):
                        R = slice(64 * d, 64 * d + 64)
                        pe.matmul(bank[6 + d][:, 0:CTX], lw[R, i, :], lin[R, i, 0:CTX], start=True, stop=True)
                        mm = pe.matmul(bank[4 + d][:, :], lw[R, i, :], lin[R, i, CTX:T], start=True, stop=True)
                    mm.then_inc(last_sem, 1)

                for n, q in enumerate(LORA_ORDER):
                    pe.wait_ge(s_lo, n + 1)
                    if n >= 2:
                        pe.wait_ge(s_zc, 4 * (n - 1))
                    z_tile(q, n)
                pe.wait_ge(s_li, 3)
                pe.wait_ge(s_zc, 12)
                for n in range(2):
                    pe.wait_ge(s_lo, 3 + n + 1)
                    z_tile(PAIR_ORDER[n], n)

                def pair(j, last):
                    hold(pe, gp, s_lw0, 16 * j + 16)
                    hold(pe, gp, s_at, 4 * j + 1)
                    hold(pe, gp, s_gc, j + 1)
                    hold(pe, gp, s_rec, j + 1)
                    lora(0, s_lw)
                    hold(pe, gp, s_lo, 3 * j + 6)
                    hold(pe, gp, s_zc, 12 * j + 20)
                    z_tile(PAIR_ORDER[2], 2)
                    hold(pe, gp, s_sq, j + 1)
                    pe.matmul(bank[2][:, 0:CTX], blk[:, :], tmp[:, 0:CTX], start=True, stop=True)
                    pe.matmul(bank[3][:, :], blk[:, :], tmp[:, CTX:T], start=True, stop=True).then_inc(s_n2, 1)
                    hold(pe, gp, s_lt, 4 * j + 4)
                    lora(1, s_la)
                    hold(pe, gp, s_at, 4 * j + 4 + 1)
                    pe.matmul(bank[4][:, :], lw[:, 2, :], gin[:, :], start=True, stop=True).then_inc(s_g, 1)
                    if not last:
                        hold(pe, gp, s_lo, 3 * j + 7)
                        hold(pe, gp, s_mx, j + 1)
                        z_tile(PAIR_ORDER[0], 0)
                    hold(pe, gp, s_bk, j + 1)
                    pe.matmul(bank[5][:, :], blk[:, :], tmp[:, 0:SEQ], start=True, stop=True).then_inc(s_bm, 1)
                    if not last:
                        hold(pe, gp, s_lo, 3 * j + 8)
                        hold(pe, gp, s_zc, 12 * j + 24)
                        z_tile(PAIR_ORDER[1], 1)

                with pe.Fori(0, NPAIR - 1) as j:
                    pair(j, False)
                pair(NPAIR - 1, True)



def scan(nc, sb, sem, g):
    ident, blk, bank, o_all, record = (g[k] for k in ("ident", "blk", "bank", "o_all", "record"))
    tri_dram, inv_dram, invt_dram, gv = (g[k] for k in ("tri_dram", "inv_dram", "invt_dram", "gv"))
    LO, HI = slice(0, 64), slice(64, P)
    B1, B2 = slice(64, 96), slice(96, P)
    XC = NC - CC
    NS = NDIR * (NC - 1)
    with ExitStack() as st:
        rec = sb(st, "rec2", [P, RC_N])
        ra = rec[:, RC_RA:RC_KB].rearrange("p (d c q s) -> p d c q s", d=NDIR, c=NC, q=2)
        kb = rec[:, RC_KB:RC_V].rearrange("p (d c q s) -> p d c q s", d=NDIR, c=NC, q=2)
        vd = rec[:, RC_V:RC_EC].rearrange("p (d t) -> p d t", d=NDIR)
        ecr = rec[:, RC_EC:RC_BO].rearrange("p (d c) -> p d c", d=NDIR)
        bo, ga = rec[:, RC_BO:RC_GA], rec[:, RC_GA:RC_N]
        pv = sb(st, "pv2", [P, PV_N])
        kbt = sb(st, "kbt", [P, NDIR, NC, P])
        vu = sb(st, "vu", [P, NDIR, NC, 2, HEAD])
        am = sb(st, "am", [P, NDIR, NC, 2, P])
        zi = sb(st, "zi", [P, NDIR, NC, 2, CHUNK])
        xi = sb(st, "xi", [P, NDIR, NC, 2, HB])
        hs = sb(st, "hs", [P, NDIR, NC, HEAD])
        he = sb(st, "he", [P, NDIR, HEAD])
        qs = sb(st, "qs", [P, 2, NDIR, HEAD])
        mask = sb(st, "mask", [P, P])
        eye = sb(st, "eye", [96, HB, HB])
        gt = sb(st, "gt", [96, HB, HB])
        gz = sb(st, "gz", [96, HB, HB])
        gx = sb(st, "gx", [96, HB, HB])
        gm = sb(st, "gm", [96, HB, HB])
        y = sb(st, "y", [P, SEQ])
        yc = sb(st, "yc", [P, SEQ])
        ysq = sb(st, "ysq", [P, SEQ])
        b64 = sb(st, "b64", [P, P])
        (s_rec, s_c, s_vt, s_vc, s_kt, s_kc, s_a, s_am, s_tri, s_gt, s_inv, s_io, s_il, s_r1, s_r1c, s_r2, s_r2c, s_p,
         s_pc, s_q, s_qs, s_u, s_uc, s_h, s_hs, s_he, s_y, s_yc, s_mu, s_cen, s_sq, s_var, s_vs, s_std, s_o, s_ch,
         s_yd, s_ra, s_ve) = (sem(st, n) for n in (
             "v_kb_loaded", "consts_c", "v_transposed", "v_copied", "kb_transposed", "kb_copied", "a_product",
             "a_masked", "triangles_out", "triangles_in", "inverted", "inverse_out", "inverse_in", "a21_x11",
             "a21_x11_copied", "z12", "z12_copied", "akv", "akv_copied", "q_product", "q_ready", "u_product", "u_ready",
             "h_product", "state_ready", "state_decayed", "y_products", "y_ready", "mean_product", "centred", "squared",
             "var_product", "var_ready", "std_ready", "readout_ready", "dve_chain_c", "y_summed",
             "ra_loaded", "vectors_loaded"))
        gp, ga_, gd, gs = (sem(st, "gate_c_" + k) for k in ("pe", "act", "dve", "sp"))
        units = lambda a: a.rearrange("p d c h s -> p (d c h) s")

        with nc.Block() as block:
            @block.gpsimd
            def _(pool):
                made = 0

                def done(ins):
                    nonlocal made
                    made += 1
                    ins.then_inc(s_c, 1)
                    pool.wait_ge(s_c, made)

                done(pool.memset(mask[:, :], 1.0))
                done(pool.memset(eye[:, :, :], 0.0))
                done(pool.memset(zi[:, :, :, :, :], 0.0))
                done(pool.memset(hs[:, :, 0:1, :], 0.0))
                done(pool.tensor_scalar(b64[:, :], blk[:, :], 1.0 / HEAD, 0.0, ALU.mult, ALU.add))
                for h in range(2):
                    R = slice(64 * h, 64 * h + 64)
                    done(pool.affine_select(out=mask[R, 0:64], in_=mask[R, 0:64], compare_op=ALU.is_ge, fill=0.0, base=0,
                                            pattern=[[1, 64]], channel_multiplier=-1))
                    done(pool.affine_select(out=mask[R, 64:P], in_=mask[R, 64:P], compare_op=ALU.is_gt, fill=0.0, base=0,
                                            pattern=[[1, 64]], channel_multiplier=-1))
                done(pool.affine_select(out=eye[:, :, :], in_=eye[:, :, :], compare_op=ALU.not_equal, fill=1.0, base=0,
                                        pattern=[[1, HB], [-1, HB]], channel_multiplier=0))

            @block.sync
            def _(sp):
                with sp.Fori(0, NPAIR) as j:
                    for freed, n, a, b in ((s_kt, 6, RC_KB, RC_V), (s_kt, 6, RC_V, RC_EC), (s_y, 1, RC_RA, RC_KB)):
                        hold(sp, gs, freed, n * j + 1)
                        sp.dma_start(rec[:, a:b], record[bass.ds(j, 1), :, a:b].rearrange("o p n -> (o p) n")).then_inc(
                            s_ra if a == RC_RA else s_rec, 16)
                    sp.wait_ge(s_am, 12 * j + 12)
                    sp.dma_start(tri_dram.rearrange("u s t -> s u t"), units(am)[HI, :, HI]).then_inc(s_tri, 16)
                    sp.wait_ge(s_tri, 16 * j + 16)
                    for h in range(2):
                        sp.dma_start(gt[UNITS * h:UNITS * h + UNITS, :, :],
                                     tri_dram[:, HB * h:HB * h + HB, HB * h:HB * h + HB]).then_inc(s_gt, 16)
                    hold(sp, gs, s_o, j + 1)
                    sp.dma_start(rec[:, RC_EC:], record[bass.ds(j, 1), :, RC_EC:].rearrange("o p n -> (o p) n")).then_inc(s_ve, 16)
                    sp.dma_start(pv[:, :], g["pvec_in"][bass.ds(j, 1), :, :].rearrange("o p v -> (o p) v")).then_inc(s_ve, 16)
                    sp.wait_ge(s_inv, j + 1)
                    sp.dma_start(inv_dram.rearrange("h u s t -> (h u) s t"), gz[:, :, :]).then_inc(s_io, 16)
                    sp.dma_start(invt_dram, gx[0:UNITS, :, :]).then_inc(s_io, 16)
                    sp.wait_ge(s_io, 32 * j + 32)
                    for h in range(2):
                        R = slice(64 + HB * h, 64 + HB * h + HB)
                        sp.dma_start(units(zi)[R, :, HB * h:HB * h + HB], inv_dram[h].rearrange("u s t -> s u t")).then_inc(s_il, 16)
                    sp.dma_start(units(xi)[B1, :, :], invt_dram.rearrange("u s t -> s u t")).then_inc(s_il, 16)
                sp.wait_ge(s_o, NPAIR + 1)

            @block.scalar
            def _(act):
                def norm_square(j):
                    hold(act, ga_, s_cen, j + 1)
                    act.activation(ysq[:, :], yc[:, :], ACT.Square).then_inc(s_sq, 1)

                def norm_root(j):
                    hold(act, ga_, s_vs, j + 1)
                    act.activation(ysq[:, :], ysq[:, :], ACT.Sqrt).then_inc(s_std, 1)

                def pair(j, first):
                    if not first:
                        norm_square(j - 1)
                    for n in range(6):
                        d, c = divmod(4 * n, NC)
                        hold(act, ga_, s_vt, 6 * j + (n + 1))
                        act.activation(vu[LO, d, c:c + 4, :, :].rearrange("p c h v -> p (c h v)"), bank[2 + n % 2][LO, :],
                                       ACT.Copy).then_inc(s_vc, 1)
                    if not first:
                        norm_root(j - 1)
                    for n in range(6):
                        d, c = divmod(4 * n, NC)
                        hold(act, ga_, s_kt, 6 * j + (n + 2))
                        act.activation(kbt[:, d, c:c + 4, :].rearrange("p c k -> p (c k)"), bank[2 + n % 2][:, :],
                                       ACT.Copy).then_inc(s_kc, 1)
                    for n in range(6):
                        hold(act, ga_, s_p, 6 * j + (n + 1))
                        hold(act, ga_, s_r1, 3 * j + 3)
                        act.activation(units(am)[HI, 8 * n:8 * n + 8, HI],
                                       bank[4 + n % 2][HI, :].rearrange("p (u v) -> p u v", v=HEAD), ACT.Copy).then_inc(s_pc, 1)
                    for n in range(3):
                        hold(act, ga_, s_r1, 3 * j + (n + 1))
                        act.activation(units(xi)[B2, 16 * n:16 * n + 16, :],
                                       bank[n][B2, :].rearrange("p (u t) -> p u t", t=HB), ACT.Copy).then_inc(s_r1c, 1)
                    for n in range(3):
                        hold(act, ga_, s_r2, 3 * j + (n + 1))
                        act.activation(units(zi)[B1, 16 * n:16 * n + 16, HB:CHUNK],
                                       bank[n][B1, :].rearrange("p (u t) -> p u t", t=HB), ACT.Copy).then_inc(s_r2c, 1)
                    hold(act, ga_, s_ve, 32 * j + 32)
                    for c in range(NC):
                        if c < NC - 1:
                            for d in range(NDIR):
                                if c:
                                    hold(act, ga_, s_hs, NS * j + (NDIR * (c - 1) + d + 1))
                                act.activation(he[:, d, :], hs[:, d, c, :], ACT.Copy, scale=ecr[:, d, c:c + 1]).then_inc(s_he, 1)
                        for d in range(NDIR):
                            hold(act, ga_, s_u, NDIR * NC * j + (NDIR * c + d + 1))
                            act.activation(vu[HI, d, c, :, :], bank[2 + 4 * d][HI, 0:2 * HEAD].rearrange(
                                "p (h v) -> p h v", h=2), ACT.Copy).then_inc(s_uc, 1)
                    hold(act, ga_, s_y, j + 1 + 1)
                    act.activation(y[:, :], bank[4][:, :], ACT.Copy).then_inc(s_yc, 1)

                pair(0, True)
                with act.Fori(0, NPAIR - 1) as i:
                    pair(i + 1, False)
                norm_square(NPAIR - 1)
                norm_root(NPAIR - 1)

            @block.vector
            def _(dve):
                ch = Chain(dve, s_ch)
                for s in (s_kt, s_y, s_o):
                    dve.sem_inc(s, 1)
                dve.wait_ge(s_c, 10)
                def read_out(j):
                    hold(dve, gd, s_mu, j + 1)
                    ch(dve.tensor_tensor(yc[:, :], y[:, :], bank[0][:, :], ALU.subtract))
                    dve.sem_inc(s_cen, 1)
                    hold(dve, gd, s_var, j + 1)
                    ch(dve.tensor_scalar(ysq[:, :], bank[1][:, :], GN_EPS, None, ALU.add))
                    dve.sem_inc(s_vs, 1)
                    hold(dve, gd, s_std, j + 1)
                    ch(dve.reciprocal(ysq[:, :], ysq[:, :]))
                    ch(dve.scalar_tensor_tensor(yc[:, :], yc[:, :], pv[:, PV_LNW:PV_LNW + 1], ysq[:, :], ALU.mult, ALU.mult))
                    ch(dve.tensor_tensor(yc[:, :], yc[:, :], bo, ALU.add))
                    ch(dve.scalar_tensor_tensor(o_all[:, bass.ds(j, 1), :].rearrange("p o t -> p (o t)"), yc[:, :],
                                                pv[:, PV_LNB:PV_LNB + 1], ga, ALU.add, ALU.mult))
                    dve.sem_inc(s_o, 1)

                def pair(j, first):
                    for n in range(12):
                        d, h, c = n // 6, n // 3 % 2, 4 * (n % 3)
                        hold(dve, gd, s_a, 12 * j + (n + 1))
                        dve.tensor_tensor(am[:, d, c:c + 4, h, :], bank[4 + n % 4][:, :].rearrange("p (c t) -> p c t", c=4),
                                          mask[:, :].unsqueeze(1).broadcast_to((P, 4, P)), ALU.mult).then_inc(s_am, 1)
                    if not first:
                        read_out(j - 1)
                    ch(dve.tensor_copy(gz[:, :, :], eye[:, :, :]))
                    hold(dve, gd, s_gt, 32 * j + 32)
                    for u in range(HB - 1):
                        n, m = u + 1, HB - 1 - u
                        o = gm[:, 0:n, 0:m]
                        ch(dve.tensor_tensor(o, gz[:, 0:n, u:u + 1].broadcast_to((96, n, m)),
                                             gt[:, u:u + 1, n:HB].broadcast_to((96, n, m)), ALU.mult))
                        ch(dve.tensor_tensor(gz[:, 0:n, n:HB], gz[:, 0:n, n:HB], o, ALU.add))
                    ch(dve.tensor_copy(gx[:, :, :], gz[:, :, :].rearrange("p s t -> p t s")))
                    dve.sem_inc(s_inv, 1)
                    hold(dve, gd, s_pc, 6 * j + 6)
                    for c in range(NC):
                        for d in range(NDIR):
                            hold(dve, gd, s_q, NDIR * NC * j + (NDIR * c + d + 1))
                            for h in range(2):
                                dve.tensor_tensor(qs[HI, h, d, :], bank[4 * d + h][HI, 0:HEAD], am[HI, d, c, h, HI],
                                                  ALU.add).then_inc(s_qs, 1)
                        if c < NC - 1:
                            for d in range(NDIR):
                                hold(dve, gd, s_h, NS * j + (NDIR * c + d + 1))
                                hold(dve, gd, s_he, NS * j + (NDIR * c + d + 1))
                                dve.scalar_tensor_tensor(hs[:, d, c + 1, :], bank[3 + 4 * d][:, 0:HEAD], ecr[:, d, c:c + 1],
                                                         he[:, d, :], ALU.mult, ALU.add).then_inc(s_hs, 1)
                    hold(dve, gd, s_yc, j + 1)
                    ch(dve.tensor_tensor(y[:, :], y[:, :], bank[6][:, :], ALU.add))
                    ch(dve.tensor_tensor(y[:, :], y[:, :], bank[5][:, ::-1], ALU.add))
                    ch(dve.tensor_tensor(y[:, :], y[:, :], bank[7][:, ::-1], ALU.add))
                    dve.sem_inc(s_yd, 1)

                pair(0, True)
                with dve.Fori(0, NPAIR - 1) as i:
                    ch.loop()
                    pair(i + 1, False)
                read_out(NPAIR - 1)

            @block.tensor
            def _(pe):
                pe.wait_ge(s_c, 10)
                def mean(j):
                    hold(pe, gp, s_yd, j + 1)
                    pe.matmul(bank[0][:, :], b64[:, :], y[:, :], start=True, stop=True).then_inc(s_mu, 1)

                def variance(j):
                    hold(pe, gp, s_sq, j + 1)
                    pe.matmul(bank[1][:, :], b64[:, :], ysq[:, :], start=True, stop=True).then_inc(s_var, 1)

                def pair(j, first):
                    hold(pe, gp, s_rec, 32 * j + 32)
                    if not first:
                        hold(pe, gp, s_yd, j)
                    for n in range(12):
                        d, h, c = n // 6, n // 3 % 2, 4 * (n % 3)
                        R = slice(64 * h, 64 * h + 64)
                        if n == 0:
                            hold(pe, gp, s_ra, 16 * j + 16)
                        if n >= 4:
                            hold(pe, gp, s_am, 12 * j + (n - 3))
                        for i in range(4):
                            mm = pe.matmul(bank[4 + n % 4][:, i * P:i * P + P],
                                           kb[R, d, c + i, :, :].rearrange("p q s -> p (q s)"),
                                           ra[R, d, c + i, :, :].rearrange("p q s -> p (q s)"), start=True, stop=True)
                        mm.then_inc(s_a, 1)
                    if not first:
                        mean(j - 1)
                    for n in range(6):
                        d, c = divmod(4 * n, NC)
                        if n >= 2:
                            hold(pe, gp, s_vc, 6 * j + (n - 1))
                        for i in range(4):
                            t = (c + i) * CHUNK
                            mm = pe.transpose(bank[2 + n % 2][LO, i * P:i * P + P], vd[:, d, t:t + CHUNK], ident[:, :])
                        mm.then_inc(s_vt, 1)
                    if not first:
                        variance(j - 1)
                    for n in range(6):
                        d, c = divmod(4 * n, NC)
                        if n >= 2:
                            hold(pe, gp, s_kc, 6 * j + (n - 1))
                        else:
                            hold(pe, gp, s_vc, 6 * j + (n + 5))
                        for i in range(4):
                            mm = pe.transpose(bank[2 + n % 2][:, i * P:i * P + P],
                                              kb[:, d, c + i, :, :].rearrange("p q s -> p (q s)"), ident[:, :])
                        mm.then_inc(s_kt, 1)
                    hold(pe, gp, s_am, 12 * j + 12)
                    vuu, amu, ziu, xiu = units(vu), units(am), units(zi), units(xi)
                    def a21(n):
                        for i in range(16):
                            u = 16 * n + i
                            mm = pe.matmul(bank[n][B2, HB * i:HB * i + HB], amu[B1, u, 64 + HB:P], xiu[B1, u, :],
                                           start=True, stop=True)
                        mm.then_inc(s_r1, 1)

                    def akv(n):
                        for i in range(8):
                            u = 8 * n + i
                            mm = pe.matmul(bank[4 + n % 2][HI, HEAD * i:HEAD * i + HEAD], amu[LO, u, HI], vuu[LO, u, :],
                                           start=True, stop=True)
                        mm.then_inc(s_p, 1)

                    akv(0)
                    akv(1)
                    hold(pe, gp, s_il, 48 * j + 48)
                    hold(pe, gp, s_kc, 6 * j + 6)
                    if not first:
                        hold(pe, gp, s_vs, j)
                    for n in range(3):
                        a21(n)
                    for n in range(2, 6):
                        hold(pe, gp, s_pc, 6 * j + (n - 1))
                        akv(n)
                    for n in range(3):
                        hold(pe, gp, s_r1c, 3 * j + (n + 1))
                        for i in range(16):
                            u = 16 * n + i
                            mm = pe.matmul(bank[n][B1, HB * i:HB * i + HB], xiu[B2, u, :], ziu[B2, u, HB:CHUNK],
                                           start=True, stop=True)
                        mm.then_inc(s_r2, 1)
                    hold(pe, gp, s_r2c, 3 * j + 3)
                    hold(pe, gp, s_pc, 6 * j + 6)
                    for c in range(NC):
                        for d in range(NDIR):
                            if c:
                                hold(pe, gp, s_hs, NS * j + (NDIR * (c - 1) + d + 1))
                            for h in range(2):
                                R = slice(64 * h, 64 * h + 64)
                                mm = pe.matmul(bank[4 * d + h][HI, 0:HEAD], ra[R, d, c, 1, :], hs[R, d, c, :],
                                               start=True, stop=True)
                            mm.then_inc(s_q, 1)
                        for d in range(NDIR):
                            hold(pe, gp, s_qs, 2 * NDIR * NC * j + (2 * NDIR * c + 2 * d + 2))
                            for h in range(2):
                                mm = pe.matmul(bank[2 + 4 * d][HI, h * HEAD:h * HEAD + HEAD], zi[HI, d, c, h, :],
                                               qs[HI, h, d, :], start=True, stop=True)
                            mm.then_inc(s_u, 1)
                        if c < NC - 1:
                            for d in range(NDIR):
                                hold(pe, gp, s_uc, NDIR * NC * j + (NDIR * c + d + 1))
                                for h in range(2):
                                    R = slice(64 * h, 64 * h + 64)
                                    mm = pe.matmul(bank[3 + 4 * d][R, 0:HEAD], kbt[:, d, c, R], vu[:, d, c, h, :],
                                                   start=True, stop=True)
                                mm.then_inc(s_h, 1)
                    hold(pe, gp, s_uc, NDIR * NC * j + NDIR * NC)
                    for d in range(NDIR):
                        for h in range(2):
                            R = slice(64 * h, 64 * h + 64)
                            for c in range(XC):
                                o = slice(c * CHUNK, c * CHUNK + CHUNK)
                                pe.matmul(bank[4 + d][R, o], hs[R, d, CC + c, :], ra[R, d, CC + c, 0, :], start=True, stop=True)
                        for h in range(2):
                            R = slice(64 * h, 64 * h + 64)
                            for c in range(XC):
                                o = slice(c * CHUNK, c * CHUNK + CHUNK)
                                mm = pe.matmul(bank[6 + d][R, o], vu[:, d, CC + c, h, :], am[:, d, CC + c, h, LO],
                                               start=True, stop=True)
                    mm.then_inc(s_y, 1)

                pair(0, True)
                with pe.Fori(0, NPAIR - 1) as i:
                    pair(i + 1, False)
                mean(NPAIR - 1)
                variance(NPAIR - 1)



def merge(nc, sb, sem, g):
    gv, bank, ht_hi, ht_lo, o_all, m_dram = (g[k] for k in ("gv", "bank", "ht_hi", "ht_lo", "o_all", "m_dram"))
    NW = len(WINDOWS)
    PAD = max(WINDOWS) // 2
    PR, PC = ROWS + 2 * PAD, GRID_W + 2 * PAD
    NM = 3 * KT + NW
    with ExitStack() as st:
        p_hi = sb(st, "p_hi", [P, NW, SEQ], F32R)
        p_lo = sb(st, "p_lo", [P, NW, SEQ], F32R)
        with ExitStack() as s1:
            wu = sb(s1, "wu", [P, NW, KT, P])
            wuh = sb(s1, "wuh", [P, 2, KT, P], F32R)
            wul = sb(s1, "wul", [P, 2, KT, P], F32R)
            wp = sb(s1, "wp", [P, NW, P])
            icn = sb(s1, "icn", [P, NW, SEQ])
            u0, ca, cb, ea, eb = (sb(s1, n, [P, PR, PC]) for n in ("u0", "ca", "cb", "ea", "eb"))
            pl = sb(s1, "pl", [P, SEQ])
            pf = sb(s1, "pf", [P, SEQ])
            s_w, s_z0, s_hi, s_lo, s_u, s_ue, s_pl, s_pp, s_pe, s_ph, s_plo, s_ch = (sem(s1, n) for n in (
                "pool_weights", "pool_zeroed", "pool_w_hi", "pool_w_lo", "u_made", "u_padded", "pooled",
                "pool_product", "pool_scaled", "pool_hi", "pool_lo", "dve_chain_d"))
            centre = lambda a: a[:, PAD:PAD + ROWS, PAD:PAD + GRID_W]
            grid = lambda a: a.rearrange("p (r c) -> p r c", c=GRID_W)
            with nc.Block() as block:
                def pool_out(act, q):
                    act.wait_ge(s_pp, q + 1)
                    if q:
                        act.wait_ge(s_plo, q)
                    act.activation(pf[:, :], bank[2 + q % 2][:, :], ACT.Copy, scale=gv[:, GV_PS + q:GV_PS + q + 1]).then_inc(s_pe, 1)
                    act.wait_ge(s_pe, q + 1)
                    act.activation(p_hi[:, q, :], pf[:, :], ACT.Copy).then_inc(s_ph, 1)

                def low(dve, q):
                    dve.wait_ge(s_ph, q + 1)
                    dve.tensor_tensor(p_lo[:, q, :], pf[:, :], p_hi[:, q, :].bitcast(FP32), ALU.subtract).then_inc(s_plo, 1)

                def pooled(pe, q):
                    pe.wait_ge(s_pl, q + 1)
                    if q >= 2:
                        pe.wait_ge(s_pe, q - 1)
                    pe.matmul(bank[2 + q % 2][:, :], wp[:, q, :], pl[:, :], start=True, stop=True).then_inc(s_pp, 1)

                @block.sync
                def _(sp):
                    sp.dma_start(wu[:, :, :, :], g["wpu_in"].rearrange("p (q k n) -> p q k n", q=NW, k=KT)).then_inc(s_w, 16)
                    sp.dma_start(wp[:, :, :], g["wpool_in"]).then_inc(s_w, 16)
                    sp.dma_start(icn[:, :, :], g["invcnt_in"].unsqueeze(0).broadcast_to((P, NW, SEQ))).then_inc(s_w, 16)
                    sp.wait_ge(s_w, 48)

                @block.gpsimd
                def _(pool):
                    for n, a in enumerate((u0, ca, cb)):
                        pool.memset(a[:, :, :], 0.0).then_inc(s_z0, 1)
                        pool.wait_ge(s_z0, n + 1)

                @block.scalar
                def _(act):
                    act.wait_ge(s_w, 48)
                    act.wait_ge(s_z0, 3)
                    for q in range(NW):
                        if q >= 2:
                            act.wait_ge(s_u, q - 1)
                        act.activation(wuh[:, q % 2, :, :], wu[:, q, :, :], ACT.Copy).then_inc(s_hi, 1)
                        if q:
                            pool_out(act, q - 1)
                        act.wait_ge(s_u, q + 1)
                        if q:
                            act.wait_ge(s_pl, q)
                        act.activation(centre(u0), grid(bank[q % 2][:, :]), ACT.Copy).then_inc(s_ue, 1)
                    pool_out(act, NW - 1)

                @block.vector
                def _(dve):
                    ch = Chain(dve, s_ch)
                    dve.wait_ge(s_z0, 3)
                    for q, w in enumerate(WINDOWS):
                        dve.wait_ge(s_hi, q + 1)
                        dve.tensor_tensor(wul[:, q % 2, :, :], wu[:, q, :, :], wuh[:, q % 2, :, :].bitcast(FP32),
                                          ALU.subtract).then_inc(s_lo, 1)
                        if q:
                            low(dve, q - 1)
                        dve.wait_ge(s_ue, q + 1)
                        src = u0
                        R = slice(PAD, PAD + ROWS)
                        for n in range(q + 1):
                            dst = (ca, cb)[n % 2]
                            m = w // 2 - (1 << n)
                            a, b = (1, 0) if n == 0 else (1 << (n - 1), 1 << (n - 1))
                            lo, hi = PAD - m, PAD + GRID_W + m
                            ch(dve.tensor_tensor(dst[:, R, lo:hi], src[:, R, lo - a:hi - a], src[:, R, lo + b:hi + b], ALU.add))
                            src = dst
                        C = slice(PAD, PAD + GRID_W)
                        for n in range(q + 1):
                            dst = (ea, eb)[n % 2]
                            m = w // 2 - (1 << n)
                            a, b = (1, 0) if n == 0 else (1 << (n - 1), 1 << (n - 1))
                            lo, hi = PAD - m, PAD + ROWS + m
                            ch(dve.tensor_tensor(dst[:, lo:hi, C], src[:, lo - a:hi - a, C], src[:, lo + b:hi + b, C], ALU.add))
                            src = dst
                        if q:
                            dve.wait_ge(s_pp, q)
                        ch(dve.tensor_tensor(grid(pl[:, :]), centre(src), grid(icn[:, q, :]), ALU.mult))
                        dve.tensor_tensor(grid(pl[:, :]), grid(pl[:, :]), centre(u0), ALU.subtract).then_inc(s_pl, 1)
                        dve.wait_ge(s_pl, q + 1)
                    low(dve, NW - 1)

                @block.tensor
                def _(pe):
                    for q in range(NW):
                        pe.wait_ge(s_lo, q + 1)
                        if q >= 2:
                            pe.wait_ge(s_ue, q - 1)
                        for k in range(KT):
                            mm = split_mm(pe, bank[q % 2][:, :], wuh[:, q % 2, k, :], wul[:, q % 2, k, :],
                                          ht_hi[:, k, CTX:T], ht_lo[:, k, CTX:T], k == 0, k == KT - 1)
                        mm.then_inc(s_u, 1)
                        if q:
                            pooled(pe, q - 1)
                    pooled(pe, NW - 1)

        wm = sb(st, "wmg", [P, NM, P])
        wh = sb(st, "wmg_hi", [P, 2, NM, P], F32R)
        wl = sb(st, "wmg_lo", [P, 2, NM, P], F32R)
        o_hi = sb(st, "o_hi", [P, NPAIR, SEQ], F32R)
        o_lo = sb(st, "o_lo", [P, NPAIR, SEQ], F32R)
        hbg = sb(st, "hbg", [P, 2, KT])
        hb = sb(st, "hb", [P, 2])
        tg = sb(st, "tg", [P, 2, SEQ])
        mt = sb(st, "mt", [P, SEQ])
        s_w, s_hi, s_lo, s_oh, s_ol, s_hb, s_mm, s_tg, s_m, s_st, s_ch = (sem(st, n) for n in (
            "merge_weights", "merge_hi", "merge_lo", "o_hi_made", "o_lo_made", "gate_bias", "merge_products",
            "gate_tanh", "m_made", "m_stored", "dve_chain_e"))
        gp, ga_, gd = (sem(st, "gate_e_" + k) for k in ("pe", "act", "dve"))
        with nc.Block() as block:
            @block.sync
            def _(sp):
                with sp.Fori(0, NPAIR) as j:
                    sp.wait_ge(s_lo, j + 1)
                    sp.wait_ge(s_hi, j + 1)
                    sp.dma_start(wm[:, :, :], g["wmerge_in"][bass.ds(j, 1), :, :].rearrange(
                        "o p (m n) -> (o p) m n", m=NM)).then_inc(s_w, 16)

            @block.scalar
            def _(act):
                for k in range(NPAIR):
                    act.activation(o_hi[:, k, :], o_all[:, k, :], ACT.Copy).then_inc(s_oh, 1)

                def high(b, loaded):
                    hold(act, ga_, s_w, loaded)
                    act.activation(wh[:, b, :, :], wm[:, :, :], ACT.Copy).then_inc(s_hi, 1)

                def two_tiles(i, last):
                    for b in range(2):
                        if b == 0 or not last:
                            high(1 - b, 32 * i + (16 * b + 32))
                        hold(act, ga_, s_hb, 2 * i + (b + 1))
                        hold(act, ga_, s_mm, 2 * i + (b + 1))
                        for q in range(2):
                            act.activation(tg[:, q, :], bank[4 * b + q][:, :], ACT.Tanh, bias=hb[:, q:q + 1],
                                           scale=0.5).then_inc(s_tg, 1)
                        hold(act, ga_, s_m, 2 * i + (b + 2))
                        act.dma_start(m_dram[bass.ds(2 * i + b, 1), :, :].rearrange("o p t -> (o p) t"),
                                      mt[:, :]).then_inc(s_st, 16)

                high(0, 16)
                with act.Fori(0, NPAIR // 2 - 1) as i:
                    two_tiles(i, False)
                two_tiles(NPAIR // 2 - 1, True)
                act.wait_ge(s_st, 16 * NPAIR + 1)

            @block.vector
            def _(dve):
                ch = Chain(dve, s_ch)
                for s in (s_hi, s_lo, s_m, s_st):
                    dve.sem_inc(s, 1)
                ch(dve.tensor_scalar(hbg[:, :, :], gv[:, GV_BG:GV_BG + 16].rearrange("p (i k) -> p i k", i=2), 0.5, None, ALU.mult))
                for k in range(NPAIR):
                    dve.wait_ge(s_oh, k + 1)
                    dve.tensor_tensor(o_lo[:, k, :], o_all[:, k, :], o_hi[:, k, :].bitcast(FP32), ALU.subtract).then_inc(s_ol, 1)

                def low(b, made):
                    hold(dve, gd, s_hi, made + 1)
                    dve.tensor_tensor(wl[:, b, :, :], wm[:, :, :], wh[:, b, :, :].bitcast(FP32), ALU.subtract).then_inc(s_lo, 1)

                def two_tiles(i, last):
                    for b in range(2):
                        if b == 0 or not last:
                            low(1 - b, 2 * i + (b + 2))
                        ch(dve.tensor_copy(hb[:, :], hbg[:, :, bass.ds(2 * i + b, 1)].rearrange("p i o -> p (i o)")))
                        dve.sem_inc(s_hb, 1)
                        hold(dve, gd, s_tg, 4 * i + (2 * b + 2))
                        hold(dve, gd, s_st, 32 * i + (16 * b + 1))
                        for q in range(2):
                            ch(dve.scalar_tensor_tensor(tg[:, q, :], tg[:, q, :], 1.0, bank[4 * b + 2 + q][:, :], ALU.add, ALU.mult))
                        ch(dve.tensor_tensor(mt[:, :], tg[:, 0, :], tg[:, 1, :], ALU.add))
                        ch(dve.tensor_scalar(mt[:, :], mt[:, :], 0.5, None, ALU.mult))
                        dve.sem_inc(s_m, 1)

                low(0, 1)
                with dve.Fori(0, NPAIR // 2 - 1) as i:
                    ch.loop()
                    two_tiles(i, False)
                two_tiles(NPAIR // 2 - 1, True)

            @block.tensor
            def _(pe):
                pe.wait_ge(s_ol, NPAIR)
                with pe.Fori(0, NPAIR // 2) as j2:
                    for b in range(2):
                        hold(pe, gp, s_lo, 2 * j2 + (b + 2))
                        hold(pe, gp, s_m, 2 * j2 + 1)
                        w = 0
                        for i, (n, xh, xl, a) in enumerate(((KT, ht_hi, ht_lo, CTX), (KT, ht_hi, ht_lo, CTX),
                                                            (KT, o_hi, o_lo, 0), (NW, p_hi, p_lo, 0))):
                            for k in range(n):
                                mm = split_mm(pe, bank[4 * b + i][:, :], wh[:, b, w, :], wl[:, b, w, :],
                                              xh[:, k, a:a + SEQ], xl[:, k, a:a + SEQ], k == 0, k == n - 1)
                                w += 1
                        mm.then_inc(s_mm, 1)


def tail(nc, sb, sem, g):
    gv, bank, colv, ident, m_dram = (g[k] for k in ("gv", "bank", "colv", "ident", "m_dram"))
    with ExitStack() as st:
        x2 = sb(st, "x2", [P, TT, D])
        h2 = sb(st, "h2", [P, TT, D])
        gt2b = sb(st, "gt2b", [P, D])
        idx = sb(st, "idx", [P, TT * SLOTS], U32)
        pg = sb(st, "pg", [P, TT * SLOTS])
        router = Router(st, sb)
        with ExitStack() as s2:
            h2h = sb(s2, "h2h", [P, KT, SEQ], F32R)
            h2l = sb(s2, "h2l", [P, KT, SEQ], F32R)
            with ExitStack() as s1:
                out_projection(nc, s1, sb, sem, dict(g, **locals()))
            qt_ = sb(s2, "qt_", [P, 2 * HEADS, SEQ])
            with ExitStack() as s1:
                queries(nc, s1, sb, sem, dict(g, **locals()))
            with ExitStack() as s1:
                routing(nc, s1, sb, sem, dict(g, **locals()))
        experts(nc, st, sb, sem, dict(g, **locals()))


def out_projection(nc, st, sb, sem, g):
    bank, colv, ident, m_dram, x2, h2, gt2b, h2h, h2l = (g[k] for k in (
        "bank", "colv", "ident", "m_dram", "x2", "h2", "gt2b", "h2h", "h2l"))
    mr = sb(st, "mr", [P, KT, SEQ])
    mh = sb(st, "mh", [P, KT, SEQ], F32R)
    ml = sb(st, "ml", [P, KT, SEQ], F32R)
    wr = sb(st, "wr", [P, KT, 512])
    wh = sb(st, "woh", [P, KT, 512], F32R)
    wl = sb(st, "wol", [P, KT, 512], F32R)
    bc = mr[:, 0:6, :].rearrange("p (a b) t -> p a (b t)", a=3)
    sq = wr[:, 0:2, :].rearrange("p a b -> p (a b)")
    rs = sb(st, "rs2", [P, 2 * TT])
    hf = sb(st, "hf2", [P, 2, 512])
    cb = sb(st, "cbx", [P, 2, 4, P])
    (s_m, s_w, s_x, s_mh, s_ml, s_wh, s_wl, s_cb, s_bm, s_bc, s_mm, s_mx, s_ch, s_ssq, s_v, s_std, s_t, s_hf, s_hh,
     s_hl) = (sem(st, n) for n in (
         "m_loaded", "wo_loaded", "x_loaded", "m_hi_made", "m_lo_made", "wo_hi", "wo_lo", "column_spread",
         "broadcast_product", "broadcast_ready", "mix_product", "mix_copied", "dve_chain_f", "row_ssq", "row_ms",
         "row_std", "h2_transposed", "h2_copied", "h2_hi", "h2_lo"))
    with nc.Block() as block:
        @block.sync
        def _(sp):
            sp.dma_start(mr[:, :, :], m_dram.rearrange("k p t -> p k t")).then_inc(s_m, 16)
            sp.dma_start(wr[:, :, :], g["wo_in"][0]).then_inc(s_w, 16)
            sp.dma_start(x2[:, :, :], g["x"].rearrange("o (t p) d -> p (o t) d", p=P)).then_inc(s_x, 16)
            sp.wait_ge(s_wl, 1)
            sp.wait_ge(s_wh, 1)
            sp.dma_start(wr[:, :, :], g["wo_in"][1]).then_inc(s_w, 16)
            sp.wait_ge(s_w, 32)

        @block.scalar
        def _(act):
            act.wait_ge(s_m, 16)
            act.activation(mh[:, :, :], mr[:, :, :], ACT.Copy).then_inc(s_mh, 1)
            for n in range(2):
                act.wait_ge(s_w, 16 * n + 16)
                if n:
                    act.wait_ge(s_mm, TT)
                act.activation(wh[:, :, :], wr[:, :, :], ACT.Copy).then_inc(s_wh, 1)
                if n == 0:
                    act.wait_ge(s_ml, 1)
                    for i in range(8):
                        act.wait_ge(s_bm, i + 1)
                        dst = bc[:, i // 2, :] if i < 6 else gt2b[:, :]
                        act.activation(dst[:, 512 * (i % 2):512 * (i % 2) + 512], bank[6 + i % 2][:, :], ACT.Copy).then_inc(s_bc, 1)
                for t in range(TT):
                    act.wait_ge(s_mm, TT * n + t + 1)
                    act.activation(h2[:, t, 512 * n:512 * n + 512], bank[t][:, :], ACT.Copy).then_inc(s_mx, 1)
            act.wait_ge(s_mx, 2 * TT)
            for t in range(TT):
                if t:
                    act.wait_ge(s_ssq, t)
                act.activation(sq, h2[:, t, :], ACT.Square, accum_out=rs[:, t:t + 1]).then_inc(s_ssq, 1)
            act.wait_ge(s_v, 1)
            act.activation(rs[:, 0:TT], rs[:, 0:TT], ACT.Sqrt).then_inc(s_std, 1)
            act.wait_ge(s_v, 2)
            for t in range(TT):
                act.wait_ge(s_ssq, TT + t)
                act.activation(sq, x2[:, t, :], ACT.Square, accum_out=rs[:, TT + t:TT + t + 1]).then_inc(s_ssq, 1)
            act.wait_ge(s_v, 3)
            act.activation(rs[:, TT:], rs[:, TT:], ACT.Sqrt).then_inc(s_std, 1)
            for k in range(KT):
                act.wait_ge(s_t, k + 1)
                if k >= 2:
                    act.wait_ge(s_hl, k - 1)
                act.activation(hf[:, k % 2, :], bank[k % 2][:, :], ACT.Copy).then_inc(s_hf, 1)
                act.wait_ge(s_hf, k + 1)
                act.activation(h2h[:, k, :], hf[:, k % 2, :], ACT.Copy).then_inc(s_hh, 1)

        @block.vector
        def _(dve):
            ch = Chain(dve, s_ch)
            dve.wait_ge(s_mh, 1)
            dve.tensor_tensor(ml[:, :, :], mr[:, :, :], mh[:, :, :].bitcast(FP32), ALU.subtract).then_inc(s_ml, 1)
            for i in range(8):
                v, n = i // 2, i % 2
                if i >= 2:
                    dve.wait_ge(s_bm, i - 1)
                dve.tensor_copy(cb[:, i % 2, :, :], colv[:, v, 4 * n:4 * n + 4].unsqueeze(2).broadcast_to((P, 4, P))).then_inc(s_cb, 1)
            for n in range(2):
                dve.wait_ge(s_wh, n + 1)
                dve.tensor_tensor(wl[:, :, :], wr[:, :, :], wh[:, :, :].bitcast(FP32), ALU.subtract).then_inc(s_wl, 1)
            dve.wait_ge(s_ssq, TT)
            dve.tensor_scalar(rs[:, 0:TT], rs[:, 0:TT], 1.0 / D, RMS_EPS, ALU.mult, ALU.add).then_inc(s_v, 1)
            dve.wait_ge(s_std, 1)
            ch(dve.reciprocal(rs[:, 0:TT], rs[:, 0:TT]))
            dve.wait_ge(s_x, 16)
            dve.wait_ge(s_bc, 8)
            for t in range(TT):
                ch(dve.scalar_tensor_tensor(h2[:, t, :], h2[:, t, :], rs[:, t:t + 1], bc[:, 0, :], ALU.mult, ALU.mult))
                ch(dve.tensor_tensor(x2[:, t, :], x2[:, t, :], h2[:, t, :], ALU.add))
            dve.sem_inc(s_v, 1)
            dve.wait_ge(s_ssq, 2 * TT)
            dve.tensor_scalar(rs[:, TT:], rs[:, TT:], 1.0 / D, RMS_EPS, ALU.mult, ALU.add).then_inc(s_v, 1)
            dve.wait_ge(s_std, 2)
            ch(dve.reciprocal(rs[:, TT:], rs[:, TT:]))
            for t in range(TT):
                ch(dve.scalar_tensor_tensor(h2[:, t, :], x2[:, t, :], rs[:, TT + t:TT + t + 1], bc[:, 1, :], ALU.mult, ALU.mult))
                ch(dve.tensor_tensor(h2[:, t, :], h2[:, t, :], bc[:, 2, :], ALU.add))
            dve.sem_inc(s_v, 1)
            for k in range(KT):
                dve.wait_ge(s_hh, k + 1)
                dve.tensor_tensor(h2l[:, k, :], hf[:, k % 2, :], h2h[:, k, :].bitcast(FP32), ALU.subtract).then_inc(s_hl, 1)

        @block.tensor
        def _(pe):
            for i in range(8):
                pe.wait_ge(s_cb, i + 1)
                if i >= 2:
                    pe.wait_ge(s_bc, i - 1)
                for q in range(4):
                    mm = pe.matmul(bank[6 + i % 2][:, q * P:q * P + P], cb[:, i % 2, q, :], ident[:, :], start=True, stop=True)
                mm.then_inc(s_bm, 1)
            pe.wait_ge(s_ml, 1)
            for n in range(2):
                pe.wait_ge(s_wl, n + 1)
                for t in range(TT):
                    if n:
                        pe.wait_ge(s_mx, t + 1)
                    for k in range(KT):
                        mm = split_mm(pe, bank[t][:, :], mh[:, k, t * P:t * P + P], ml[:, k, t * P:t * P + P],
                                      wh[:, k, :], wl[:, k, :], k == 0, k == KT - 1)
                    mm.then_inc(s_mm, 1)
            pe.wait_ge(s_mx, 2 * TT)
            pe.wait_ge(s_v, 4)
            for k in range(KT):
                if k >= 2:
                    pe.wait_ge(s_hf, k - 1)
                for t in range(TT):
                    mm = pe.transpose(bank[k % 2][:, t * P:t * P + P], h2[:, t, k * P:k * P + P], ident[:, :])
                mm.then_inc(s_t, 1)


def queries(nc, st, sb, sem, g):
    bank, qt_, h2h, h2l = (g[k] for k in ("bank", "qt_", "h2h", "h2l"))
    wr = sb(st, "wqr", [P, 2, KT, P])
    wh = sb(st, "wqh", [P, 2, KT, P], F32R)
    wl = sb(st, "wql", [P, 2, KT, P], F32R)
    s_w = [sem(st, "wq0_loaded"), sem(st, "wq1_loaded")]
    s_hi, s_lo, s_mm, s_qc = (sem(st, n) for n in ("wq_hi", "wq_lo", "q_product2", "q_copied"))
    gp, ga_, gd = (sem(st, "gate_q_" + k) for k in ("pe", "act", "dve"))
    N2 = HEADS
    with nc.Block() as block:
        @block.sync
        def _(sp):
            with sp.Fori(0, N2) as i:
                for b in range(2):
                    sp.wait_ge(s_lo, 2 * i + 1)
                    sp.wait_ge(s_hi, 2 * i + 1)
                    sp.dma_start(wr[:, b, :, :], g["wq_in"][bass.ds(2 * i + b, 1), :, :].rearrange(
                        "o p (k n) -> (o p) k n", k=KT)).then_inc(s_w[b], 16)

        @block.scalar
        def _(act):
            with act.Fori(0, N2) as i:
                for b in range(2):
                    hold(act, ga_, s_w[b], 16 * i + 16)
                    hold(act, ga_, s_mm, 2 * i + 1)
                    act.activation(wh[:, b, :, :], wr[:, b, :, :], ACT.Copy).then_inc(s_hi, 1)
                for b in range(2):
                    hold(act, ga_, s_mm, 2 * i + (b + 2))
                    act.activation(qt_[:, bass.ds(2 * i + b, 1), :].rearrange("p o t -> p (o t)"), bank[b][:, :],
                                   ACT.Copy).then_inc(s_qc, 1)

        @block.vector
        def _(dve):
            for s in (s_hi, s_lo, s_mm, s_qc):
                dve.sem_inc(s, 1)
            with dve.Fori(0, N2) as i:
                for b in range(2):
                    hold(dve, gd, s_hi, 2 * i + (b + 2))
                    dve.tensor_tensor(wl[:, b, :, :], wr[:, b, :, :], wh[:, b, :, :].bitcast(FP32), ALU.subtract).then_inc(s_lo, 1)

        @block.tensor
        def _(pe):
            with pe.Fori(0, N2) as i:
                for b in range(2):
                    hold(pe, gp, s_lo, 2 * i + (b + 2))
                    hold(pe, gp, s_qc, 2 * i + 1)
                    for k in range(KT):
                        mm = split_mm(pe, bank[b][:, :], wh[:, b, k, :], wl[:, b, k, :], h2h[:, k, :], h2l[:, k, :],
                                      k == 0, k == KT - 1)
                    mm.then_inc(s_mm, 1)


class Router:
    NEG = -3.0e38

    def __init__(self, st, sb):
        self.sc = sb(st, "sc_", [P, 2 * HEADS, NKEYS])
        self.sc2 = sb(st, "sc2", [P, NKEYS])
        self.sv = sb(st, "sv", [P, HEADS, 2, TOPK])
        self.si = sb(st, "si", [P, HEADS, 2, TOPK], U32)
        self.sif = sb(st, "sif", [P, HEADS, 2, TOPK])
        self.cand = sb(st, "cand", [P, TOPK, TOPK])
        self.cand2 = sb(st, "cand2", [P, TOPK * TOPK])
        self.cs = sb(st, "cs", [P, HEADS, TOPK])
        self.ci = sb(st, "ci", [P, HEADS, TOPK], U32)
        self.cj = sb(st, "cj", [P, 2, SLOTS], U32)
        self.cjf = sb(st, "cjf", [P, 2, SLOTS])
        self.iot = sb(st, "iot", [P, TOPK])
        self.oh = sb(st, "oh", [P, SLOTS, TOPK])
        self.kf = sb(st, "kf2", [P, 2, SLOTS])
        self.sm = sb(st, "sm", [P, HEADS])
        self.pgn = sb(st, "pgn", [P, HEADS, TOPK])

    def top16(self, dve, ch, vals, scratch, v, i):
        ch(dve.max(v[:, 0:8], vals))
        ch(dve.max_index(i[:, 0:8], v[:, 0:8], vals))
        ch(dve.match_replace(scratch, v[:, 0:8], vals, self.NEG))
        ch(dve.max(v[:, 8:16], scratch))
        ch(dve.max_index(i[:, 8:16], v[:, 8:16], scratch))

    def head(self, dve, ch, h):
        for p in range(2):
            self.top16(dve, ch, self.sc[:, 2 * h + p, :], self.sc2[:, :], self.sv[:, h, p, :], self.si[:, h, p, :])
        ch(dve.tensor_tensor(self.cand[:, :, :], self.sv[:, h, 0, :].unsqueeze(2).broadcast_to((P, TOPK, TOPK)),
                             self.sv[:, h, 1, :].unsqueeze(1).broadcast_to((P, TOPK, TOPK)), ALU.add))
        self.top16(dve, ch, self.cand[:, :, :].rearrange("p a b -> p (a b)"), self.cand2[:, :], self.cs[:, h, :], self.ci[:, h, :])

    def numbers(self, dve, ch, idx_out):
        cif = self.ci[:, :, :].rearrange("p h k -> p (h k)")
        oh, kf = self.oh, self.kf
        ch(dve.tensor_scalar(self.cj[:, 0, :], cif, 4, None, ALU.logical_shift_right))
        ch(dve.tensor_scalar(self.cj[:, 1, :], cif, 15, None, ALU.bitwise_and))
        ch(dve.tensor_copy(self.cjf[:, :, :], self.cj[:, :, :]))
        ch(dve.tensor_copy(self.sif[:, :, :, :], self.si[:, :, :, :]))
        for p in range(2):
            ch(dve.tensor_tensor(oh[:, :, :], self.cjf[:, p, :].unsqueeze(2).broadcast_to((P, SLOTS, TOPK)),
                                 self.iot[:, :].unsqueeze(1).broadcast_to((P, SLOTS, TOPK)), ALU.is_equal))
            o4 = oh[:, :, :].rearrange("p (h k) i -> p h k i", h=HEADS)
            ch(dve.tensor_tensor(o4, o4, self.sif[:, :, p, :].unsqueeze(2).broadcast_to((P, HEADS, TOPK, TOPK)), ALU.mult))
            ch(dve.tensor_reduce(kf[:, p, :], oh[:, :, :], AX.X, ALU.add))
        ch(dve.scalar_tensor_tensor(kf[:, 0, :], kf[:, 0, :], float(NKEYS), kf[:, 1, :], ALU.mult, ALU.add))
        ch(dve.tensor_copy(idx_out, kf[:, 0, :]))

    def shifted(self, dve, ch):
        ch(dve.tensor_copy(self.sm[:, :], self.cs[:, :, 0]))
        ch(dve.tensor_tensor(self.cs[:, :, :], self.cs[:, :, :], self.sm[:, :].unsqueeze(2).broadcast_to((P, HEADS, TOPK)),
                             ALU.subtract))

    def exp(self, act):
        return act.activation(self.pgn[:, :, :], self.cs[:, :, :], ACT.Exp)

    def gates(self, dve, ch, pg_out):
        ch(dve.tensor_reduce(self.sm[:, :], self.pgn[:, :, :], AX.X, ALU.add))
        ch(dve.reciprocal(self.sm[:, :], self.sm[:, :]))
        ch(dve.tensor_tensor(self.pgn[:, :, :], self.pgn[:, :, :], self.sm[:, :].unsqueeze(2).broadcast_to((P, HEADS, TOPK)), ALU.mult))
        ch(dve.tensor_copy(pg_out, self.pgn[:, :, :].rearrange("p h k -> p (h k)")))


def routing(nc, st, sb, sem, g):
    bank, qt_, idx, pg, rt, scores_dram = (g[k] for k in ("bank", "qt_", "idx", "pg", "router", "scores_dram"))
    HP = 2 * HEADS
    kt = sb(st, "keys_sb", [P, HP, NKEYS])
    later = sb(st, "later", [P, TT - 1, HP * NKEYS])
    s_k, s_c, s_s, s_sc, s_ch, s_e, s_x, s_st = (sem(st, n) for n in (
        "keys_loaded", "iota_made", "scores", "scores_copied", "dve_chain_g", "gates_exp", "gates_shifted", "scores_stored"))
    with nc.Block() as block:
        @block.sync
        def _(sp):
            sp.dma_start(kt[:, :, :], g["keys_in"]).then_inc(s_k, 16)
            for t in range(1, TT):
                sp.wait_ge(s_sc, 4 * t + 4)
                sp.dma_start(scores_dram[t - 1], later[:, t - 1, :]).then_inc(s_st, 16)
            sp.wait_ge(s_st, 16 * (TT - 1))

        @block.gpsimd
        def _(pool):
            pool.iota(rt.iot[:, :], pattern=[[1, TOPK]], base=0, channel_multiplier=0,
                      allow_small_or_imprecise_dtypes=True).then_inc(s_c, 1)

        @block.tensor
        def _(pe):
            pe.wait_ge(s_k, 16)
            for t in range(TT):
                for b in range(4):
                    if t >= 2:
                        pe.wait_ge(s_sc, 4 * (t - 2) + b + 1)
                    for i in range(4):
                        hp = 4 * b + i
                        mm = pe.matmul(bank[4 * (t % 2) + b][:, i * P:i * P + P], qt_[:, hp, t * P:t * P + P], kt[:, hp, :],
                                       start=True, stop=True)
                    mm.then_inc(s_s, 1)

        @block.scalar
        def _(act):
            for t in range(TT):
                for b in range(4):
                    act.wait_ge(s_s, 4 * t + b + 1)
                    dst = rt.sc[:, 4 * b:4 * b + 4, :].rearrange("p a k -> p (a k)") if t == 0 else \
                        later[:, t - 1, 512 * b:512 * b + 512]
                    act.activation(dst, bank[4 * (t % 2) + b][:, :], ACT.Copy).then_inc(s_sc, 1)
            act.wait_ge(s_x, 1)
            rt.exp(act).then_inc(s_e, 1)

        @block.vector
        def _(dve):
            ch = Chain(dve, s_ch)
            dve.wait_ge(s_c, 1)
            for h in range(HEADS):
                if h % 2 == 0:
                    dve.wait_ge(s_sc, h // 2 + 1)
                rt.head(dve, ch, h)
            rt.shifted(dve, ch)
            dve.sem_inc(s_x, 1)
            rt.numbers(dve, ch, idx[:, 0:SLOTS])
            dve.wait_ge(s_e, 1)
            rt.gates(dve, ch, pg[:, 0:SLOTS])


def experts(nc, st, sb, sem, g):
    x2, h2, gt2b, idx, pg, rt, bank, ident, scores_dram = (g[k] for k in (
        "x2", "h2", "gt2b", "idx", "pg", "router", "bank", "ident", "scores_dram"))
    URING = 8
    ur = sb(st, "ur", [P, URING, D])
    vr = sb(st, "vr", [P, TOPK, D])
    ic = sb(st, "ic", [P, 2, TOPK], U32)
    gc = sb(st, "gc_", [P, 2, TOPK])
    dg = sb(st, "dg", [P, TOPK, P])
    hc = sb(st, "hc", [P, D])
    junk = sb(st, "junk", [P, 2, D])
    dt = sb(st, "dt_", [P, TOPK])
    ge = sb(st, "ge", [P, TOPK])
    rs = sb(st, "rs3", [P, 2])
    sq = sb(st, "sq3", [P, 512])
    res = sb(st, "res", [P, D])
    su = [sem(st, f"u_row{k}") for k in range(URING)]
    sv = [sem(st, f"v_row{k}") for k in range(TOPK)]
    s_ic, s_ch, s_ud, s_ge, s_gc, s_vd, s_ssq, s_v, s_std, s_res, s_out, s_dg, s_top, s_scl, s_x, s_e = (
        sem(st, n) for n in ("numbers_set", "dve_chain_h", "u_used", "gelu_done", "coefficients", "v_used", "peer_ssq",
                             "peer_ms", "peer_std", "result_made", "out_stored", "diagonal_made",
                             "scores_routed", "scores_loaded", "coming_shifted", "coming_exp"))
    gp, ga_, gd, gq, gs = (sem(st, "gate_h_" + k) for k in ("pe", "act", "dve", "pool", "sp"))
    outv = g["out"].rearrange("o (t p) d -> (o t) p d", p=P)

    def tiles(eng, body, chain=None):
        body(0, True, False)
        with eng.Fori(0, TT - 2) as i:
            if chain:
                chain.loop()
            body(i + 1, False, False)
        body(TT - 1, False, True)

    with nc.Block() as block:
        @block.gpsimd
        def _(pool):
            def tile(t, first, last):
                for h in range(HEADS):
                    hold(pool, gq, s_ic, t * HEADS + (h + 1))
                    for ring, s, n, src, used in ((ur, su, URING, g["peer_u"], s_ud), (vr, sv, TOPK, g["peer_v"], s_vd)):
                        for k in range(TOPK):
                            if k % 4 == 0:
                                hold(pool, gq, used, t * SLOTS + (TOPK * h + k + 4))
                            pool.indirect_dma_start(ring[:, k % n, :], None, src, bass.IndirectOffsetOnAxis(
                                ap=ic[:, h % 2, k:k + 1], axis=0)).then_inc(s[k % n], 16)
            tiles(pool, tile)

        @block.scalar
        def _(act):
            def squares(t):
                hold(act, ga_, s_vd, t * SLOTS + (SLOTS + TOPK))
                for n in range(2):
                    if n:
                        hold(act, ga_, s_ssq, 2 * t + 1)
                    act.activation(sq[:, :], bank[n][:, :], ACT.Square, accum_out=rs[:, n:n + 1]).then_inc(s_ssq, 1)
                hold(act, ga_, s_v, t + 1)
                act.activation(rs[:, 0:1], rs[:, 0:1], ACT.Sqrt).then_inc(s_std, 1)

            def tile(t, first, last):
                for h in range(HEADS):
                    hold(act, ga_, s_ud, t * SLOTS + (TOPK * (h + 1) + URING))
                    act.activation(ge[:, :], dt[:, :], ACT.Gelu).then_inc(s_ge, 1)
                    hold(act, ga_, s_gc, t * HEADS + (h + 1))
                    hold(act, ga_, s_vd, t * SLOTS + TOPK * (h + 1))
                    for k in range(TOPK):
                        act.activation(dg[:, k, :], ident[:, :], ACT.Copy, scale=gc[:, h % 2, k:k + 1]).then_inc(s_dg, 1)
                    if h == 0 and not first:
                        squares(t - 1)
                    if h == HEADS // 2 and not last:
                        hold(act, ga_, s_x, t + 1)
                        rt.exp(act).then_inc(s_e, 1)
            tiles(act, tile)
            squares(TT - 1)

        @block.sync
        def _(sp):
            def tile(t, first, last):
                if not last:
                    if not first:
                        hold(sp, gs, s_top, t)
                    sp.dma_start(rt.sc[:, :, :], scores_dram[bass.ds(t, 1), :, :].rearrange(
                        "o p (a k) -> (o p) a k", k=NKEYS)).then_inc(s_scl, 16)
                if not first:
                    store(t - 1)

            def store(t):
                hold(sp, gs, s_res, t + 1)
                sp.dma_start(outv[bass.ds(t, 1), :, :].rearrange("o p d -> (o p) d"), res[:, :]).then_inc(s_out, 16)

            tiles(sp, tile)
            store(TT - 1)
            sp.wait_ge(s_out, 16 * TT + 1)

        @block.vector
        def _(dve):
            ch = Chain(dve, s_ch)
            dve.tensor_copy(ic[:, 0, :], idx[:, 0:TOPK]).then_inc(s_ic, 1)
            for s, n in ((s_ud, URING), (s_vd, TOPK), (s_out, 1)):
                dve.sem_inc(s, n)

            def finish(t):
                hold(dve, gd, s_ssq, 2 * t + 2)
                ch(dve.tensor_tensor(rs[:, 0:1], rs[:, 0:1], rs[:, 1:2], ALU.add))
                ch(dve.tensor_scalar(rs[:, 0:1], rs[:, 0:1], 1.0 / D, RMS_EPS, ALU.mult, ALU.add))
                dve.sem_inc(s_v, 1)
                hold(dve, gd, s_std, t + 1)
                ch(dve.reciprocal(rs[:, 0:1], rs[:, 0:1]))
                hold(dve, gd, s_out, 16 * t + 1)
                for n in range(2):
                    C = slice(512 * n, 512 * n + 512)
                    ch(dve.scalar_tensor_tensor(res[:, C], bank[n][:, :], rs[:, 0:1], gt2b[:, C], ALU.mult, ALU.mult))
                ch(dve.tensor_tensor(res[:, :], res[:, :], x2[:, bass.ds(t, 1), :].rearrange("p o d -> p (o d)"), ALU.add))
                dve.sem_inc(s_res, 1)

            def tile(t, first, last):
                ch(dve.tensor_copy(hc[:, :], h2[:, bass.ds(t, 1), :].rearrange("p o d -> p (o d)")))
                for h in range(HEADS):
                    b = h % 2
                    for k in range(TOPK):
                        hold(dve, gd, su[k % URING], t * (16 * SLOTS // URING) + 16 * (2 * h + k // URING + 1))
                        hold(dve, gd, s_ud, t * SLOTS + (TOPK * h + k + URING - 1))
                        dve.scalar_tensor_tensor(junk[:, k % 2, :], ur[:, k % URING, :], 1.0, hc[:, :], ALU.mult, ALU.mult,
                                                 accum_out=dt[:, k:k + 1]).then_inc(s_ud, 1)
                    if not (last and h == HEADS - 1):
                        if h:
                            hold(dve, gd, sv[TOPK - 1], t * (16 * HEADS) + 16 * h)
                        dve.tensor_copy(ic[:, 1 - b, :], idx[:, bass.ds(t * SLOTS + TOPK * (h + 1), TOPK)]).then_inc(s_ic, 1)
                    hold(dve, gd, s_ge, t * HEADS + (h + 1))
                    dve.tensor_tensor(gc[:, b, :], ge[:, :], pg[:, bass.ds(t * SLOTS + TOPK * h, TOPK)], ALU.mult).then_inc(s_gc, 1)
                    if h == 0 and not first:
                        finish(t - 1)
                    if not last:
                        if h == 0:
                            hold(dve, gd, s_scl, 16 * t + 16)
                        if h < HEADS // 2:
                            rt.head(dve, ch, 2 * h)
                            rt.head(dve, ch, 2 * h + 1)
                        if h == HEADS // 2 - 1:
                            dve.sem_inc(s_top, 1)
                        if h == HEADS // 2:
                            rt.shifted(dve, ch)
                            dve.sem_inc(s_x, 1)
                            rt.numbers(dve, ch, idx[:, bass.ds((t + 1) * SLOTS, SLOTS)])
                            hold(dve, gd, s_e, t + 1)
                            rt.gates(dve, ch, pg[:, bass.ds((t + 1) * SLOTS, SLOTS)])
            tiles(dve, tile, ch)
            finish(TT - 1)

        @block.tensor
        def _(pe):
            def tile(t, first, last):
                if not first:
                    hold(pe, gp, s_res, t)
                for h in range(HEADS):
                    hold(pe, gp, s_dg, t * SLOTS + TOPK * (h + 1))
                    for k in range(TOPK):
                        hold(pe, gp, sv[k], t * (16 * HEADS) + 16 * (h + 1))
                        begin, end = h == 0 and k == 0, h == HEADS - 1 and k == TOPK - 1
                        for n in range(2):
                            mm = pe.matmul(bank[n][:, :], dg[:, k, :], vr[:, k, 512 * n:512 * n + 512], start=begin, stop=end)
                        mm.then_inc(s_vd, 1)
            tiles(pe, tile)




def _tiles(w, cols):
    k = w.shape[0] // P
    return [np.ascontiguousarray(w[:, c:c + P].reshape(k, P, P).transpose(1, 0, 2).reshape(P, k * P)) for c in cols]


def _cols(v):
    return v.reshape(-1, P).T


def _pack(a):
    i = {k: np.asarray(v) for k, v in a.items()}
    w_in, w_mod = i["w_in"][0], i["w_mod"][0]
    shift = 3 * D + 3 * P
    gvec = np.concatenate([_cols(i["c"][0]), _cols(i["c_ctx"]), _cols(i["b_mod"][0]), _cols(i["g_pre_mix"][0]),
                           _cols(i["g_post_mix"][0]), _cols(i["g_pre_ffn"][0]), _cols(i["g_post_ffn"][0]),
                           _cols(i["mu_shift"][0][3 * D:]), _cols(i["b_gate"][0]), _cols(i["pool_scale"][0])], axis=1)
    mu = i["mu_shift"][0][:3 * D].reshape(3, NPAIR, P)
    rows = [mu[0], mu[1], mu[2]] + [i[n][0][d].reshape(NPAIR, P) for n in ("w0", "a0") for d in range(2)] + [
        i[n][0].reshape(NPAIR, P) for n in ("k_k", "k_a", "r_k", "ln_x_w", "ln_x_b")]
    lora = np.stack([i["w2"][0].reshape(P, NPAIR, P), i["a2"][0].reshape(P, NPAIR, P), i["g2"][0].reshape(P, NPAIR, P)])
    wa, wb, wo = i["w_a_out"][0], i["w_b_out"][0], i["w_o"][0]
    half = np.arange(SEQ)
    inv = []
    for w in WINDOWS:
        r, c = half // GRID_W, half % GRID_W
        n = (np.minimum(r + w // 2, ROWS) - np.maximum(r - w // 2, 0)) * (
            np.minimum(c + w // 2, GRID_W) - np.maximum(c - w // 2, 0))
        inv.append(1.0 / n)
    return {
        "x": i["x"], "ctx_in": i["ctx"], "gvec_in": gvec,
        "wmod": w_mod.reshape(KT, P, MODG, 512).transpose(2, 1, 0, 3).reshape(MODG, P, KT * 512),
        "wlora_in": np.concatenate(_tiles(w_in, [3 * D + q * P for q in range(3)]), axis=1),
        "wpair_in": np.stack([np.concatenate(_tiles(w_in, [q * D + j * P for q in range(3)]), axis=1) for j in range(NPAIR)]),
        "pvec_in": np.stack(rows).transpose(1, 2, 0),
        "lora_in": lora.transpose(2, 1, 0, 3).reshape(NPAIR, P, 3 * P),
        "wpu_in": np.concatenate(_tiles(w_in, [shift + q * P for q in range(4)]), axis=1),
        "wpool_in": i["w_pool"][0].transpose(1, 0, 2),
        "invcnt_in": np.array(inv, dtype=np.float32),
        "wmerge_in": np.stack([np.concatenate(
            _tiles(w_in, [shift + 512 + j * P, shift + 512 + D + j * P]) + _tiles(wa, [j * P]) + _tiles(wb, [j * P]),
            axis=1) for j in range(NPAIR)]),
        "wo_in": wo.reshape(KT, P, 2, 512).transpose(2, 1, 0, 3),
        "wq_in": np.stack(_tiles(i["peer_wq"][0], [q * P for q in range(16)])),
        "keys_in": i["peer_keys"][0].reshape(16, P, P).transpose(2, 0, 1),
        "peer_u": i["peer_u"][0], "peer_v": i["peer_v"][0],
    }


def kernel(**inputs):
    import concourse.bacc as bacc
    from concourse.bass_utils import run_bass_kernel_spmd
    nc = bacc.Bacc("TRN2", target_bir_lowering=False, num_devices=1)
    arrays, args = {}, {}
    for name, a in _pack(inputs).items():
        a = np.ascontiguousarray(a)
        arrays["in_" + name] = a
        args[name] = nc.dram_tensor("in_" + name, a.shape, mybir.dt.from_np(a.dtype), kind="ExternalInput").ap()
    args["out"] = nc.dram_tensor("out_0", (1, SEQ, D), FP32, kind="ExternalOutput").ap()
    build(nc, **args)
    r = run_bass_kernel_spmd(nc, [arrays], core_ids=[0])
    return r.results[0]["out_0"]
```
